# Optimizing a Trainium2 kernel written in Bass

```python
import jax, jax.numpy as jnp
from jax import lax
import numpy as np

D_MODEL = 1024
BATCH = 1
SEQ = 256
DEPTH = 1

MEM_LEN = 256
N_MIXERS = 4
GROUP_WIDTH = D_MODEL // N_MIXERS
N_HEADS = 4
HEAD_DIM = GROUP_WIDTH // N_HEADS
GLA_KEY_DIM = HEAD_DIM // 2
GLA_LOWRANK = 16
GLA_GATE_NORM = 16.0
GDN_CONV = 4
CHUNK = 64
ROPE_BASE = 10000.0
XATTN_HEADS = 4
XATTN_HEAD_DIM = D_MODEL // XATTN_HEADS
D_FF = 2816
FFN_CONV = 3
EPS = 1e-6

IN_SPLITS = (
    GROUP_WIDTH, GROUP_WIDTH, GROUP_WIDTH, GROUP_WIDTH,
    GROUP_WIDTH, GROUP_WIDTH, GROUP_WIDTH, N_HEADS, N_HEADS, GROUP_WIDTH,
    N_HEADS * GLA_KEY_DIM, N_HEADS * GLA_KEY_DIM, GROUP_WIDTH, GLA_LOWRANK, GROUP_WIDTH,
    GROUP_WIDTH, GROUP_WIDTH, GROUP_WIDTH, GROUP_WIDTH,
)
IN_WIDTH = sum(IN_SPLITS)


def _rmsnorm(x, w):
    xf = x.astype(jnp.float32)
    y = xf * lax.rsqrt(jnp.mean(xf * xf, axis=-1, keepdims=True) + EPS)
    return (y * w.astype(jnp.float32)).astype(x.dtype)

def _norm_f32(x):
    return x * lax.rsqrt(jnp.mean(x * x, axis=-1, keepdims=True) + EPS)

def _l2norm(x):
    return x * lax.rsqrt(jnp.sum(x * x, axis=-1, keepdims=True) + EPS)

def _rope(x, positions):
    d = x.shape[-1]
    freqs = ROPE_BASE ** (-jnp.arange(0, d, 2, dtype=jnp.float32) / d)
    ang = positions.astype(jnp.float32)[..., None] * freqs
    cos, sin = jnp.cos(ang)[:, :, None, :], jnp.sin(ang)[:, :, None, :]
    x1, x2 = jnp.split(x, 2, axis=-1)
    return jnp.concatenate([x1 * cos - x2 * sin, x1 * sin + x2 * cos], axis=-1)

def _causal_dwconv(x, w):
    k, c = w.shape
    return lax.conv_general_dilated(
        x, w[:, None, :].astype(x.dtype), window_strides=(1,), padding=[(k - 1, 0)],
        dimension_numbers=('NWC', 'WIO', 'NWC'), feature_group_count=c)

def _to_chunks(t):
    b, tt, h = t.shape[:3]
    t = t.reshape((b, tt // CHUNK, CHUNK, h) + t.shape[3:])
    return jnp.moveaxis(t, 3, 1)

def _from_chunks(t):
    b, h, n, c, d = t.shape
    return jnp.moveaxis(t, 1, 3).reshape(b, n * c, h, d)

def _retention_chunked(q, k, v, log_gamma):
    c = q.shape[3]
    idx = jnp.arange(c, dtype=jnp.float32)
    lg = log_gamma[:, None]
    rel = idx[:, None] - idx[None, :]
    decay = jnp.where(rel >= 0, jnp.exp(lg[:, :, None] * jnp.maximum(rel, 0.0)), 0.0)
    scores = jnp.einsum('bhncd,bhnsd->bhncs', q, k) * decay[None, :, None]
    o_intra = jnp.einsum('bhncs,bhnsv->bhncv', scores, v)
    q_decay = jnp.exp(lg * (idx + 1.0))
    k_decay = jnp.exp(lg * (c - 1.0 - idx))
    chunk_decay = jnp.exp(log_gamma * c)
    kv = jnp.einsum('bhncd,bhncv->bhndv', k * k_decay[None, :, None, :, None], v)

    def step(state, inp):
        kv_n, q_n = inp
        o = jnp.einsum('bhcd,bhdv->bhcv', q_n, state) * q_decay[None, :, :, None]
        state = state * chunk_decay[None, :, None, None] + kv_n
        return state, o

    b, h, _, _, dk = q.shape
    s0 = jnp.zeros((b, h, dk, v.shape[-1]), jnp.float32)
    _, o_inter = lax.scan(step, s0, (jnp.moveaxis(kv, 2, 0), jnp.moveaxis(q, 2, 0)))
    return o_intra + jnp.moveaxis(o_inter, 0, 2)

def _gated_delta_chunked(q, k, v, beta, g):
    c = q.shape[3]
    gc = jnp.cumsum(g, axis=-1)
    causal = jnp.tril(jnp.ones((c, c), dtype=bool))
    strict = jnp.tril(jnp.ones((c, c), dtype=bool), k=-1)
    ratio = jnp.exp(jnp.where(causal, gc[..., :, None] - gc[..., None, :], -jnp.inf))
    kk = jnp.where(strict, jnp.einsum('bhncd,bhnsd->bhncs', k, k) * ratio, 0.0)
    a_mat = jnp.eye(c, dtype=jnp.float32) + beta[..., None] * kk
    gamma = jnp.exp(gc)
    u_v = lax.linalg.triangular_solve(a_mat, beta[..., None] * v, left_side=True, lower=True, unit_diagonal=True)
    w_k = lax.linalg.triangular_solve(a_mat, (beta * gamma)[..., None] * k, left_side=True, lower=True, unit_diagonal=True)
    qk = jnp.einsum('bhncd,bhnsd->bhncs', q, k) * ratio
    q_g = q * gamma[..., None]
    k_tail = k * jnp.exp(gc[..., -1:] - gc)[..., None]
    chunk_decay = jnp.exp(gc[..., -1])

    def step(state, inp):
        uv_n, w_n, qk_n, qg_n, kt_n, cd_n = inp
        u = uv_n - jnp.einsum('bhcd,bhdv->bhcv', w_n, state)
        o = jnp.einsum('bhcd,bhdv->bhcv', qg_n, state) + jnp.einsum('bhcs,bhsv->bhcv', qk_n, u)
        state = cd_n[..., None, None] * state + jnp.einsum('bhcd,bhcv->bhdv', kt_n, u)
        return state, o

    b, h, _, _, dk = q.shape
    s0 = jnp.zeros((b, h, dk, v.shape[-1]), jnp.float32)
    xs = tuple(jnp.moveaxis(t, 2, 0) for t in (u_v, w_k, qk, q_g, k_tail, chunk_decay))
    _, o = lax.scan(step, s0, xs)
    return jnp.moveaxis(o, 0, 2)

def _gated_linear_chunked(q, k, v, log_f):
    c = q.shape[3]
    gc = jnp.cumsum(log_f, axis=3)
    causal = jnp.tril(jnp.ones((c, c), dtype=bool))[:, :, None]

    def step(state, inp):
        q_n, k_n, v_n, g_n = inp
        diff = g_n[:, :, :, None, :] - g_n[:, :, None, :, :]
        decay = jnp.exp(jnp.where(causal, diff, -jnp.inf))
        scores = jnp.einsum('bhcd,bhsd,bhcsd->bhcs', q_n, k_n, decay)
        o = jnp.einsum('bhcs,bhsv->bhcv', scores, v_n) + jnp.einsum('bhcd,bhdv->bhcv', q_n * jnp.exp(g_n), state)
        k_tail = k_n * jnp.exp(g_n[:, :, -1:] - g_n)
        state = jnp.exp(g_n[:, :, -1])[..., None] * state + jnp.einsum('bhcd,bhcv->bhdv', k_tail, v_n)
        return state, o

    b, h, _, _, dk = q.shape
    s0 = jnp.zeros((b, h, dk, v.shape[-1]), jnp.float32)
    xs = tuple(jnp.moveaxis(t, 2, 0) for t in (q, k, v, gc))
    _, o = lax.scan(step, s0, xs)
    return jnp.moveaxis(o, 0, 2)

def _hybrid_mixer(h, positions, w_in, gdn_conv_w, gdn_a_log, gdn_dt_bias, gdn_norm_w,
                  gla_gk_up, gla_gk_bias, gla_norm_w, hgrn_lb, hgrn_norm_w, w_out):
    b, t, _ = h.shape
    f32 = jnp.float32
    z = jnp.matmul(h, w_in).astype(f32)
    split_points = [int(p) for p in np.cumsum(IN_SPLITS)[:-1]]
    (rq, rk, rv, rg, bq, bk, bv, ba, bb, bg,
     cq, ck, cv, c_lr, cg, dq, df, di, dg) = jnp.split(z, split_points, axis=-1)

    def heads(a):
        return a.reshape(b, t, N_HEADS, -1)

    q_a = _rope(heads(rq), positions)
    k_a = _rope(heads(rk), positions) * HEAD_DIM ** -0.5
    log_gamma = jnp.log(1.0 - jnp.exp2(-5.0 - jnp.arange(N_HEADS, dtype=f32)))
    o_a = _from_chunks(_retention_chunked(_to_chunks(q_a), _to_chunks(k_a), _to_chunks(heads(rv)), log_gamma))
    o_a = _norm_f32(o_a) * jax.nn.silu(heads(rg))

    qkv = jax.nn.silu(_causal_dwconv(jnp.concatenate([bq, bk, bv], axis=-1), gdn_conv_w.astype(f32)))
    q_b, k_b, v_b = jnp.split(qkv, 3, axis=-1)
    q_b = _l2norm(heads(q_b)) * HEAD_DIM ** -0.5
    k_b = _l2norm(heads(k_b))
    beta = jax.nn.sigmoid(bb)
    g_b = -jnp.exp(gdn_a_log.astype(f32)) * jax.nn.softplus(ba + gdn_dt_bias.astype(f32))
    o_b = _from_chunks(_gated_delta_chunked(_to_chunks(q_b), _to_chunks(k_b), _to_chunks(heads(v_b)),
                                            _to_chunks(beta), _to_chunks(g_b)))
    o_b = _norm_f32(o_b) * gdn_norm_w.astype(f32) * jax.nn.silu(heads(bg))

    q_c = heads(cq) * GLA_KEY_DIM ** -0.5
    log_f_c = jax.nn.log_sigmoid(jnp.matmul(c_lr, gla_gk_up.astype(f32)) + gla_gk_bias.astype(f32)) / GLA_GATE_NORM
    o_c = _from_chunks(_gated_linear_chunked(_to_chunks(q_c), _to_chunks(heads(ck)), _to_chunks(heads(cv)),
                                             _to_chunks(heads(log_f_c))))
    o_c = _norm_f32(o_c) * gla_norm_w.astype(f32) * jax.nn.silu(heads(cg))

    lb = hgrn_lb.reshape(N_HEADS, HEAD_DIM)
    f_pre = heads(df)
    log_f_d = jnp.logaddexp(jnp.log(lb), jnp.log1p(-lb) + jax.nn.log_sigmoid(f_pre))
    k_d = (1.0 - lb) * jax.nn.sigmoid(-f_pre)
    o_d = _from_chunks(_gated_linear_chunked(_to_chunks(heads(dq)), _to_chunks(k_d), _to_chunks(heads(di)),
                                             _to_chunks(log_f_d)))
    o_d = _norm_f32(o_d) * hgrn_norm_w.astype(f32) * jax.nn.silu(heads(dg))

    o = jnp.concatenate([o_a.reshape(b, t, GROUP_WIDTH), o_b.reshape(b, t, GROUP_WIDTH),
                         o_c.reshape(b, t, GROUP_WIDTH), o_d.reshape(b, t, GROUP_WIDTH)], axis=-1)
    return jnp.matmul(o.astype(h.dtype), w_out)

def _memory_cross_attn(h, mem_n, wq, wk, wv, wo):
    b, t, _ = h.shape
    m = mem_n.shape[1]
    q = jnp.matmul(h, wq).reshape(b, t, XATTN_HEADS, XATTN_HEAD_DIM)
    k = jnp.matmul(mem_n, wk).reshape(b, m, XATTN_HEADS, XATTN_HEAD_DIM)
    v = jnp.matmul(mem_n, wv).reshape(b, m, XATTN_HEADS, XATTN_HEAD_DIM)
    s = jnp.einsum('bthd,bmhd->bhtm', q, k).astype(jnp.float32) * XATTN_HEAD_DIM ** -0.5
    p = jax.nn.softmax(s, axis=-1).astype(v.dtype)
    o = jnp.einsum('bhtm,bmhd->bthd', p, v).reshape(b, t, D_MODEL)
    return jnp.matmul(o, wo)

def _conv_ffn(h, w_up, conv_w, w_down):
    u = _causal_dwconv(jnp.matmul(h, w_up), conv_w)
    gate, val = jnp.split(u, 2, axis=-1)
    return jnp.matmul(jax.nn.silu(gate) * val, w_down)

def first_inputs(seed: int = 0) -> dict:
    key = jax.random.key(seed)
    ks = jax.random.split(key, 26)
    nrm = jax.random.normal

    def gain(k, shape):
        return 1.0 + 0.02 * nrm(k, shape, jnp.float32)

    dt = jnp.exp(jax.random.uniform(ks[6], (DEPTH, N_HEADS), jnp.float32, np.log(1e-3), np.log(1e-1)))
    pos_offset = jax.random.randint(ks[2], (BATCH, 1), 0, 4096, dtype=jnp.int32)
    return {
        'x': nrm(ks[0], (BATCH, SEQ, D_MODEL), jnp.float32),
        'mem': nrm(ks[1], (BATCH, MEM_LEN, D_MODEL), jnp.float32),
        'positions': pos_offset + jnp.arange(SEQ, dtype=jnp.int32)[None, :],
        'mix_norm_w': gain(ks[3], (DEPTH, D_MODEL)),
        'w_in': nrm(ks[4], (DEPTH, D_MODEL, IN_WIDTH), jnp.float32) * D_MODEL ** -0.5,
        'gdn_conv_w': nrm(ks[5], (DEPTH, GDN_CONV, 3 * GROUP_WIDTH), jnp.float32) * GDN_CONV ** -0.5,
        'gdn_a_log': jnp.log(jax.random.uniform(ks[7], (DEPTH, N_HEADS), jnp.float32, 1.0, 16.0)),
        'gdn_dt_bias': dt + jnp.log(-jnp.expm1(-dt)),
        'gdn_norm_w': gain(ks[8], (DEPTH, HEAD_DIM)),
        'gla_gk_up': nrm(ks[9], (DEPTH, GLA_LOWRANK, N_HEADS * GLA_KEY_DIM), jnp.float32) * GLA_LOWRANK ** -0.5,
        'gla_gk_bias': 0.02 * nrm(ks[10], (DEPTH, N_HEADS * GLA_KEY_DIM), jnp.float32),
        'gla_norm_w': gain(ks[11], (DEPTH, HEAD_DIM)),
        'hgrn_lb_logits': 0.1 * nrm(ks[12], (DEPTH, GROUP_WIDTH), jnp.float32),
        'hgrn_norm_w': gain(ks[13], (DEPTH, HEAD_DIM)),
        'w_out': nrm(ks[14], (DEPTH, D_MODEL, D_MODEL), jnp.float32) * D_MODEL ** -0.5,
        'xattn_norm_w': gain(ks[15], (DEPTH, D_MODEL)),
        'mem_norm_w': gain(ks[16], (D_MODEL,)),
        'xattn_wq': nrm(ks[17], (DEPTH, D_MODEL, D_MODEL), jnp.float32) * D_MODEL ** -0.5,
        'xattn_wk': nrm(ks[18], (DEPTH, D_MODEL, D_MODEL), jnp.float32) * D_MODEL ** -0.5,
        'xattn_wv': nrm(ks[19], (DEPTH, D_MODEL, D_MODEL), jnp.float32) * D_MODEL ** -0.5,
        'xattn_wo': nrm(ks[20], (DEPTH, D_MODEL, D_MODEL), jnp.float32) * D_MODEL ** -0.5,
        'ffn_norm_w': gain(ks[21], (DEPTH, D_MODEL)),
        'ffn_up': nrm(ks[22], (DEPTH, D_MODEL, 2 * D_FF), jnp.float32) * D_MODEL ** -0.5,
        'ffn_conv_w': nrm(ks[23], (DEPTH, FFN_CONV, 2 * D_FF), jnp.float32) * FFN_CONV ** -0.5,
        'ffn_down': nrm(ks[24], (DEPTH, D_FF, D_MODEL), jnp.float32) * D_FF ** -0.5,
        'final_norm_w': gain(ks[25], (D_MODEL,)),
    }

def first_block(x, mem, positions, mix_norm_w, w_in, gdn_conv_w, gdn_a_log, gdn_dt_bias, gdn_norm_w,
              gla_gk_up, gla_gk_bias, gla_norm_w, hgrn_lb_logits, hgrn_norm_w, w_out,
              xattn_norm_w, mem_norm_w, xattn_wq, xattn_wk, xattn_wv, xattn_wo,
              ffn_norm_w, ffn_up, ffn_conv_w, ffn_down, final_norm_w):
    lb_all = jnp.cumsum(jax.nn.softmax(hgrn_lb_logits.astype(jnp.float32), axis=0), axis=0)
    lb_all = lb_all - lb_all[0]
    mem_n = _rmsnorm(mem, mem_norm_w)
    h = x
    for l in range(DEPTH):
        h = h + _hybrid_mixer(_rmsnorm(h, mix_norm_w[l]), positions, w_in[l], gdn_conv_w[l], gdn_a_log[l],
                              gdn_dt_bias[l], gdn_norm_w[l], gla_gk_up[l], gla_gk_bias[l], gla_norm_w[l],
                              lb_all[l], hgrn_norm_w[l], w_out[l])
        h = h + _memory_cross_attn(_rmsnorm(h, xattn_norm_w[l]), mem_n, xattn_wq[l], xattn_wk[l],
                                   xattn_wv[l], xattn_wo[l])
        h = h + _conv_ffn(_rmsnorm(h, ffn_norm_w[l]), ffn_up[l], ffn_conv_w[l], ffn_down[l])
    return _rmsnorm(h, final_norm_w)


DEPTH_2 = 2

GRID_W = 64
CTX_LEN = 256
D_FF_2 = 2752
N_MOD = 9
D_FOURIER = D_MODEL // 2
FOURIER_CH = 128
FOURIER_GROUPS = D_FOURIER // FOURIER_CH
D_SGU = D_MODEL // 2
SGU_CH = 128
SGU_GROUPS = D_SGU // SGU_CH
CHUNK_2 = 128
HEAD_DIM_2 = 128
N_HEADS_2 = D_MODEL // HEAD_DIM_2
N_KV_HEADS = 2
GROUP = N_HEADS_2 // N_KV_HEADS
ROPE_AXIS_DIM = HEAD_DIM_2 // 2
ROPE_THETA = 10000.0
Q_BLOCK = 128


def rms_norm(x, g):
    xf = x.astype(jnp.float32)
    y = xf * lax.rsqrt(jnp.mean(jnp.square(xf), axis=-1, keepdims=True) + EPS)
    return (y * g.astype(jnp.float32)).astype(x.dtype)

def adaln(cvec, w_mod, b_mod):
    m = jax.nn.silu(cvec) @ w_mod + b_mod
    m = m.reshape(m.shape[0], 1, N_MOD, D_MODEL)
    return [m[:, :, i] for i in range(N_MOD)]

def modulated_norm(x, g, shift, scale):
    return rms_norm(x, g) * (1 + scale) + shift

def swiglu(h, w_gu, w_down):
    gate, up = jnp.split(h @ w_gu, 2, axis=-1)
    return (jax.nn.silu(gate) * up) @ w_down

def ffn_half_step(x, mods, g, w_gu, w_down):
    shift, scale, gate = mods
    return x + 0.5 * gate * swiglu(modulated_norm(x, g, shift, scale), w_gu, w_down)

def fourier_mix(a):
    b_, n, _ = a.shape
    a4 = a.reshape(b_, n, FOURIER_GROUPS, FOURIER_CH).astype(jnp.float32)
    f = jnp.fft.fftn(a4, axes=(1, 3), norm="ortho").real
    return f.reshape(b_, n, D_FOURIER).astype(a.dtype)

def chunk_sgu(u, v, g_v, w_s, b_s):
    b_, n, _ = v.shape
    vh = rms_norm(v.reshape(b_, n, SGU_GROUPS, SGU_CH), g_v)
    vc = vh.reshape(b_, n // CHUNK_2, CHUNK_2, SGU_GROUPS, SGU_CH)
    mixed = jnp.einsum('hpq,bcqhd->bcphd', w_s, vc) + b_s.T[None, None, :, :, None]
    return u * mixed.reshape(b_, n, D_SGU)

def fourier_sgu_mixer(h, w_in, g_v, w_s, b_s, w_out):
    a, uv = jnp.split(h @ w_in, [D_FOURIER], axis=-1)
    u, v = jnp.split(jax.nn.gelu(uv), 2, axis=-1)
    out = jnp.concatenate([fourier_mix(a), chunk_sgu(u, v, g_v, w_s, b_s)], axis=-1)
    return out @ w_out

def axial_angles(rows):
    row = jnp.repeat(jnp.arange(rows, dtype=jnp.float32), GRID_W)
    col = jnp.tile(jnp.arange(GRID_W, dtype=jnp.float32), rows)
    inv_freq = ROPE_THETA ** (-jnp.arange(0, ROPE_AXIS_DIM, 2, dtype=jnp.float32) / ROPE_AXIS_DIM)
    return row[:, None] * inv_freq, col[:, None] * inv_freq

def rotate(x, ang):
    full = jnp.concatenate([ang, ang], axis=-1)[:, None, :]
    cos = jnp.cos(full).astype(x.dtype)
    sin = jnp.sin(full).astype(x.dtype)
    x1, x2 = jnp.split(x, 2, axis=-1)
    return x * cos + jnp.concatenate([-x2, x1], axis=-1) * sin

def axial_rope(x, ang_row, ang_col):
    xr, xc = jnp.split(x, 2, axis=-1)
    return jnp.concatenate([rotate(xr, ang_row), rotate(xc, ang_col)], axis=-1)

def project_kv(kv, g_k):
    b_, n, _ = kv.shape
    k, v = jnp.split(kv, 2, axis=-1)
    k = rms_norm(k.reshape(b_, n, N_KV_HEADS, HEAD_DIM_2), g_k)
    return k, v.reshape(b_, n, N_KV_HEADS, HEAD_DIM_2)

def project_q(q, g_q):
    b_, n, _ = q.shape
    return rms_norm(q.reshape(b_, n, N_HEADS_2, HEAD_DIM_2), g_q)

def gqa_attend(q, k, v):
    b_, nq = q.shape[:2]
    qg = q.reshape(b_, nq, N_KV_HEADS, GROUP, HEAD_DIM_2)
    s = jnp.einsum('bqkgd,bskd->bkgqs', qg, k, preferred_element_type=jnp.float32) * (HEAD_DIM_2 ** -0.5)
    p = jax.nn.softmax(s, axis=-1).astype(v.dtype)
    o = jnp.einsum('bkgqs,bskd->bqkgd', p, v)
    return o.reshape(b_, nq, N_HEADS_2 * HEAD_DIM_2)

def blocked_attention(q, k_all, v_all):
    b_, n = q.shape[:2]
    n_blk = n // Q_BLOCK
    qb = jnp.moveaxis(q.reshape(b_, n_blk, Q_BLOCK, N_HEADS_2, HEAD_DIM_2), 1, 0)
    o = lax.map(lambda qblk: gqa_attend(qblk, k_all, v_all), qb)
    return jnp.moveaxis(o, 0, 1).reshape(b_, n, N_HEADS_2 * HEAD_DIM_2)

def second_inputs(seed: int = 0) -> dict:
    key = jax.random.key(seed)
    ks = jax.random.split(key, 24)
    n_even = (DEPTH_2 + 1) // 2
    n_odd = DEPTH_2 // 2

    def nrm(k, shape, fan_in, s=1.0):
        return s * jax.random.normal(k, shape, jnp.float32) * (fan_in ** -0.5)

    def gain(k, shape):
        return 1.0 + 0.05 * jax.random.normal(k, shape, jnp.float32)

    return {
        "x": jax.random.normal(ks[0], (BATCH, SEQ, D_MODEL), jnp.float32),
        "c": jax.random.normal(ks[1], (BATCH, D_MODEL), jnp.float32),
        "ctx": jax.random.normal(ks[2], (BATCH, CTX_LEN, D_MODEL), jnp.float32),
        "c_ctx": jax.random.normal(ks[3], (D_MODEL,), jnp.float32),
        "w_mod": nrm(ks[4], (DEPTH_2, D_MODEL, N_MOD * D_MODEL), D_MODEL, 0.5),
        "b_mod": 0.02 * jax.random.normal(ks[5], (DEPTH_2, N_MOD * D_MODEL), jnp.float32),
        "g_ffn1": gain(ks[6], (DEPTH_2, D_MODEL)),
        "w_ffn1_gu": nrm(ks[7], (DEPTH_2, D_MODEL, 2 * D_FF_2), D_MODEL),
        "w_ffn1_down": nrm(ks[8], (DEPTH_2, D_FF_2, D_MODEL), D_FF_2),
        "g_mix": gain(ks[9], (DEPTH_2, D_MODEL)),
        "g_ffn2": gain(ks[10], (DEPTH_2, D_MODEL)),
        "w_ffn2_gu": nrm(ks[11], (DEPTH_2, D_MODEL, 2 * D_FF_2), D_MODEL),
        "w_ffn2_down": nrm(ks[12], (DEPTH_2, D_FF_2, D_MODEL), D_FF_2),
        "g_final": gain(ks[13], (D_MODEL,)),
        "w_in_ab": nrm(ks[14], (n_even, D_MODEL, D_FOURIER + 2 * D_SGU), D_MODEL),
        "g_v": gain(ks[15], (n_even, SGU_GROUPS, SGU_CH)),
        "w_s": nrm(ks[16], (n_even, SGU_GROUPS, CHUNK_2, CHUNK_2), CHUNK_2, 0.5),
        "b_s": 1.0 + 0.02 * jax.random.normal(ks[17], (n_even, SGU_GROUPS, CHUNK_2), jnp.float32),
        "w_out_ab": nrm(ks[18], (n_even, D_FOURIER + D_SGU, D_MODEL), D_FOURIER + D_SGU),
        "w_qkv": nrm(ks[19], (n_odd, D_MODEL, (N_HEADS_2 + 2 * N_KV_HEADS) * HEAD_DIM_2), D_MODEL),
        "g_q": gain(ks[20], (n_odd, HEAD_DIM_2)),
        "g_k": gain(ks[21], (n_odd, HEAD_DIM_2)),
        "w_o": nrm(ks[22], (n_odd, N_HEADS_2 * HEAD_DIM_2, D_MODEL), N_HEADS_2 * HEAD_DIM_2),
    }

def second_block(x, c, ctx, c_ctx, w_mod, b_mod, g_ffn1, w_ffn1_gu, w_ffn1_down, g_mix,
              g_ffn2, w_ffn2_gu, w_ffn2_down, g_final, w_in_ab, g_v, w_s, b_s, w_out_ab,
              w_qkv, g_q, g_k, w_o):
    n_tok = x.shape[1]
    ROWS = n_tok // GRID_W
    ang_row, ang_col = axial_angles(ROWS)
    q_cols = N_HEADS_2 * HEAD_DIM_2

    for l in range(DEPTH_2):
        last = l == DEPTH_2 - 1
        even = l % 2 == 0
        j = l // 2
        mx = adaln(c, w_mod[l], b_mod[l])
        mc = adaln(c_ctx[None], w_mod[l], b_mod[l])
        ctx_live = (not last) or (not even)

        x = ffn_half_step(x, mx[0:3], g_ffn1[l], w_ffn1_gu[l], w_ffn1_down[l])
        if ctx_live:
            ctx = ffn_half_step(ctx, mc[0:3], g_ffn1[l], w_ffn1_gu[l], w_ffn1_down[l])

        hx = modulated_norm(x, g_mix[l], mx[3], mx[4])
        if even:
            out_x = fourier_sgu_mixer(hx, w_in_ab[j], g_v[j], w_s[j], b_s[j], w_out_ab[j])
            if not last:
                hc = modulated_norm(ctx, g_mix[l], mc[3], mc[4])
                out_c = fourier_sgu_mixer(hc, w_in_ab[j], g_v[j], w_s[j], b_s[j], w_out_ab[j])
        else:
            hc = modulated_norm(ctx, g_mix[l], mc[3], mc[4])
            qkv_x = hx @ w_qkv[j]
            q_x = axial_rope(project_q(qkv_x[..., :q_cols], g_q[j]), ang_row, ang_col)
            k_x, v_x = project_kv(qkv_x[..., q_cols:], g_k[j])
            k_x = axial_rope(k_x, ang_row, ang_col)
            if last:
                k_c, v_c = project_kv(hc @ w_qkv[j][:, q_cols:], g_k[j])
            else:
                qkv_c = hc @ w_qkv[j]
                k_c, v_c = project_kv(qkv_c[..., q_cols:], g_k[j])
                q_c = project_q(qkv_c[..., :q_cols], g_q[j])
                out_c = gqa_attend(q_c, k_c, v_c) @ w_o[j]
            k_all = jnp.concatenate([k_x, k_c], axis=1)
            v_all = jnp.concatenate([v_x, v_c], axis=1)
            out_x = blocked_attention(q_x, k_all, v_all) @ w_o[j]

        x = x + mx[5] * out_x
        x = ffn_half_step(x, mx[6:9], g_ffn2[l], w_ffn2_gu[l], w_ffn2_down[l])
        if not last:
            ctx = ctx + mc[5] * out_c
            ctx = ffn_half_step(ctx, mc[6:9], g_ffn2[l], w_ffn2_gu[l], w_ffn2_down[l])

    return rms_norm(x, g_final)


def setup_inputs(seed=0):
    out = dict(first_inputs(seed))
    for name, value in second_inputs(seed + 1).items():
        if name != "x":
            out[name + "_2"] = value
    return out


def reference(
    x, mem, positions, mix_norm_w, w_in, gdn_conv_w, gdn_a_log, gdn_dt_bias, gdn_norm_w,
    gla_gk_up, gla_gk_bias, gla_norm_w, hgrn_lb_logits, hgrn_norm_w, w_out, xattn_norm_w,
    mem_norm_w, xattn_wq, xattn_wk, xattn_wv, xattn_wo, ffn_norm_w, ffn_up, ffn_conv_w,
    ffn_down, final_norm_w, c_2, ctx_2, c_ctx_2, w_mod_2, b_mod_2, g_ffn1_2, w_ffn1_gu_2,
    w_ffn1_down_2, g_mix_2, g_ffn2_2, w_ffn2_gu_2, w_ffn2_down_2, g_final_2, w_in_ab_2, g_v_2,
    w_s_2, b_s_2, w_out_ab_2, w_qkv_2, g_q_2, g_k_2, w_o_2,
):
    x = first_block(
        x, mem, positions, mix_norm_w, w_in, gdn_conv_w, gdn_a_log, gdn_dt_bias, gdn_norm_w,
        gla_gk_up, gla_gk_bias, gla_norm_w, hgrn_lb_logits, hgrn_norm_w, w_out, xattn_norm_w,
        mem_norm_w, xattn_wq, xattn_wk, xattn_wv, xattn_wo, ffn_norm_w, ffn_up, ffn_conv_w,
        ffn_down, final_norm_w,
    )
    return second_block(
        x, c_2, ctx_2, c_ctx_2, w_mod_2, b_mod_2, g_ffn1_2, w_ffn1_gu_2, w_ffn1_down_2, g_mix_2,
        g_ffn2_2, w_ffn2_gu_2, w_ffn2_down_2, g_final_2, w_in_ab_2, g_v_2, w_s_2, b_s_2,
        w_out_ab_2, w_qkv_2, g_q_2, g_k_2, w_o_2,
    )


_drawn_inputs = setup_inputs


def setup_inputs(seed=0):
    import zlib

    import numpy as np

    out = dict(_drawn_inputs(seed))
    spreads = {}
    factors = {'gdn_norm_w': 8.0,
     'gla_gk_bias': 8.0,
     'gla_norm_w': 8.0,
     'hgrn_norm_w': 8.0,
     'xattn_norm_w': 8.0,
     'mem_norm_w': 8.0,
     'ffn_norm_w': 3.953,
     'final_norm_w': 2.733,
     'ctx_2': 3.536,
     'g_ffn1_2': 5.278,
     'g_mix_2': 4.672,
     'g_ffn2_2': 5.176,
     'g_v_2': 8.0,
     'b_s_2': 8.0,
     'g_q_2': 8.0,
     'g_k_2': 8.0}
    for name, (base, spread) in spreads.items():
        noise = np.random.default_rng([zlib.crc32(name.encode()), seed]).standard_normal(out[name].shape)
        drawn = base * np.exp(spread * noise) if base else spread * noise
        out[name] = __import__('jax').numpy.asarray(drawn.astype(out[name].dtype))
    for name, factor in factors.items():
        out[name] = (out[name] * factor).astype(out[name].dtype)
    return out
```

```python
from contextlib import ExitStack

import numpy as np

import concourse.bass as bass
from concourse import mybir

F32 = mybir.dt.float32
F32R = mybir.dt.float32r
I32 = mybir.dt.int32
ACT = mybir.ActivationFunctionType
ALU = mybir.AluOpType
AX_X = mybir.AxisListType.X

P = 128
T = 256
D = 1024
KT = D // P
SLOTS = 3
CHUNK = 2048
EPS = 1e-6
HEADS = 4
HD = 64
FF_TILES = 22
HALF = FF_TILES // 2
LAG = 16
LEVELS = (128, 64, 32, 16)
MAGIC = 1.5 * 2.0**23
TWO_PI_A = 6.28125
TWO_PI_B = 0.0019353071693331003

RQ, RK, BQ, BK, BV, CQ, DQ, CK, DF, RV, CV, DI, RG, BG, CG, DG = 0, 2, 4, 6, 8, 10, 11, 13, 14, 16, 18, 20, 22, 24, 26, 28
Z_TILES = 30


class Job:

    def __init__(self, base, n, size, dram, first=False):
        self.base, self.n, self.size, self.dram, self.first = base, n, size, dram, first


class Step:

    def __init__(self, job, c, u):
        self.job, self.c = job, c
        self.g = c + job.base
        self.static = c if isinstance(c, int) else None
        self.slot = (job.base + u) % SLOTS
        self.bank = 2 * self.slot


def steps(eng, job, ahead=0):
    loops = max(0, job.n - ahead) // SLOTS
    done = 0
    if loops >= 2:
        peeled = 1 if job.first else 0
        for c in range(peeled * SLOTS):
            s = Step(job, c, c)
            s.turn = (job.base + c) // SLOTS
            s.looped = False
            yield s
        with eng.Fori(peeled, loops) as i:
            for u in range(SLOTS):
                s = Step(job, i * SLOTS + u, u)
                s.turn = i + (job.base + u) // SLOTS
                s.looped = True
                s.i = i
                s.u = u
                yield s
        done = loops * SLOTS
    for c in range(done, job.n):
        s = Step(job, c, c)
        s.turn = (job.base + c) // SLOTS
        s.looped = False
        yield s


def build(nc, io, plan):
    jobs = {}
    sizes = []
    for name, n, size, dram in plan:
        jobs[name] = Job(len(sizes), n, size, dram, first=name in ("w_in_a", "ffn_up0"))
        sizes += [size] * n
    total = len(sizes)

    with ExitStack() as ctx:
        def sb(name, shape, dt=F32, scope=ctx):
            return scope.enter_context(nc.sbuf_tensor(name, shape, dt))

        def sem(name):
            return ctx.enter_context(nc.semaphore(name))

        psum = ctx.enter_context(nc.psum_tensor("psum", [P, 8, 512], F32))

        raw = sb("raw", [P, SLOTS, CHUNK])
        w_hi = sb("w_hi", [P, SLOTS, CHUNK], F32R)
        w_lo = sb("w_lo", [P, SLOTS, CHUNK], F32R)
        xc = sb("xc", [P, KT, 2 * T])
        xn_hi = sb("xn_hi", [P, KT, 2 * T], F32R)
        xn_lo = sb("xn_lo", [P, KT, 2 * T], F32R)
        small = sb("small", [P, io["small"].shape[1]])
        ident = sb("ident", [P, P])
        ones = sb("ones", [P, P])
        rot = sb("rot", [P, P])
        row_sums = sb("row_sums", [P, 2])
        zeros = sb("zeros", [P, T + P], mybir.dt.bfloat16)
        work = sb("work", [P, 8192])
        nrm = work[:, 0:KT * 2 * T].rearrange("p (k t) -> p k t", k=KT)
        rstd = sb("rstd", [P, 2 * T])
        mean = sb("mean", [P, 2 * T])
        mods = sb("mods", [P, 144, 2])
        gains = sb("gains", [P, 6, KT])
        scales = sb("scales", [P, 6, KT, 2])
        b_mod = sb("b_mod", [P, 144])
        c_in = sb("c_in", [P, KT, 2])
        c4 = sb("c4", [P, KT, 4], F32R)
        X = slice(0, T)
        C = slice(T, 2 * T)
        XC = slice(0, 2 * T)

        cols = io["cols"]

        def col(name, k=0):
            return small[:, cols[name] + k:cols[name] + k + 1]

        raw_landed = [sem(f"raw_landed{s}") for s in range(SLOTS)]
        tables_in = sem("tables_in")
        start_in = sem("start_in")
        hi_ready = sem("hi_ready")
        lo_ready = sem("lo_ready")
        chunk_done = sem("chunk_done")
        evacuated = sem("evacuated")

        def load(sp, s):
            if s.looped or s.g >= SLOTS:
                sp.wait_ge(lo_ready, s.g + (1 - SLOTS))
            sp.dma_start(raw[:, s.slot, 0:s.job.size], s.job.dram[s.c]).then_inc(raw_landed[s.slot], 16)

        def split_hi(act, s, ahead=2):
            if not s.looped and s.g + ahead >= total:
                return
            slot = (s.slot + ahead) % SLOTS
            size = s.job.size if s.looped else sizes[s.g + ahead]
            g = s.g + ahead
            turn = (s.i + (s.job.base + s.u + ahead) // SLOTS) if s.looped else g // SLOTS
            act.wait_ge(raw_landed[slot], turn * 16 + 16)
            if s.looped or g >= SLOTS:
                act.wait_ge(chunk_done, s.g + (ahead + 1 - SLOTS))
            act.activation(w_hi[:, slot, 0:size], raw[:, slot, 0:size], ACT.Copy).then_inc(hi_ready, 1)

        def split_lo(dve, s, ahead=2):
            if not s.looped and s.g + ahead >= total:
                return
            slot = (s.slot + ahead) % SLOTS
            size = s.job.size if s.looped else sizes[s.g + ahead]
            dve.wait_ge(hi_ready, s.g + (ahead + 1))
            dve.tensor_tensor(w_lo[:, slot, 0:size], raw[:, slot, 0:size], w_hi[:, slot, 0:size].bitcast(F32),
                              ALU.subtract).then_inc(lo_ready, 1)

        def first_splits(eng, split):
            for c in range(2):
                s = Step(Job(0, total, 0, None), c - 2, c - 2)
                s.g = c - 2
                s.slot = (c - 2) % SLOTS
                s.looped = False
                split(eng, s)

        def bank_free(pe, s):
            if s.looped or s.g >= SLOTS:
                pe.wait_ge(evacuated, s.g + (1 - SLOTS))

        def three_passes(pe, out, lhs, rhs, first, last, group=False):
            (lh, ll), (rh, rl) = lhs, rhs
            pe.matmul(out, lh, rh, start=first, stop=False, skip_group_check=group)
            pe.matmul(out, lh, rl, start=False, stop=False, skip_group_check=group)
            return pe.matmul(out, ll, rh, start=False, stop=last, skip_group_check=group)

        def pe_feature_major(pe, job, act_hi, act_lo, span, n_tiles=2, k_tiles=KT, before_k=None):
            for s in steps(pe, job):
                bank_free(pe, s)
                pe.wait_ge(lo_ready, s.g + 1)
                for n in range(n_tiles):
                    for k in range(k_tiles):
                        if before_k is not None and n == 0:
                            before_k(s, k)
                        w = slice((n * k_tiles + k) * P, (n * k_tiles + k + 1) * P)
                        mm = three_passes(pe, psum[:, s.bank + n, 0:span.stop - span.start],
                                          (w_hi[:, s.slot, w], w_lo[:, s.slot, w]),
                                          (act_hi[:, k, span], act_lo[:, k, span]), k == 0, k == k_tiles - 1)
                mm.then_inc(chunk_done, 1)

        def pe_token_major(pe, job, span):
            for s in steps(pe, job):
                bank_free(pe, s)
                pe.wait_ge(lo_ready, s.g + 1)
                for tt in range((span.stop - span.start) // P):
                    tok = slice(span.start + tt * P, span.start + (tt + 1) * P)
                    for k in range(KT):
                        w = slice(k * 256, (k + 1) * 256)
                        mm = three_passes(pe, psum[:, s.bank + tt // 2, (tt % 2) * 256:(tt % 2) * 256 + 256],
                                          (xn_hi[:, k, tok], xn_lo[:, k, tok]),
                                          (w_hi[:, s.slot, w], w_lo[:, s.slot, w]), k == 0, k == KT - 1)
                mm.then_inc(chunk_done, 1)

        n_sq, n_sum, n_mean, n_guess, n_rstd, n_scaled, n_hi, n_lo = [sem(x) for x in (
            "norm_squares", "norm_sums", "norm_mean", "norm_guess", "norm_rstd", "norm_scaled", "norm_hi", "norm_lo")]

        class Norm:
            made, scaled, split = 0, 0, 0

            def __init__(self, span, scale, shift=None, out=None):
                self.j, self.span, self.scale, self.shift, self.out = Norm.made, span, scale, shift, out
                self.w = span.stop - span.start
                self.halves = self.w // T
                self.scaled_base, self.split_base = Norm.scaled, Norm.split
                Norm.made += 1
                Norm.scaled += KT * self.halves
                Norm.split += 0 if out is not None else KT * self.halves

            def act_squares(self, act):
                act.activation(nrm[:, :, 0:self.w], xc[:, :, self.span], ACT.Square).then_inc(n_sq, 1)

            def pe(self, pe):
                pe.wait_ge(n_sq, self.j + 1)
                for k in range(KT):
                    mm = pe.matmul(psum[:, 6, 0:self.w], ones[:, :], nrm[:, k, 0:self.w], start=(k == 0), stop=(k == KT - 1))
                mm.then_inc(n_sum, 1)

            def act_rest(self, act):
                act.wait_ge(n_mean, self.j + 1)
                act.activation(rstd[:, 0:self.w], mean[:, 0:self.w], ACT.Abs_reciprocal_sqrt).then_inc(n_guess, 1)
                if self.out is not None:
                    return
                for k in range(KT):
                    act.wait_ge(n_scaled, self.scaled_base + (k + 1) * self.halves)
                    for h in range(self.halves):
                        t, o = slice(h * T, (h + 1) * T), slice(self.span.start + h * T, self.span.start + (h + 1) * T)
                        if self.shift is None:
                            act.activation(xn_hi[:, k, o], nrm[:, k, t], ACT.Copy).then_inc(n_hi, 1)
                        else:
                            act.activation(xn_hi[:, k, o], nrm[:, k, t], ACT.Identity, bias=self.shift(k, h)).then_inc(n_hi, 1)

            def dve(self, dve):
                m, r, j3 = mean[:, 0:self.w], rstd[:, 0:self.w], 3 * self.j
                tmp = work[:, 7168:7168 + self.w]
                dve.wait_ge(n_sum, self.j + 1)
                dve.tensor_scalar(m, psum[:, 6, 0:self.w], 1.0 / D, EPS, ALU.mult, ALU.add).then_inc(n_mean, 1)
                dve.wait_ge(n_guess, self.j + 1)
                dve.scalar_tensor_tensor(tmp, r, -0.5, r, ALU.mult, ALU.mult).then_inc(n_rstd, 1)
                dve.wait_ge(n_rstd, j3 + 1)
                dve.tensor_tensor(tmp, tmp, m, ALU.mult).then_inc(n_rstd, 1)
                dve.wait_ge(n_rstd, j3 + 2)
                dve.scalar_tensor_tensor(r, tmp, 1.5, r, ALU.add, ALU.mult).then_inc(n_rstd, 1)
                dve.wait_ge(n_rstd, j3 + 3)

                def low(k):
                    dve.wait_ge(n_hi, self.split_base + (k + 1) * self.halves)
                    for h in range(self.halves):
                        t, o = slice(h * T, (h + 1) * T), slice(self.span.start + h * T, self.span.start + (h + 1) * T)
                        if self.shift is None:
                            dve.tensor_tensor(xn_lo[:, k, o], nrm[:, k, t], xn_hi[:, k, o].bitcast(F32), ALU.subtract).then_inc(n_lo, 1)
                        else:
                            dve.scalar_tensor_tensor(xn_lo[:, k, o], nrm[:, k, t], self.shift(k, h), xn_hi[:, k, o].bitcast(F32),
                                                     ALU.add, ALU.subtract).then_inc(n_lo, 1)

                for k in range(KT):
                    for h in range(self.halves):
                        t, o = slice(h * T, (h + 1) * T), slice(self.span.start + h * T, self.span.start + (h + 1) * T)
                        dst = nrm[:, k, t] if self.out is None else self.out[:, k, t]
                        dve.scalar_tensor_tensor(dst, xc[:, k, o], self.scale(k, h), r[:, t], ALU.mult, ALU.mult).then_inc(n_scaled, 1)
                    if self.out is None and k:
                        low(k - 1)
                if self.out is None:
                    low(KT - 1)

            def ready(self, pe, k):
                pe.wait_ge(n_lo, self.split_base + (k + 1) * self.halves)

        AT = {
            "ret_act": dict(sines=2),
            "ret_dve": dict(angle=6, rotated=11, v_tok=12, decayed=14, out=15),
            "ret_pe": dict(turned=1, v_tok=2, scores=3, out=4),
            "gdn_act": dict(taps=1, softplus=4, rate=5, beta=6, silu=7, squares=8, rsqrt=9, tail=10, col_decays=11,
                            ratio=12, q_decay=13),
            "gdn_dve": dict(cleared=1, conv=4, rows=7, tok=8, spread=10, cums=11, cum_rows=12, beta_rows=13, tail=14,
                            log_ratio=16, sums=17, unit=22, tokens=24, strict=31, products=38, u0=39,
                            s1=40, rest=42, u1=43, out=44),
            "gdn_pe": dict(tok=1, cums=2, cum_rows=3, beta_rows=4, sums=5, tokens=6, kk=7, u0=8, s1=9, w=10, u1=11,
                           out=12),
            "gat_act": dict(u=1, ln=4, key=5),
            "gat_dve": dict(u=1, log_f=3, scaled=4, tok=6, out=7),
            "gat_pe": dict(gk=1, tok=2, zero=3, out=4),
            "post_act": dict(squares=1, rsqrt=2),
            "post_dve": dict(mean=1, unit=4, scaled=13),
            "post_pe": dict(sums=1),
        }
        stage_sem = {name: sem(name) for name in AT}

        class order:
            def __init__(self, eng, name):
                self.eng, self.name, self.n = eng, name, 0

            def __call__(self, ins, result=None):
                self.n += 1
                ins.then_inc(stage_sem[self.name], 1)
                if result is not None:
                    assert AT[self.name][result] == self.n, (self.name, result, self.n)
                self.eng.wait_ge(stage_sem[self.name], self.n)

        def need(eng, name, result):
            eng.wait_ge(stage_sem[name], AT[name][result])

        def bank(b):
            return psum[:, b, :]

        def area(at, n, w=P):
            return work[:, at:at + n * w].rearrange("p (n t) -> p n t", t=w)

        mix = ExitStack()
        z = sb("z", [P, Z_TILES, T], scope=mix)
        zs = sb("zs", [P, T], scope=mix)
        headones = sb("headones", [P, P], scope=mix)
        lagsel = sb("lagsel", [P, 2, P], scope=mix)
        triu = sb("triu", [P, P], scope=mix)
        triu_strict = sb("triu_strict", [P, P], scope=mix)
        second_half = sb("second_half", [P, 7, P], scope=mix)
        decay = sb("decay", [P, HEADS, T], scope=mix)
        gk_up = sb("gk_up", [P, P], scope=mix)
        pos = sb("pos", [P, T], I32, scope=mix)
        gt = sb("gt", [P, 2, P], scope=mix)
        s1 = sb("s1", [P, 2, HD], scope=mix)
        MIX = ["headones", "lagsel", "triu", "triu_strict", "second_half", "decay", "gk_up", "pos"]
        MIX_T = dict(headones=headones, lagsel=lagsel, triu=triu, triu_strict=triu_strict, second_half=second_half,
                     decay=decay, gk_up=gk_up, pos=pos)

        def load_mixer_tables(sp):
            for name in MIX:
                sp.dma_start(MIX_T[name][:], io[name]).then_inc(tables_in, 16)

        ret_a = work[:, 10 * T:16 * T].rearrange("p (h n) -> p h n", h=HEADS)
        ret_v = area(8 * T, 2, T)

        def retention_dve(dve):
            o = order(dve, "ret_dve")
            ang, kk_, sn = work[:, 0:T], work[:, T:2 * T], work[:, 2 * T:3 * T]
            dve.wait_ge(tables_in, 16 * len(MIX))
            o(dve.tensor_copy(ang, pos[:, :]))
            o(dve.tensor_scalar(ang, ang, col("freq"), None, ALU.mult))
            o(dve.tensor_scalar(kk_, ang, 1.0 / (2 * np.pi), MAGIC, ALU.mult, ALU.add))
            o(dve.tensor_scalar(kk_, kk_, MAGIC, None, ALU.subtract))
            o(dve.scalar_tensor_tensor(ang, kk_, -TWO_PI_A, ang, ALU.mult, ALU.add))
            o(dve.scalar_tensor_tensor(ang, kk_, -TWO_PI_B, ang, ALU.mult, ALU.add), "angle")
            need(dve, "ret_act", "sines")
            o(dve.tensor_tensor(kk_, sn, sn, ALU.mult))
            o(dve.tensor_scalar(kk_, kk_, -2.0, 1.0, ALU.mult, ALU.add))
            qk = z[:, RQ:RQ + 4, :]
            turned = psum[:, 0:2, :].rearrange("p b (t n) -> p (b t) n", n=T)
            part = area(4 * T, 4, T)
            need(dve, "ret_pe", "turned")
            sines = work[:, 3 * T:4 * T].unsqueeze(1).to_broadcast([P, 4, T])
            coss = kk_.unsqueeze(1).to_broadcast([P, 4, T])
            o(dve.tensor_tensor(part, turned, sines, ALU.mult))
            o(dve.tensor_tensor(qk, qk, coss, ALU.mult))
            o(dve.tensor_tensor(qk, qk, part, ALU.add), "rotated")
            need(dve, "ret_pe", "v_tok")
            o(dve.tensor_copy(ret_v, psum[:, 2, :].rearrange("p (t n) -> p t n", n=T)), "v_tok")
            need(dve, "ret_pe", "scores")
            o(dve.tensor_tensor(ret_a[:, :, 0:T], psum[:, 3:7, 0:T], decay[:, :, :], ALU.mult))
            o(dve.tensor_tensor(ret_a[:, :, T:T + P], psum[:, 3:7, T:T + P], decay[:, :, 0:P], ALU.mult), "decayed")
            need(dve, "ret_pe", "out")
            o(dve.tensor_copy(z[:, 0:2, :], psum[:, 7, :].rearrange("p (t n) -> p t n", n=T)), "out")

        def retention_act(act):
            o = order(act, "ret_act")
            need(act, "ret_dve", "angle")
            o(act.activation(work[:, 2 * T:3 * T], work[:, 0:T], ACT.Sin, scale=0.5))
            o(act.activation(work[:, 3 * T:4 * T], work[:, 0:T], ACT.Sin), "sines")

        def retention_pe(pe):
            pe.wait_ge(evacuated, jobs["w_in_small"].base + 1)
            pe.wait_ge(tables_in, 16 * len(MIX))
            o = order(pe, "ret_pe")
            pe.matmul(bank(0), rot[:, :], z[:, RQ:RQ + 2, :], start=True, stop=True)
            o(pe.matmul(bank(1), rot[:, :], z[:, RK:RK + 2, :], start=True, stop=True), "turned")
            for tt in range(2):
                for n in range(2):
                    mm = pe.transpose(psum[:, 2, tt * T + n * P:tt * T + (n + 1) * P], z[:, RV + n, tt * P:(tt + 1) * P], ident[:, :])
            o(mm, "v_tok")
            need(pe, "ret_dve", "rotated")
            for h in range(HEADS):
                r = slice((h % 2) * HD, (h % 2) * HD + HD)
                for st in range(2):
                    mm = pe.matmul(psum[:, 3 + h, st * T:st * T + T - st * P], z[r, RK + h // 2, st * P:(st + 1) * P],
                                   z[r, RQ + h // 2, st * P:T], start=True, stop=True)
            o(mm, "scores")
            need(pe, "ret_dve", "decayed")
            for h in range(HEADS):
                r = slice((h % 2) * HD, (h % 2) * HD + HD)
                c = (h // 2) * T
                v = slice(h * HD, (h + 1) * HD)
                pe.matmul(psum[r, 7, c:c + T], ret_v[:, 0, v], ret_a[:, h, 0:T], start=True, stop=False, skip_group_check=True)
                mm = pe.matmul(psum[r, 7, c + P:c + T], ret_v[:, 1, v], ret_a[:, h, T:T + P], start=False, stop=True, skip_group_check=True)
            o(mm, "out")

        XM, XT, NT, QT, YM, BR, GR, RT = (area(i * 1024, 8) for i in range(8))
        taps = area(0, 6, T)
        ssum, unit_tmp = area(0, 4, T), area(1024, 4, T)
        g_spread, b_spread = NT, QT
        sq4 = area(4096, 4, T)
        gb = work[:, 5120:5120 + T]
        U0, U1, REST = (work[:, 5120 + i * T:5120 + (i + 1) * T] for i in range(3))
        qg = area(5120 + 3 * T, 2)
        k_tok, v_tok = z[:, 16:18, :], z[:, 2:4, :]
        gcol, bcol, gam = (small[:, cols[x]:cols[x] + 8].rearrange("p (n h) -> p n h", n=2) for x in ("gcol", "bcol", "gam"))
        tailc = small[:, cols["tailc"]:cols["tailc"] + 4]
        level_y, level_x, level_pe = sem("inverse_masked"), sem("inverse_updated"), sem("inverse_products")

        def by_head(ap):
            return ap.rearrange("p n (h d) -> p n h d", d=HD)

        def by_parity(ap, n):
            return ap[:, n * 4:n * 4 + 4, :].rearrange("p (b a) t -> p a b t", a=2)

        def two_banks(b, w=P):
            return psum[:, b:b + 2, :].rearrange("p b (n t) -> p (b n) t", t=w)

        def newton(dve, o, y, v, tmp, result=None):
            o(dve.scalar_tensor_tensor(tmp, y, -0.5, y, ALU.mult, ALU.mult))
            o(dve.tensor_tensor(tmp, tmp, v, ALU.mult))
            o(dve.scalar_tensor_tensor(y, tmp, 1.5, y, ALU.add, ALU.mult), result)

        def delta_act(act):
            o = order(act, "gdn_act")
            need(act, "ret_dve", "out")
            for k in range(6):
                mm = act.activation(taps[:, k, :], z[:, BQ + k, :], ACT.Copy, scale=col("gdn_conv3", k))
            o(mm, "taps")
            need(act, "gdn_dve", "cleared")
            o(act.activation(gb[0:4, :], zs[0:4, :], ACT.Abs, bias=col("gdn_dt")[0:4, :]))
            o(act.activation(gb[0:4, :], gb[0:4, :], ACT.Exp, scale=-1.0))
            o(act.activation(gb[0:4, :], gb[0:4, :], ACT.Ln, bias=1.0), "softplus")
            o(act.activation(col("rate")[0:4, :], col("gdn_a_log")[0:4, :], ACT.Exp), "rate")
            o(act.activation(gb[32:36, :], zs[32:36, :], ACT.Sigmoid), "beta")
            need(act, "gdn_dve", "conv")
            o(act.activation(z[:, BQ:BQ + 6, :], taps, ACT.Silu), "silu")
            o(act.activation(sq4, z[:, BQ:BQ + 4, :], ACT.Square), "squares")
            need(act, "gdn_dve", "sums")
            o(act.activation(sq4, ssum, ACT.Abs_reciprocal_sqrt), "rsqrt")
            o(act.activation(tailc, tailc, ACT.Exp), "tail")
            o(act.activation(gam, gcol, ACT.Exp), "col_decays")
            o(act.activation(RT, RT, ACT.Exp), "ratio")
            o(act.activation(GR[:, 4:8, :], GR[:, 4:8, :], ACT.Exp), "q_decay")

        def delta_dve(dve):
            o = order(dve, "gdn_dve")
            o(dve.memset(gb, 0.0), "cleared")
            need(dve, "gdn_act", "taps")
            for back in range(1, 4):
                for k in range(6):
                    mm = dve.scalar_tensor_tensor(taps[:, k, back:T], z[:, BQ + k, 0:T - back], col(f"gdn_conv{3 - back}", k),
                                                  taps[:, k, back:T], ALU.mult, ALU.add)
                o(mm, "conv" if back == 3 else None)
            need(dve, "gdn_act", "beta")
            o(dve.tensor_scalar(zs[0:4, :], zs[0:4, :], col("gdn_dt")[0:4, :], 0.0, ALU.add, ALU.max))
            o(dve.tensor_tensor(gb[0:4, :], gb[0:4, :], zs[0:4, :], ALU.add))
            o(dve.tensor_scalar(gb[0:4, :], gb[0:4, :], col("rate")[0:4, :], -1.0, ALU.mult, ALU.mult), "rows")
            need(dve, "gdn_pe", "tok")
            o(dve.tensor_copy(gt[:, :, :], psum[:, 0, 0:2 * P].rearrange("p (n t) -> p n t", n=2)), "tok")
            for dst, c in ((g_spread, 0), (b_spread, 32)):
                o(dve.tensor_copy(dst.rearrange("p (n h) t -> p n h t", n=2),
                                  gt[:, :, c:c + 4].unsqueeze(3).to_broadcast([P, 2, HEADS, P])), "spread" if c else None)
            need(dve, "gdn_pe", "cums")
            o(dve.tensor_copy(gcol, psum[:, 1, 0:8].rearrange("p (n h) -> p n h", n=2)), "cums")
            need(dve, "gdn_pe", "cum_rows")
            o(dve.tensor_copy(GR, two_banks(2)), "cum_rows")
            need(dve, "gdn_pe", "beta_rows")
            o(dve.tensor_copy(BR, two_banks(4)), "beta_rows")
            o(dve.tensor_tensor(tailc, GR[:, 0:4, P - 1], gcol[:, 0, :], ALU.subtract), "tail")
            gc8 = small[:, cols["gcol"]:cols["gcol"] + 8].unsqueeze(2).to_broadcast([P, 8, P])
            o(dve.tensor_tensor(RT, GR, gc8, ALU.subtract))
            o(dve.tensor_scalar(RT, RT, 0.0, None, ALU.min), "log_ratio")
            need(dve, "gdn_pe", "sums")
            o(dve.tensor_scalar(ssum, two_banks(6, T), EPS, None, ALU.add), "sums")
            need(dve, "gdn_act", "rsqrt")
            newton(dve, o, sq4, ssum, unit_tmp)
            qs, ks = z[:, BQ:BQ + 2, :], z[:, BK:BK + 2, :]
            o(dve.scalar_tensor_tensor(qs, qs, HD ** -0.5, sq4[:, 0:2, :], ALU.mult, ALU.mult))
            o(dve.tensor_tensor(ks, ks, sq4[:, 2:4, :], ALU.mult), "unit")
            need(dve, "gdn_pe", "tokens")
            o(dve.tensor_copy(k_tok, psum[:, 0, :].rearrange("p (n t) -> p n t", n=2)))
            beta = gt[:, :, 32:36]
            o(dve.tensor_tensor(by_head(v_tok), by_head(psum[:, 1, :].rearrange("p (n t) -> p n t", n=2)),
                                beta.unsqueeze(3).to_broadcast([P, 2, HEADS, HD]), ALU.mult), "tokens")
            need(dve, "gdn_act", "q_decay")
            o(dve.tensor_tensor(RT, RT, triu[:, :].unsqueeze(1).to_broadcast([P, 8, P]), ALU.mult))
            o(dve.tensor_tensor(BR, BR, RT, ALU.mult))
            o(dve.tensor_tensor(BR, BR, triu_strict[:, :].unsqueeze(1).to_broadcast([P, 8, P]), ALU.mult))
            o(dve.tensor_tensor(bcol, beta, gam, ALU.mult))
            k0 = k_tok[:, 0, :].rearrange("p (h d) -> p h d", d=HD)
            o(dve.tensor_tensor(k0, k0, tailc.unsqueeze(2).to_broadcast([P, HEADS, HD]), ALU.mult))
            need(dve, "gdn_pe", "kk")
            for dst, b, factor in ((NT, 2, BR), (QT, 4, RT)):
                for n in range(2):
                    o(dve.tensor_tensor(by_parity(dst, n), psum[:, b:b + 2, n * T:(n + 1) * T].rearrange("p a (b t) -> p a b t", t=P),
                                        by_parity(factor, n), ALU.mult), "strict" if b == 2 and n else None)
            for h in range(HEADS):
                r = slice((h % 2) * HD, (h % 2) * HD + HD)
                o(dve.tensor_tensor(qg[r, h // 2, :], z[r, BQ + h // 2, P:T], GR[r, 4 + h, :], ALU.mult))
            o(dve.tensor_copy(XM, ident[:, :].unsqueeze(1).to_broadcast([P, 8, P])), "products")
            dve.tensor_copy(XT, ident[:, :].unsqueeze(1).to_broadcast([P, 8, P])).then_inc(level_x, 1)
            with dve.Fori(0, 7) as i:
                dve.wait_ge(level_pe, i * 2 + 1)
                dve.tensor_tensor(YM, two_banks(0), second_half[:, bass.ds(i, 1), :].to_broadcast([P, 8, P]), ALU.mult).then_inc(level_y, 1)
                dve.wait_ge(level_pe, i * 2 + 2)
                dve.tensor_tensor(XT, XT, two_banks(4), ALU.subtract).then_inc(level_x, 1)
                dve.tensor_tensor(XM, XM, two_banks(2), ALU.subtract).then_inc(level_x, 1)
                dve.wait_ge(level_x, i * 2 + 3)
            need(dve, "gdn_pe", "u0")
            o(dve.tensor_copy(U0, psum[:, 6, 0:T]), "u0")
            need(dve, "gdn_pe", "s1")
            o(dve.tensor_copy(s1[:, :, :], psum[:, 7, 0:P].rearrange("p (n d) -> p n d", d=HD)), "s1")
            need(dve, "gdn_pe", "w")
            o(dve.tensor_tensor(REST.rearrange("p (b a d) -> p a b d", a=2, d=HD), psum[:, 0:2, 0:P].rearrange("p a (b d) -> p a b d", d=HD),
                                bcol[:, 1, :].rearrange("p (b a) -> p a b", a=2).unsqueeze(3).to_broadcast([P, 2, 2, HD]), ALU.mult))
            o(dve.tensor_tensor(REST, v_tok[:, 1, :], REST, ALU.subtract), "rest")
            need(dve, "gdn_pe", "u1")
            o(dve.tensor_copy(U1, psum[:, 1, 0:T]), "u1")
            need(dve, "gdn_pe", "out")
            o(dve.tensor_copy(z[:, 2:4, :], psum[:, 2, :].rearrange("p (n t) -> p n t", n=2)), "out")

        def delta_pe(pe):
            o = order(pe, "gdn_pe")
            heads4 = [(h, slice((h % 2) * HD, (h % 2) * HD + HD), slice(h * HD, (h + 1) * HD)) for h in range(HEADS)]
            need(pe, "gdn_dve", "rows")
            need(pe, "gdn_act", "beta")
            for n in range(2):
                mm = pe.transpose(psum[:, 0, n * P:(n + 1) * P], gb[:, n * P:(n + 1) * P], ident[:, :])
            o(mm, "tok")
            need(pe, "gdn_dve", "tok")
            for n in range(2):
                mm = pe.matmul(psum[:, 1, n * 4:n * 4 + 4], triu[:, :], gt[:, n, 0:4], start=True, stop=True)
            o(mm, "cums")
            need(pe, "gdn_dve", "spread")
            for nh in range(8):
                mm = pe.matmul(two_banks(2)[:, nh, :], g_spread[:, nh, :], triu[:, :], start=True, stop=True)
            o(mm, "cum_rows")
            for nh in range(8):
                mm = pe.matmul(two_banks(4)[:, nh, :], b_spread[:, nh, :], ident[:, :], start=True, stop=True)
            o(mm, "beta_rows")
            need(pe, "gdn_act", "squares")
            need(pe, "ret_dve", "out")
            for i in range(2):
                mm = pe.matmul(bank(6 + i), headones[:, :], sq4[:, 2 * i:2 * i + 2, :], start=True, stop=True)
            o(mm, "sums")
            need(pe, "gdn_dve", "unit")
            for b, tile in ((0, BK), (1, BV)):
                for n in range(2):
                    for i in range(2):
                        mm = pe.transpose(psum[:, b, n * T + i * P:n * T + (i + 1) * P], z[:, tile + i, n * P:(n + 1) * P], ident[:, :])
            o(mm, "tokens")
            for b, tile in ((2, BK), (4, BQ)):
                for n in range(2):
                    for h, r, _ in heads4:
                        mm = pe.matmul(psum[:, b + h % 2, (n * 2 + h // 2) * P:(n * 2 + h // 2 + 1) * P], z[r, BK + h // 2, n * P:(n + 1) * P],
                                       z[r, tile + h // 2, n * P:(n + 1) * P], start=True, stop=True)
            o(mm, "kk")
            need(pe, "gdn_dve", "products")
            with pe.Fori(0, 7) as i:
                pe.wait_ge(level_x, i * 2 + 1)
                for nh in range(8):
                    mm = pe.matmul(two_banks(0)[:, nh, :], NT[:, nh, :], XM[:, nh, :], start=True, stop=True)
                mm.then_inc(level_pe, 1)
                pe.wait_ge(level_y, i + 1)
                for nh in range(8):
                    pe.matmul(two_banks(4)[:, nh, :], YM[:, nh, :], XT[:, nh, :], start=True, stop=True)
                    mm = pe.matmul(two_banks(2)[:, nh, :], XT[:, nh, :], YM[:, nh, :], start=True, stop=True)
                mm.then_inc(level_pe, 1)
            pe.wait_ge(level_x, 15)
            for h, _, f in heads4:
                mm = pe.matmul(psum[:, 6, f], XT[:, h, :], v_tok[:, 0, f], start=True, stop=True)
            o(mm, "u0")
            need(pe, "gdn_dve", "u0")
            for h, r, f in heads4:
                mm = pe.matmul(psum[r, 7, (h // 2) * HD:(h // 2) * HD + HD], k_tok[:, 0, f], U0[:, f], start=True, stop=True)
            o(mm, "s1")
            need(pe, "gdn_dve", "s1")
            for h, r, f in heads4:
                mm = pe.matmul(psum[:, h % 2, (h // 2) * HD:(h // 2) * HD + HD], z[r, BK + h // 2, P:T], s1[r, h // 2, :], start=True, stop=True)
            o(mm, "w")
            need(pe, "gdn_dve", "rest")
            for h, _, f in heads4:
                mm = pe.matmul(psum[:, 1, f], XT[:, 4 + h, :], REST[:, f], start=True, stop=True)
            o(mm, "u1")
            need(pe, "gdn_dve", "u1")
            for h, r, f in heads4:
                c = (h // 2) * T
                pe.matmul(psum[r, 2, c:c + P], U0[:, f], QT[:, h, :], start=True, stop=True)
                pe.matmul(psum[r, 2, c + P:c + T], U1[:, f], QT[:, 4 + h, :], start=True, stop=False)
                mm = pe.matmul(psum[r, 2, c + P:c + T], s1[r, h // 2, :], qg[r, h // 2, :], start=False, stop=True)
            o(mm, "out")

        Q3, K3, V4, O4 = z[:, CQ:CQ + 3, :], z[:, CK:CK + 3, :], z[:, CV:CV + 4, :], z[:, 4:8, :]
        U3, C3, E3 = area(0, 3, T), area(768, 3, T), area(1536, 3, T)
        QK = [area(2304, 3, T), area(3072, 3, T)]
        A8 = area(3840, 8, T + P)
        resets = area(6912, 4, T)
        toks = [z[:, 16:18, :], z[:, 8:10, :]]
        LE = [area(1536, 3, T), area(0, 3, T)]
        LTMP = [area(3840, 4, T), area(4864, 4, T)]
        lv_cum, lv_exp, lv_qk, lv_pe = sem("level_cum"), sem("level_decays"), sem("level_scaled"), sem("level_scores")
        copied = sem("scores_copied")
        lag_diff, lag_exp, lag_p, lag_bc, lag_tmp, lag_acc = (sem(x) for x in (
            "lag_diff", "lag_decays", "lag_products", "lag_spread", "lag_values", "lag_added"))

        def halves_of(ap, L, side):
            return ap.rearrange("p g (b s l) -> p (g b) s l", s=2, l=L)[:, :, side, :]

        def gated_dve(dve):
            o = order(dve, "gat_dve")
            o(dve.tensor_copy(U3[:, 1:3, :], z[:, DF:DF + 2, :]), "u")
            need(dve, "gat_act", "ln")
            o(dve.scalar_tensor_tensor(U3, U3, 0.0, E3, ALU.min, ALU.subtract))
            o(dve.tensor_scalar(U3[:, 0, :], U3[:, 0, :], 1.0 / 16.0, None, ALU.mult), "log_f")
            o(dve.tensor_scalar(z[:, CQ, :], z[:, CQ, :], (HD // 2) ** -0.5, None, ALU.mult), "scaled")
            need(dve, "gat_pe", "tok")
            for i in range(2):
                o(dve.tensor_copy(toks[i], psum[:, 1 + i, :].rearrange("p (n t) -> p n t", n=2)), "tok" if i else None)
            for i, L in enumerate(LEVELS):
                dve.memset(resets[:, i, :], 1.0).then_inc(lv_cum, 1)
                dve.wait_ge(lv_cum, 2 * i + 1)
                dve.memset(resets[:, i, :].rearrange("p (b l) -> p b l", l=L)[:, :, 0], 0.0).then_inc(lv_cum, 1)
            dve.wait_ge(lv_cum, 8)
            need(dve, "gat_act", "key")
            for i, L in enumerate(LEVELS):
                if i:
                    dve.wait_ge(lv_exp, 2 * i)
                for g in range(3):
                    mm = dve.tensor_tensor_scan(C3[:, g, :], resets[:, i, :], U3[:, g, :], 0.0, ALU.mult, ALU.add)
                mm.then_inc(lv_cum, 1)
                dve.wait_ge(lv_cum, 8 + 2 * i + 1)
                left = halves_of(C3, L, 0)
                dve.tensor_tensor(halves_of(E3, L, 0), left[:, :, L - 1:L].to_broadcast([P, left.shape[1], L]), left,
                                  ALU.subtract).then_inc(lv_cum, 1)
                dve.wait_ge(lv_exp, 2 * i + 2)
                if i >= 2:
                    dve.wait_ge(lv_pe, i - 1)
                for side, src in ((0, K3), (1, Q3)):
                    dve.tensor_tensor(halves_of(QK[i % 2], L, side), halves_of(src, L, side), halves_of(E3, L, side),
                                      ALU.mult).then_inc(lv_qk, 1)
            dve.wait_ge(lv_pe, len(LEVELS))
            for j in range(4, 8):
                dve.tensor_copy(A8[:, j, :], psum[:, j, 0:T + P]).then_inc(copied, 1)
            need(dve, "gat_pe", "out")
            o(dve.tensor_copy(O4, two_banks(0, T)), "out")
            for lag in range(LAG + 1):
                if lag < LAG:
                    w = LAG - lag
                    lp = QK[lag % 2].rearrange("p g t -> p (g t)")[:, 0:48 * w].rearrange("p (b l) -> p b l", l=w)
                    q = Q3.rearrange("p g (b l) -> p (g b) l", l=LAG)[:, :, lag:LAG]
                    k = K3.rearrange("p g (b l) -> p (g b) l", l=LAG)[:, :, 0:w]
                    if lag >= 2:
                        dve.wait_ge(lag_bc, lag - 1)
                    if lag == 0:
                        dve.tensor_tensor(lp, q, k, ALU.mult).then_inc(lag_p, 2)
                    else:
                        dve.tensor_tensor(lp, q, k, ALU.mult).then_inc(lag_p, 1)
                        dve.wait_ge(lag_p, 2 * lag + 1)
                        dve.wait_ge(lag_exp, lag)
                        le = LE[lag % 2].rearrange("p g t -> p (g t)")[:, 0:48 * w].rearrange("p (b l) -> p b l", l=w)
                        dve.tensor_tensor(lp, lp, le, ALU.mult).then_inc(lag_p, 1)
                if lag:
                    d = lag - 1
                    w = LAG - d
                    dve.wait_ge(lag_bc, d + 1)
                    if d >= 2:
                        dve.wait_ge(lag_acc, d - 1)
                    got = two_banks(2 * (d % 2), T)[:, :, 0:LAG * w].rearrange("p o (b l) -> p o b l", l=w)
                    tmp = LTMP[d % 2][:, :, 0:LAG * w].rearrange("p o (b l) -> p o b l", l=w)
                    v = V4.rearrange("p o (b l) -> p o b l", l=LAG)[:, :, :, 0:w]
                    dve.tensor_tensor(tmp, got, v, ALU.mult).then_inc(lag_tmp, 1)

        def gated_pool(pool):
            pool.wait_ge(lv_qk, 2 * len(LEVELS))
            for d in range(1, LAG + 2):
                if d < LAG:
                    w = LAG - d
                    le = LE[d % 2].rearrange("p g t -> p (g t)")[:, 0:48 * w].rearrange("p (b l) -> p b l", l=w)
                    c = C3.rearrange("p g (b l) -> p (g b) l", l=LAG)
                    if d >= 3:
                        pool.wait_ge(lag_p, 2 * (d - 2) + 2)
                    pool.tensor_tensor(le, c[:, :, d:LAG], c[:, :, 0:w], ALU.subtract).then_inc(lag_diff, 1)
                if d >= 2:
                    e = d - 2
                    w = LAG - e
                    tmp = LTMP[e % 2][:, :, 0:LAG * w].rearrange("p o (b l) -> p o b l", l=w)
                    acc = O4.rearrange("p o (b l) -> p o b l", l=LAG)[:, :, :, e:LAG]
                    pool.wait_ge(lag_tmp, e + 1)
                    if e:
                        pool.wait_ge(lag_acc, e)
                    pool.tensor_tensor(acc, acc, tmp, ALU.add).then_inc(lag_acc, 1)

        def gated_act(act):
            o = order(act, "gat_act")
            need(act, "gdn_dve", "out")
            need(act, "gat_pe", "gk")
            o(act.activation(U3[:, 0, :], psum[:, 0, 0:T], ACT.Identity, bias=col("gk_bias")), "u")
            need(act, "gat_dve", "u")
            o(act.activation(E3, U3, ACT.Abs))
            o(act.activation(E3, E3, ACT.Exp, scale=-1.0))
            o(act.activation(E3, E3, ACT.Ln, bias=1.0), "ln")
            o(act.activation(K3[:, 1:3, :], K3[:, 1:3, :], ACT.Sigmoid, scale=-1.0), "key")
            for i, L in enumerate(LEVELS):
                act.wait_ge(lv_cum, 8 + 2 * i + 2)
                act.activation(halves_of(E3, L, 0), halves_of(E3, L, 0), ACT.Exp).then_inc(lv_exp, 1)
                if i:
                    act.wait_ge(lv_qk, 2 * i)
                act.activation(halves_of(E3, L, 1), halves_of(C3, L, 1), ACT.Exp).then_inc(lv_exp, 1)
            act.wait_ge(lv_pe, len(LEVELS))
            for j in range(4):
                act.activation(A8[:, j, :], psum[:, j, 0:T + P], ACT.Copy).then_inc(copied, 1)
            for d in range(1, LAG):
                w = LAG - d
                le = LE[d % 2].rearrange("p g t -> p (g t)")[:, 0:48 * w]
                act.wait_ge(lag_diff, d)
                act.activation(le, le, ACT.Exp).then_inc(lag_exp, 1)

        def gated_pe(pe):
            o = order(pe, "gat_pe")
            need(pe, "gdn_dve", "out")
            o(pe.matmul(psum[:, 0, 0:T], gk_up[64:80, :], zs[64:80, :], start=True, stop=True), "gk")
            for b, tile in ((1, CV), (2, DI)):
                for n in range(2):
                    for i in range(2):
                        mm = pe.transpose(psum[:, b, n * T + i * P:n * T + (i + 1) * P], z[:, tile + i, n * P:(n + 1) * P], ident[:, :])
            o(mm, "tok")
            need(pe, "gat_dve", "tok")
            need(pe, "gat_act", "u")
            for j in range(8):
                mm = pe.matmul(psum[:, j, 0:T + P], zeros[:, 0:P], zeros[:, 0:T + P], start=True, stop=False, skip_group_check=True)
            o(mm, "zero")
            heads8 = [(j, 0, slice(32 * j, 32 * j + 32)) if j < 4 else (j, 1 + (j - 4) // 2, slice(HD * (j % 2), HD * (j % 2) + HD))
                      for j in range(8)]
            for i, L in enumerate(LEVELS):
                pe.wait_ge(lv_qk, 2 * i + 2)
                for j, tile, r in heads8:
                    for s0 in range(0, T, 2 * L):
                        st, at = s0 // P, s0 % P
                        c = s0 + L + (P if st else 0)
                        mm = pe.matmul(psum[at:at + L, j, c:c + L], QK[i % 2][r, tile, s0:s0 + L], QK[i % 2][r, tile, s0 + L:s0 + 2 * L],
                                       start=False, stop=(i == len(LEVELS) - 1), skip_group_check=True)
                mm.then_inc(lv_pe, 1)
            pe.wait_ge(copied, 8)
            for j in range(8):
                tok, f = toks[j // 4], slice((j % 4) * HD, (j % 4) * HD + HD)
                r, out = slice(HD * (j % 2), HD * (j % 2) + HD), two_banks(0, T)[:, j // 2, :]
                pe.matmul(out[r, :], tok[:, 0, f], A8[:, j, 0:T], start=True, stop=False, skip_group_check=True)
                mm = pe.matmul(out[r, P:T], tok[:, 1, f], A8[:, j, T:T + P], start=False, stop=True, skip_group_check=True)
            o(mm, "out")
            need(pe, "gat_dve", "out")
            for d in range(LAG):
                w = LAG - d
                pe.wait_ge(lag_p, 2 * d + 2)
                if d >= 2:
                    pe.wait_ge(lag_tmp, d - 1)
                lp = QK[d % 2].rearrange("p g t -> p (g t)")
                for out in range(4):
                    tile, sel = (0, lagsel[:, out, :]) if out < 2 else (out - 1, headones[:, :])
                    mm = pe.matmul(two_banks(2 * (d % 2), T)[:, out, 0:LAG * w], sel, lp[:, tile * LAG * w:(tile + 1) * LAG * w],
                                   start=True, stop=True, skip_group_check=True)
                mm.then_inc(lag_bc, 1)

        post_hi, post_lo = sem("mixed_hi"), sem("mixed_lo")
        OSQ, OSUM, OTMP = (area(i * 2048, 8, T) for i in range(3))

        def post_act(act):
            o = order(act, "post_act")
            act.wait_ge(lag_acc, LAG)
            o(act.activation(OSQ, z[:, 0:8, :], ACT.Square), "squares")
            need(act, "post_dve", "mean")
            o(act.activation(OSQ, OSUM, ACT.Abs_reciprocal_sqrt), "rsqrt")
            need(act, "post_dve", "scaled")
            act.activation(xn_hi[:, :, X], z[:, 0:8, :], ACT.Copy).then_inc(post_hi, 1)

        def post_pe(pe):
            o = order(pe, "post_pe")
            need(pe, "post_act", "squares")
            for i in range(4):
                mm = pe.matmul(bank(4 + i), headones[:, :], OSQ[:, 2 * i:2 * i + 2, :], start=True, stop=True)
            o(mm, "sums")

        def post_dve(dve):
            o = order(dve, "post_dve")
            need(dve, "post_pe", "sums")
            o(dve.tensor_scalar(OSUM, psum[:, 4:8, :].rearrange("p b (n t) -> p (b n) t", t=T), 1.0 / HD, EPS, ALU.mult, ALU.add), "mean")
            need(dve, "post_act", "rsqrt")
            newton(dve, o, OSQ, OSUM, OTMP, "unit")
            for k in range(8):
                o(dve.scalar_tensor_tensor(z[:, k, :], z[:, k, :], col("head_gain", k), z[:, RG + k, :], ALU.mult, ALU.mult))
            o(dve.tensor_tensor(z[:, 0:8, :], z[:, 0:8, :], OSQ, ALU.mult), "scaled")
            dve.wait_ge(post_hi, 1)
            dve.tensor_tensor(xn_lo[:, :, X], z[:, 0:8, :], xn_hi[:, :, X].bitcast(F32), ALU.subtract).then_inc(post_lo, 1)

        at_scores, at_max, at_exp, at_norm, at_turn, at_pt, at_out, at_hi, at_lo, at_self = (sem(x) for x in (
            "att_scores", "att_max", "att_probs", "att_scaled", "att_turned", "att_turned_out", "att_out", "att_hi",
            "att_lo", "att_small"))
        at_col = small[:, cols["att"]:cols["att"] + 8]
        PROB = [work[:, i * 512:(i + 1) * 512] for i in range(2)]
        PT = [area(1024 + i * 1024, 4, T) for i in range(2)]

        class Attention:
            units, heads_before = 0, 0

            def __init__(self, heads, parts, keys, q, k, v):
                self.heads, self.parts, self.keys, self.q, self.k, self.v = heads, parts, keys, q, k, v
                self.scale = (parts * P) ** -0.5
                self.u0, self.h0 = Attention.units, Attention.heads_before
                Attention.units += 2 * heads
                Attention.heads_before += heads

            def pe(self, pe):
                key_tiles = self.keys // P

                def scores(u):
                    h, tt = u // 2, u % 2
                    if u >= 2:
                        pe.wait_ge(at_exp, self.u0 + u - 1)
                    for i in range(self.parts):
                        mm = pe.matmul(psum[:, u % 2, 0:self.keys], self.q(h, i)[:, tt * P:(tt + 1) * P], self.k(h, i),
                                       start=(i == 0), stop=(i == self.parts - 1))
                    mm.then_inc(at_scores, 1)

                scores(0)
                for u in range(2 * self.heads):
                    h, tt = u // 2, u % 2
                    if u + 1 < 2 * self.heads:
                        scores(u + 1)
                    pe.wait_ge(at_norm, self.u0 + u + 1)
                    if u >= 2:
                        pe.wait_ge(at_pt, self.u0 + u - 1)
                    for j in range(key_tiles):
                        mm = pe.transpose(psum[:, 2 + u % 2, j * P:(j + 1) * P], PROB[u % 2][:, j * P:(j + 1) * P], ident[:, :])
                    mm.then_inc(at_turn, 1)
                    if tt:
                        pe.wait_ge(at_pt, self.u0 + u + 1)
                        if h >= 2:
                            pe.wait_ge(at_lo, self.h0 + h - 1)
                        for i in range(self.parts):
                            for j in range(key_tiles):
                                mm = pe.matmul(psum[:, 4 + h % 2, i * T:(i + 1) * T], self.v(h, j)[:, i * P:(i + 1) * P],
                                               PT[h % 2][:, j, :], start=(j == 0), stop=(j == key_tiles - 1))
                        mm.then_inc(at_out, 1)

            def act(self, act):
                def turned(u):
                    h, tt = u // 2, u % 2
                    act.wait_ge(at_turn, self.u0 + u + 1)
                    if h >= 2 and tt == 0:
                        act.wait_ge(at_out, self.h0 + h - 1)
                    act.activation(PT[h % 2][:, 0:self.keys // P, tt * P:(tt + 1) * P],
                                   psum[:, 2 + u % 2, 0:self.keys].rearrange("p (j t) -> p j t", t=P), ACT.Copy).then_inc(at_pt, 1)

                def out_hi(h):
                    act.wait_ge(at_out, self.h0 + h + 1)
                    act.activation(xn_hi[:, self.parts * h:self.parts * (h + 1), X],
                                   psum[:, 4 + h % 2, 0:self.parts * T].rearrange("p (i t) -> p i t", t=T), ACT.Copy).then_inc(at_hi, 1)

                for u in range(2 * self.heads):
                    act.wait_ge(at_max, self.u0 + u + 1)
                    if u >= 2:
                        act.wait_ge(at_turn, self.u0 + u - 1)
                    act.activation(PROB[u % 2][:, 0:self.keys], psum[:, u % 2, 0:self.keys], ACT.Exp, scale=self.scale,
                                   bias=at_col[:, u % 2:u % 2 + 1], accum_out=at_col[:, 2 + u % 2:3 + u % 2]).then_inc(at_exp, 1)
                    if u:
                        turned(u - 1)
                    if u >= 3 and u % 2:
                        out_hi((u - 3) // 2)
                turned(2 * self.heads - 1)
                out_hi(self.heads - 1)

            def dve(self, dve):
                def out_lo(h):
                    dve.wait_ge(at_hi, self.h0 + h + 1)
                    o = xn_hi[:, self.parts * h:self.parts * (h + 1), X].bitcast(F32)
                    dve.tensor_tensor(xn_lo[:, self.parts * h:self.parts * (h + 1), X],
                                      psum[:, 4 + h % 2, 0:self.parts * T].rearrange("p (i t) -> p i t", t=T), o,
                                      ALU.subtract).then_inc(at_lo, 1)

                for u in range(2 * self.heads):
                    n = 2 * (self.u0 + u)
                    dve.wait_ge(at_scores, self.u0 + u + 1)
                    top, bias = at_col[:, 4:5], at_col[:, u % 2:u % 2 + 1]
                    dve.tensor_reduce(top, psum[:, u % 2, 0:self.keys], AX_X, ALU.max).then_inc(at_self, 1)
                    dve.wait_ge(at_self, n + 1)
                    dve.tensor_scalar(bias, top, -self.scale, None, ALU.mult).then_inc(at_max, 1)
                    dve.wait_ge(at_exp, self.u0 + u + 1)
                    dve.reciprocal(at_col[:, 5:6], at_col[:, 2 + u % 2:3 + u % 2]).then_inc(at_self, 1)
                    dve.wait_ge(at_self, n + 2)
                    dve.tensor_scalar(PROB[u % 2][:, 0:self.keys], PROB[u % 2][:, 0:self.keys], at_col[:, 5:6], None, ALU.mult).then_inc(at_norm, 1)
                    if u >= 3 and u % 2:
                        out_lo((u - 3) // 2)
                out_lo(self.heads - 1)

        def run_act(act, job, evac):
            for s in steps(act, job, 2):
                split_hi(act, s)
                if evac is not None:
                    evac(s)

        def run_dve(dve, job, evac):
            for s in steps(dve, job, 2):
                split_lo(dve, s)
                if evac is not None:
                    evac(s)

        def pairs_of(s, dst, w=2):
            at = s.c * w
            return dst[:, bass.ds(at, w), :] if s.looped else dst[:, at:at + w, :]

        def act_copy_to(act, dst, func=ACT.Copy, w=T):
            def evac(s):
                act.wait_ge(chunk_done, s.g + 1)
                act.activation(pairs_of(s, dst), psum[:, s.bank:s.bank + 2, 0:w], func).then_inc(evacuated, 1)
            return evac

        def act_tokens_to(act, dst, func=ACT.Copy):
            tiles = dst.shape[1]

            def evac(s):
                act.wait_ge(chunk_done, s.g + 1)
                at = s.c * 256
                out = dst[:, :, bass.ds(at, 256)] if s.looped else dst[:, :, at:at + 256]
                got = psum[:, s.bank:s.bank + 2, :].rearrange("p b (n f) -> p (b n) f", f=256)[:, 0:tiles, :]
                act.activation(out, got, func).then_inc(evacuated, 1)
            return evac

        def dve_add_gated(dve, tiles, gate, halves):
            def evac(s):
                dve.wait_ge(chunk_done, s.g + 1)
                for n in range(tiles):
                    k = s.c * tiles + n
                    tile = bass.ds(k, 1) if s.looped else slice(k, k + 1)
                    for h in range(halves):
                        t = slice(h * T, (h + 1) * T)
                        x, got = xc[:, tile, t], psum[:, s.bank + n:s.bank + n + 1, t]
                        if gate is None:
                            mm = dve.tensor_tensor(x, x, got, ALU.add)
                        else:
                            mm = dve.scalar_tensor_tensor(x, got, gate[:, tile, h], x, ALU.mult, ALU.add)
                mm.then_inc(evacuated, 1)
            return evac

        ff_gate, ff_hi, ff_lo, ff_conv, ff_tap = (sem(x) for x in (
            "ff_gate", "ff_hi", "ff_lo", "ff_convolved", "ff_newest_tap"))
        later = ExitStack()
        mix.close()
        h_hi = sb("h_hi", [P, HALF, 2 * T], F32R, scope=later)
        h_lo = sb("h_lo", [P, HALF, 2 * T], F32R, scope=later)
        fbuf = [work[:, 4096 + i * 1024:4096 + (i + 1) * 1024].rearrange("p (n t) -> p n t", n=2) for i in range(SLOTS)]

        class Feed:
            chunks = 0

            def __init__(self, name, norm, w, gate, conv=None):
                self.name, self.norm, self.w, self.gate, self.conv = name, norm, w, gate, conv
                self.bases = [Feed.chunks, Feed.chunks + HALF]
                Feed.chunks += FF_TILES

            def pe(self, pe):
                for half in range(2):
                    base = self.bases[half]
                    up, down = jobs[f"{self.name}_up{half}"], jobs[f"{self.name}_down{half}"]

                    def norm_k(s, k):
                        if s.looped and s.u == 0 or s.static == 0:
                            self.norm.ready(pe, k)

                    pe_feature_major(pe, up, xn_hi, xn_lo, slice(0, self.w), before_k=norm_k if half == 0 else None)

                    def hidden_k(s, k):
                        if (s.looped and s.u == 0 or s.static == 0) and k in (0, HALF - 1):
                            pe.wait_ge(ff_lo, base + (HALF - 1 if k == 0 else HALF))

                    pe_feature_major(pe, down, h_hi, h_lo, slice(0, self.w), n_tiles=1, k_tiles=HALF, before_k=hidden_k)

            def act(self, act):
                for half in range(2):
                    base, job = self.bases[half], jobs[f"{self.name}_up{half}"]

                    def evac(s):
                        b = fbuf[s.slot]
                        n = s.c + base
                        act.wait_ge(chunk_done, s.g + 1)
                        if s.looped or n >= 3:
                            act.wait_ge(ff_lo, n - 2)
                        if self.conv is None:
                            act.activation(b[:, 0, 0:self.w], psum[:, s.bank, 0:self.w], ACT.Silu).then_inc(ff_gate, 1)
                        else:
                            k = s.c + half * HALF
                            for i in range(2):
                                tap = small[:, bass.ds(k + (cols["ff_conv2"] + i * FF_TILES), 1)] if s.looped else col("ff_conv2", k + i * FF_TILES)
                                mm = act.activation(b[:, i, 0:T], psum[:, s.bank + i, 0:T], ACT.Copy, scale=tap)
                            mm.then_inc(ff_tap, 1)
                            act.wait_ge(ff_conv, n * 2 + 2)
                            act.activation(b[:, 0, 0:T], b[:, 0, 0:T], ACT.Silu).then_inc(ff_gate, 1)
                        act.wait_ge(evacuated, s.g + 1)
                        out = h_hi[:, bass.ds(s.c, 1), 0:self.w] if s.looped else h_hi[:, s.c:s.c + 1, 0:self.w]
                        act.activation(out, b[:, 1:2, 0:self.w], ACT.Copy).then_inc(ff_hi, 1)

                    run_act(act, job, evac)
                    run_act(act, jobs[f"{self.name}_down{half}"], None)

            def dve(self, dve):
                for half in range(2):
                    base, job = self.bases[half], jobs[f"{self.name}_up{half}"]

                    def evac(s):
                        b = fbuf[s.slot]
                        n = s.c + base
                        if self.conv is not None:
                            dve.wait_ge(ff_tap, n + 1)
                            k = s.c + half * HALF
                            for back in (1, 2):
                                for i in range(2):
                                    name = f"ff_conv{2 - back}"
                                    tap = small[:, bass.ds(k + (cols[name] + i * FF_TILES), 1)] if s.looped else col(name, k + i * FF_TILES)
                                    mm = dve.scalar_tensor_tensor(b[:, i, back:T], psum[:, s.bank + i, 0:T - back], tap, b[:, i, back:T],
                                                                  ALU.mult, ALU.add)
                                mm.then_inc(ff_conv, 1)
                                dve.wait_ge(ff_conv, n * 2 + back)
                            up = b[:, 1, 0:T]
                        else:
                            up = psum[:, s.bank + 1, 0:self.w]
                        dve.wait_ge(ff_gate, n + 1)
                        dve.tensor_tensor(b[:, 1, 0:self.w], b[:, 0, 0:self.w], up, ALU.mult).then_inc(evacuated, 1)

                    run_dve(dve, job, evac)
                    run_dve(dve, jobs[f"{self.name}_down{half}"], dve_add_gated(dve, 1, self.gate, self.w // T))

            def pool(self, pool):
                for half in range(2):
                    base, job = self.bases[half], jobs[f"{self.name}_up{half}"]
                    for s in steps(pool, job, 2):
                        n = s.c + base
                        b = fbuf[s.slot]
                        pool.wait_ge(ff_hi, n + 1)
                        lo = h_lo[:, bass.ds(s.c, 1), 0:self.w] if s.looped else h_lo[:, s.c:s.c + 1, 0:self.w]
                        hi = h_hi[:, bass.ds(s.c, 1), 0:self.w] if s.looped else h_hi[:, s.c:s.c + 1, 0:self.w]
                        pool.tensor_tensor(lo, b[:, 1:2, 0:self.w], hi.bitcast(F32), ALU.subtract).then_inc(ff_lo, 1)
        mrow = work[:, 0:SLOTS * 256].rearrange("p (s f) -> p s f", s=SLOTS)
        mod_act, mod_dve, mod_rows, mod_turned = sem("mod_inputs"), sem("mod_prepared"), sem("mod_rows"), sem("mod_turned")

        def mod_pe(pe):
            pe.wait_ge(mod_dve, 2)
            for s in steps(pe, jobs["mod"]):
                bank_free(pe, s)
                pe.wait_ge(lo_ready, s.g + 1)
                for k in range(KT):
                    w = slice(k * 256, (k + 1) * 256)
                    pe.matmul(psum[0:4, s.bank, 0:256], c4[:, k, :], w_hi[:, s.slot, w], start=(k == 0), stop=False)
                    mm = pe.matmul(psum[0:4, s.bank, 0:256], c4[:, k, :], w_lo[:, s.slot, w], start=False, stop=(k == KT - 1))
                mm.then_inc(chunk_done, 1)
                pe.wait_ge(mod_rows, s.c + 1)
                for n in range(2):
                    mm = pe.matmul(psum[:, s.bank + 1, n * 2:n * 2 + 2], mrow[:, s.slot, n * P:(n + 1) * P], row_sums[:, :], start=True, stop=True)
                mm.then_inc(mod_turned, 1)

        def mod_scalar(act):
            act.wait_ge(start_in, 16 * len(START))
            act.activation(c_in[:, :, :], c_in[:, :, :], ACT.Silu).then_inc(mod_act, 1)
            act.wait_ge(mod_act, 1)
            act.activation(c4[:, :, :].rearrange("p k (w l) -> p k w l", l=2)[:, :, :, 0], c_in[:, :, :], ACT.Copy).then_inc(mod_act, 1)

            def rows(s):
                act.wait_ge(chunk_done, s.g + 1)
                act.activation(mrow[0:4, s.slot, :], psum[0:4, s.bank, 0:256], ACT.Copy).then_inc(mod_rows, 1)
            run_act(act, jobs["mod"], rows)

        def mod_vector(dve):
            dve.memset(mrow, 0.0).then_inc(mod_dve, 1)
            dve.wait_ge(mod_act, 2)
            hl = c4[:, :, :].rearrange("p k (w l) -> p k w l", l=2)
            dve.tensor_tensor(hl[:, :, :, 1], c_in[:, :, :], hl[:, :, :, 0].bitcast(F32), ALU.subtract).then_inc(mod_dve, 1)

            def columns(s):
                dve.wait_ge(mod_turned, s.c + 1)
                got = psum[:, s.bank + 1, 0:4].rearrange("p (n w) -> p n w", n=2)
                at = s.c * 2
                out = mods[:, bass.ds(at, 2), :] if s.looped else mods[:, at:at + 2, :]
                dve.tensor_copy(out, got).then_inc(evacuated, 1)
            run_dve(dve, jobs["mod"], columns)
            dve.wait_ge(evacuated, jobs["mod"].base + jobs["mod"].n)
            dve.tensor_tensor(mods[:, :, :], mods[:, :, :], b_mod[:, :].unsqueeze(2).to_broadcast([P, 144, 2]), ALU.add).then_inc(mod_dve, 1)
            dve.wait_ge(mod_dve, 3)
            for ln in range(6):
                at = (ln // 3) * 72 + (ln % 3) * 24
                dve.scalar_tensor_tensor(scales[:, ln, :, :], mods[:, at + 8:at + 16, :], 1.0,
                                         gains[:, ln, :].unsqueeze(2).to_broadcast([P, KT, 2]), ALU.add, ALU.mult)
                if ln % 3 != 1:
                    dve.tensor_scalar(mods[:, at + 16:at + 24, :], mods[:, at + 16:at + 24, :], 0.5, None, ALU.mult)
            dve.memset(c_in[:, :, :], 0.0).then_inc(mod_dve, 1)

        def modulated(ln, span):
            at = (ln // 3) * 72 + (ln % 3) * 24
            return Norm(span, lambda k, h: scales[:, ln, k, h:h + 1], lambda k, h: mods[:, at + k, h:h + 1])

        def gate_of(ln):
            at = (ln // 3) * 72 + (ln % 3) * 24 + 16
            return mods[:, at:at + KT, :]

        later.close()
        l0 = ExitStack()
        a_t, u_t, v_t = (sb(n, [P, 4, 2 * T], scope=l0) for n in ("a_t", "u_t", "v_t"))
        dft_c = sb("dft_c", [P, 2 * P], scope=l0)
        dft_cos = sb("dft_cos", [P, 2, T], scope=l0)
        dft_sin = sb("dft_sin", [P, 2, T], scope=l0)
        ws_t = sb("ws_t", [P, 4, P], scope=l0)
        bs_row = sb("bs_row", [P, 4, P], scope=l0)
        gv_row = sb("gv_row", [P, 4, P], scope=l0)
        L0_TABLES = dict(dft_c=dft_c, dft_cos=dft_cos, dft_sin=dft_sin, ws_t=ws_t, bs_row=bs_row, gv_row=gv_row)
        o_t = area(0, KT, 2 * T)
        mid = [area(4096 + i * 512, 2, T) for i in range(2)]
        vsq = work[:, 5120:7168].rearrange("p (n f) -> p n f", f=P)
        vst = work[:, 7168:7184]
        vst2, vst3 = work[:, 7184:7200], work[:, 7200:7216]
        l0_tables_in, f_mid, f_mid_out, f_sum, f_sum_out, g_dve, g_act, g_pe, o_hi, o_lo = (sem(x) for x in (
            "l0_tables_in", "fourier_channels", "fourier_channels_out", "fourier_tokens", "fourier_tokens_out", "gating_dve",
            "gating_rsqrt", "gating_mixed", "branch_hi", "branch_lo"))

        def branch_pe(pe, norm):
            def norm_k(s, k):
                if s.c == 0:
                    norm.ready(pe, k)
            pe_feature_major(pe, jobs["ab_a"], xn_hi, xn_lo, XC, before_k=norm_k)
            pe_feature_major(pe, jobs["ab_u"], xn_hi, xn_lo, XC)
            pe_token_major(pe, jobs["ab_v"], XC)
            pe.wait_ge(evacuated, jobs["ab_v"].base + 2)
            pe.wait_ge(l0_tables_in, 16 * len(L0_TABLES))

            def channels(j):
                q, g = j // 4, j % 4
                if j >= 2:
                    pe.wait_ge(f_mid_out, j - 1)
                for nt in range(2):
                    mm = pe.matmul(psum[:, j % 2, nt * T:(nt + 1) * T], a_t[:, g, q * T + nt * P:q * T + (nt + 1) * P], dft_c[:, :],
                                   start=True, stop=True)
                mm.then_inc(f_mid, 1)

            channels(0)
            for j in range(8):
                if j + 1 < 8:
                    channels(j + 1)
                pe.wait_ge(f_mid_out, j + 1)
                if j >= 2:
                    pe.wait_ge(f_sum_out, j - 1)
                for nt in range(2):
                    pe.matmul(psum[:, 2 + j % 2, 0:T], mid[j % 2][:, nt, 0:P], dft_cos[:, nt, :], start=(nt == 0), stop=False)
                    mm = pe.matmul(psum[:, 2 + j % 2, 0:T], mid[j % 2][:, nt, P:T], dft_sin[:, nt, :], start=False, stop=(nt == 1))
                mm.then_inc(f_sum, 1)
            pe.wait_ge(g_dve, 8)
            for tt in range(4):
                for g in range(4):
                    mm = pe.matmul(psum[:, 4 + g, tt * P:(tt + 1) * P], v_t[:, tt, g * P:(g + 1) * P], ws_t[:, g, :], start=True, stop=True)
            mm.then_inc(g_pe, 1)
            pe.wait_ge(o_lo, 2)
            pe_feature_major(pe, jobs["ab_out"], xn_hi, xn_lo, XC)

        def branch_act(act, norm):
            for name in L0_TABLES:
                act.dma_start(L0_TABLES[name][:], io[name]).then_inc(l0_tables_in, 16)
            norm.act_squares(act)
            norm.act_rest(act)
            run_act(act, jobs["ab_a"], act_copy_to(act, a_t, w=2 * T))
            run_act(act, jobs["ab_u"], act_copy_to(act, u_t, ACT.Gelu_apprx_tanh, w=2 * T))
            run_act(act, jobs["ab_v"], act_tokens_to(act, v_t, ACT.Gelu_apprx_tanh))
            act.wait_ge(g_dve, 3)
            act.activation(vst2, vst, ACT.Abs_reciprocal_sqrt).then_inc(g_act, 1)
            for j in range(8):
                act.wait_ge(f_mid, j + 1)
                if j >= 2:
                    act.wait_ge(f_sum, j - 1)
                act.activation(mid[j % 2], psum[:, j % 2, :].rearrange("p (n t) -> p n t", n=2), ACT.Copy).then_inc(f_mid_out, 1)
            act.wait_ge(f_sum_out, 8)
            act.activation(xn_hi[:, 0:4, :], o_t[:, 0:4, :], ACT.Copy).then_inc(o_hi, 1)
            act.wait_ge(g_dve, 10)
            act.activation(xn_hi[:, 4:8, :], o_t[:, 4:8, :], ACT.Copy).then_inc(o_hi, 1)
            run_act(act, jobs["ab_out"], None)

        def branch_dve(dve, norm):
            norm.dve(dve)
            for name in ("ab_a", "ab_u", "ab_v"):
                run_dve(dve, jobs[name], None)
            n = 0

            def o(ins):
                nonlocal n
                n += 1
                ins.then_inc(g_dve, 1)
                dve.wait_ge(g_dve, n)
            v = v_t[:, :, :].rearrange("p n (g f) -> p (n g) f", f=P)
            dve.wait_ge(evacuated, jobs["ab_v"].base + 2)
            dve.wait_ge(l0_tables_in, 16 * len(L0_TABLES))
            o(dve.tensor_tensor(vsq, v, v, ALU.mult))
            o(dve.tensor_reduce(vst3, vsq, AX_X, ALU.add))
            o(dve.tensor_scalar(vst, vst3, 1.0 / P, EPS, ALU.mult, ALU.add))
            dve.wait_ge(g_act, 1)
            o(dve.scalar_tensor_tensor(vst3, vst2, -0.5, vst2, ALU.mult, ALU.mult))
            o(dve.tensor_tensor(vst3, vst3, vst, ALU.mult))
            o(dve.scalar_tensor_tensor(vst2, vst3, 1.5, vst2, ALU.add, ALU.mult))
            o(dve.tensor_tensor(v, v, vst2.unsqueeze(2).to_broadcast([P, 16, P]), ALU.mult))
            gv = gv_row[:, :, :].unsqueeze(1).to_broadcast([P, 4, 4, P])
            v4 = v_t[:, :, :].rearrange("p n (g f) -> p n g f", f=P)
            o(dve.tensor_tensor(v4, v4, gv, ALU.mult))
            for j in range(8):
                dve.wait_ge(f_sum, j + 1)
                dve.tensor_copy(o_t[:, j % 4, (j // 4) * T:(j // 4 + 1) * T], psum[:, 2 + j % 2, 0:T]).then_inc(f_sum_out, 1)
            dve.wait_ge(g_pe, 1)
            gated = o_t[:, 4:8, :].rearrange("p g (n t) -> p g n t", t=P)
            bs = bs_row[:, :, :].unsqueeze(2).to_broadcast([P, 4, 4, P])
            o(dve.tensor_tensor(gated, psum[:, 4:8, :].rearrange("p g (n t) -> p g n t", t=P), bs, ALU.add))
            o(dve.tensor_tensor(o_t[:, 4:8, :], o_t[:, 4:8, :], u_t[:, :, :], ALU.mult))
            for i in range(2):
                dve.wait_ge(o_hi, i + 1)
                k = slice(4 * i, 4 * i + 4)
                dve.tensor_tensor(xn_lo[:, k, :], o_t[:, k, :], xn_hi[:, k, :].bitcast(F32), ALU.subtract).then_inc(o_lo, 1)
            run_dve(dve, jobs["ab_out"], dve_add_gated(dve, 2, gate_of(1), 2))

        l0.close()
        l1 = ctx.enter_context(ExitStack())
        qk12 = sb("qk12", [P, 12, T], scope=l1)
        qk_tmp = sb("qk_tmp", [P, 12, T], scope=l1)
        v2 = sb("v2", [P, 4, T], scope=l1)
        ax_cos, ax_sin = sb("ax_cos", [P, T], scope=l1), sb("ax_sin", [P, T], scope=l1)
        ax_in, r_act, r_dve, r_pe = sem("axial_in"), sem("rope_act"), sem("rope_dve"), sem("rope_pe")
        qk_mean, qk_rstd = work[:, 0:12 * T].rearrange("p (n t) -> p n t", t=T), work[:, 12 * T:24 * T].rearrange("p (n t) -> p n t", t=T)
        kx = qk12[:, 8:12, :].rearrange("p (h w) t -> p h w t", w=2)[:, :, 0, :]
        k_all = qk12[:, 8:12, :].rearrange("p (h w) t -> p h (w t)", w=2)

        first = Norm(XC, lambda k, h: col("mix_norm_w", k) if h == 0 else col("mem_norm_w", k))
        cross = Norm(X, lambda k, h: col("xattn_norm_w", k))
        ffn = Norm(X, lambda k, h: col("ffn_norm_w", k))
        between = Norm(X, lambda k, h: col("final_norm_w", k), out=xc[:, :, X])
        n20, n21 = modulated(0, XC), modulated(1, XC)
        n22, n23, n24 = modulated(2, XC), modulated(3, XC), modulated(4, XC)
        n25 = modulated(5, X)
        last = Norm(X, lambda k, h: col("g_final", k), out=nrm)
        feed0 = Feed("ffn", ffn, T, None, conv=True)
        feed1 = Feed("a1", n20, 2 * T, gate_of(0))
        feed2 = Feed("a2", n22, 2 * T, gate_of(2))
        feed3 = Feed("b1", n23, 2 * T, gate_of(3))
        feed4 = Feed("b2", n25, T, gate_of(5))
        k1, v1, q1 = z[:, 0:8, :], z[:, 8:16, :].rearrange("p (n a) t -> p n (a t)", n=2), z[:, 16:24, :]
        att1 = Attention(4, 2, T, lambda h, i: q1[:, 2 * h + i, :], lambda h, i: k1[:, 2 * h + i, :], lambda h, j: v1[:, j, h * T:(h + 1) * T])
        att2 = Attention(8, 1, 2 * T, lambda h, i: qk12[:, h, :], lambda h, i: k_all[:, h // 4, :], lambda h, j: v2[:, j, (h // 4) * P:(h // 4 + 1) * P])
        START = dict(small=small, ident=ident, ones=ones, rot=rot, row_sums=row_sums, gains=gains, b_mod=b_mod, c_in=c_in)
        residual_in, ctx_in, out_in, set_up = sem("residual_in"), sem("ctx_in"), sem("out_stored"), sem("constants_set")

        block = ctx.enter_context(nc.Block())

        @block.sync
        def _(sp):
            sp.dma_start(xc[:, :, X], io["x"]).then_inc(residual_in, 16)
            sp.dma_start(xc[:, :, C], io["mem"]).then_inc(residual_in, 16)
            for name in START:
                sp.dma_start(START[name][:], io[name]).then_inc(start_in, 16)
            for n, (name, _, _, _) in enumerate(plan):
                for s in steps(sp, jobs[name]):
                    load(sp, s)
                if n == 0:
                    load_mixer_tables(sp)
            sp.wait_ge(n_scaled, last.scaled_base + KT)
            sp.dma_start(io["out"], nrm[:, :, X]).then_inc(out_in, 16)
            sp.wait_ge(out_in, 16)

        @block.tensor
        def _(pe):
            pe.wait_ge(start_in, 16 * len(START))
            pe.wait_ge(set_up, 2)
            first.pe(pe)
            first.ready(pe, KT - 1)
            for name in ("w_in_a", "w_in_g"):
                pe_feature_major(pe, jobs[name], xn_hi, xn_lo, X)
            pe_feature_major(pe, jobs["w_in_small"], xn_hi, xn_lo, X, n_tiles=1)
            retention_pe(pe)
            delta_pe(pe)
            gated_pe(pe)
            post_pe(pe)
            pe.wait_ge(post_lo, 1)
            pe_feature_major(pe, jobs["w_out"], xn_hi, xn_lo, X)
            pe_feature_major(pe, jobs["wk"], xn_hi, xn_lo, C)
            pe_token_major(pe, jobs["wv"], C)
            cross.pe(pe)
            cross.ready(pe, KT - 1)
            pe_feature_major(pe, jobs["wq"], xn_hi, xn_lo, X)
            pe.wait_ge(evacuated, jobs["wq"].base + 4)
            att1.pe(pe)
            pe.wait_ge(at_lo, att1.heads)
            pe_feature_major(pe, jobs["wo"], xn_hi, xn_lo, X)
            ffn.pe(pe)
            feed0.pe(pe)
            between.pe(pe)
            mod_pe(pe)
            n20.pe(pe)
            feed1.pe(pe)
            n21.pe(pe)
            branch_pe(pe, n21)
            n22.pe(pe)
            feed2.pe(pe)
            n23.pe(pe)
            feed3.pe(pe)
            n24.pe(pe)
            n24.ready(pe, KT - 1)
            pe_feature_major(pe, jobs["q2"], xn_hi, xn_lo, X)
            pe_feature_major(pe, jobs["k2"], xn_hi, xn_lo, XC)
            pe_token_major(pe, jobs["v2"], XC)
            pe.wait_ge(r_act, 1)
            for i in range(6):
                mm = pe.matmul(bank(i), ones[:, :], qk_tmp[:, 2 * i:2 * i + 2, :], start=True, stop=True)
            mm.then_inc(r_pe, 1)
            pe.wait_ge(r_dve, 6)
            for i in range(4):
                pe.matmul(bank(i), rot[:, :], qk12[:, 2 * i:2 * i + 2, :], start=True, stop=True)
            pe.matmul(bank(4), rot[:, :], kx, start=True, stop=True).then_inc(r_pe, 1)
            pe.wait_ge(r_dve, 11)
            att2.pe(pe)
            pe.wait_ge(at_lo, att1.heads + att2.heads)
            pe_feature_major(pe, jobs["wo2"], xn_hi, xn_lo, X)
            n25.pe(pe)
            feed4.pe(pe)
            last.pe(pe)

        @block.scalar
        def _(act):
            act.wait_ge(residual_in, 32)
            first_splits(act, split_hi)
            act.wait_ge(start_in, 16 * len(START))
            first.act_squares(act)
            first.act_rest(act)
            act.wait_ge(n_scaled, first.scaled_base + 2 * KT)
            act.dma_start(xc[:, :, C], io["ctx"]).then_inc(ctx_in, 16)
            run_act(act, jobs["w_in_a"], act_copy_to(act, z))
            run_act(act, jobs["w_in_g"], act_copy_to(act, z[:, RG:RG + 8, :], ACT.Silu))

            def small_rows(s):
                act.wait_ge(chunk_done, s.g + 1)
                act.activation(zs[:, :], psum[:, s.bank, 0:T], ACT.Copy).then_inc(evacuated, 1)
            run_act(act, jobs["w_in_small"], small_rows)
            retention_act(act)
            delta_act(act)
            gated_act(act)
            post_act(act)
            run_act(act, jobs["w_out"], None)
            act.wait_ge(post_lo, 1)
            run_act(act, jobs["wk"], act_copy_to(act, k1))
            run_act(act, jobs["wv"], act_tokens_to(act, v1))
            act.wait_ge(evacuated, jobs["w_out"].base + 4)
            cross.act_squares(act)
            cross.act_rest(act)
            run_act(act, jobs["wq"], act_copy_to(act, q1))
            att1.act(act)
            run_act(act, jobs["wo"], None)
            act.wait_ge(evacuated, jobs["wo"].base + 4)
            ffn.act_squares(act)
            ffn.act_rest(act)
            feed0.act(act)
            act.wait_ge(evacuated, jobs["ffn_down1"].base + 8)
            between.act_squares(act)
            between.act_rest(act)
            mod_scalar(act)
            act.wait_ge(ctx_in, 16)
            act.wait_ge(mod_dve, 4)
            act.wait_ge(n_scaled, between.scaled_base + KT)
            n20.act_squares(act)
            n20.act_rest(act)
            feed1.act(act)
            act.wait_ge(evacuated, jobs["a1_down1"].base + 8)
            branch_act(act, n21)
            act.wait_ge(evacuated, jobs["ab_out"].base + 4)
            n22.act_squares(act)
            n22.act_rest(act)
            feed2.act(act)
            act.wait_ge(evacuated, jobs["a2_down1"].base + 8)
            n23.act_squares(act)
            n23.act_rest(act)
            feed3.act(act)
            act.wait_ge(evacuated, jobs["b1_down1"].base + 8)
            act.dma_start(ax_cos[:, :], io["ax_cos"]).then_inc(ax_in, 16)
            act.dma_start(ax_sin[:, :], io["ax_sin"]).then_inc(ax_in, 16)
            n24.act_squares(act)
            n24.act_rest(act)
            run_act(act, jobs["q2"], act_copy_to(act, qk12[:, 0:8, :]))

            def keys(s):
                act.wait_ge(chunk_done, s.g + 1)
                act.activation(k_all, psum[:, s.bank:s.bank + 2, :], ACT.Copy).then_inc(evacuated, 1)
            run_act(act, jobs["k2"], keys)
            run_act(act, jobs["v2"], act_tokens_to(act, v2))
            act.wait_ge(evacuated, jobs["v2"].base + 1)
            act.activation(qk_tmp[:, :, :], qk12[:, :, :], ACT.Square).then_inc(r_act, 1)
            act.wait_ge(r_dve, 1)
            act.activation(qk_rstd, qk_mean, ACT.Abs_reciprocal_sqrt).then_inc(r_act, 1)
            act.wait_ge(r_dve, 11)
            att2.act(act)
            run_act(act, jobs["wo2"], None)
            act.wait_ge(evacuated, jobs["wo2"].base + 4)
            n25.act_squares(act)
            n25.act_rest(act)
            feed4.act(act)
            act.wait_ge(evacuated, jobs["b2_down1"].base + 8)
            last.act_squares(act)
            last.act_rest(act)

        @block.vector
        def _(dve):
            dve.memset(zeros[:, :], 0.0).then_inc(set_up, 1)
            dve.memset(mean[:, :], 0.0).then_inc(set_up, 1)
            dve.wait_ge(set_up, 2)
            first_splits(dve, split_lo)
            dve.wait_ge(start_in, 16 * len(START))
            first.dve(dve)
            for name in ("w_in_a", "w_in_g", "w_in_small"):
                run_dve(dve, jobs[name], None)
            retention_dve(dve)
            delta_dve(dve)
            gated_dve(dve)
            post_dve(dve)
            run_dve(dve, jobs["w_out"], dve_add_gated(dve, 2, None, 1))
            run_dve(dve, jobs["wk"], None)
            run_dve(dve, jobs["wv"], None)
            cross.dve(dve)
            run_dve(dve, jobs["wq"], None)
            att1.dve(dve)
            run_dve(dve, jobs["wo"], dve_add_gated(dve, 2, None, 1))
            ffn.dve(dve)
            feed0.dve(dve)
            between.dve(dve)
            mod_vector(dve)
            n20.dve(dve)
            feed1.dve(dve)
            branch_dve(dve, n21)
            n22.dve(dve)
            feed2.dve(dve)
            n23.dve(dve)
            feed3.dve(dve)
            n24.dve(dve)
            for name in ("q2", "k2", "v2"):
                run_dve(dve, jobs[name], None)
            n = 0

            def o(ins):
                nonlocal n
                n += 1
                ins.then_inc(r_dve, 1)
                dve.wait_ge(r_dve, n)
            flat = lambda ap: ap.rearrange("p n t -> p (n t)")
            dve.wait_ge(r_pe, 1)
            o(dve.tensor_scalar(flat(qk_mean), psum[:, 0:6, :].rearrange("p b t -> p (b t)"), 1.0 / P, EPS, ALU.mult, ALU.add))
            dve.wait_ge(r_act, 2)
            y, tmp = flat(qk_rstd), flat(qk_tmp[:, :, :])
            o(dve.scalar_tensor_tensor(tmp, y, -0.5, y, ALU.mult, ALU.mult))
            o(dve.tensor_tensor(tmp, tmp, flat(qk_mean), ALU.mult))
            o(dve.scalar_tensor_tensor(y, tmp, 1.5, y, ALU.add, ALU.mult))
            o(dve.scalar_tensor_tensor(qk12[:, 0:8, :], qk12[:, 0:8, :], col("g_q"), qk_rstd[:, 0:8, :], ALU.mult, ALU.mult))
            o(dve.scalar_tensor_tensor(qk12[:, 8:12, :], qk12[:, 8:12, :], col("g_k"), qk_rstd[:, 8:12, :], ALU.mult, ALU.mult))
            dve.wait_ge(r_pe, 2)
            dve.wait_ge(ax_in, 32)
            o(dve.tensor_tensor(qk_tmp[:, 0:10, :], psum[:, 0:5, :].rearrange("p b (n t) -> p (b n) t", t=T),
                                ax_sin[:, :].unsqueeze(1).to_broadcast([P, 10, T]), ALU.mult))
            o(dve.tensor_tensor(qk12[:, 0:8, :], qk12[:, 0:8, :], ax_cos[:, :].unsqueeze(1).to_broadcast([P, 8, T]), ALU.mult))
            o(dve.tensor_tensor(qk12[:, 0:8, :], qk12[:, 0:8, :], qk_tmp[:, 0:8, :], ALU.add))
            o(dve.tensor_tensor(kx, kx, ax_cos[:, :].unsqueeze(1).to_broadcast([P, 2, T]), ALU.mult))
            o(dve.tensor_tensor(kx, kx, qk_tmp[:, 8:10, :], ALU.add))
            att2.dve(dve)
            run_dve(dve, jobs["wo2"], dve_add_gated(dve, 2, gate_of(4), 1))
            n25.dve(dve)
            feed4.dve(dve)
            last.dve(dve)

        @block.gpsimd
        def _(pool):
            gated_pool(pool)
            for feed in (feed0, feed1, feed2, feed3, feed4):
                feed.pool(pool)


def shape_tables():
    f64 = np.float64
    i = np.arange(P)
    t = {}
    t["ident"] = np.eye(P)
    t["ones"] = np.ones((P, P))
    rot = np.zeros((P, P))
    for m in range(P):
        if m % 64 < 32:
            rot[m + 32, m] = -1.0
        else:
            rot[m - 32, m] = 1.0
    t["rot"] = rot
    t["row_sums"] = (i[:, None] // 2 == np.arange(2)[None, :]) & (i[:, None] < 4)
    t["headones"] = (i[:, None] // HD == i[None, :] // HD)
    t["lagsel"] = np.stack([i[:, None] // 32 == 2 * j + i[None, :] // HD for j in range(2)], 1)
    t["triu"] = i[:, None] <= i[None, :]
    t["triu_strict"] = i[:, None] < i[None, :]
    t["second_half"] = np.stack([(i[:, None] // (2 * L) == i[None, :] // (2 * L)) & (i[:, None] // L % 2 == 1) & (i[None, :] // L % 2 == 0)
                                 for L in (1, 2, 4, 8, 16, 32, 64)], 1)
    gamma = np.log(1.0 - np.exp2(-5.0 - np.arange(HEADS)))
    rel = np.arange(T)[None, :] - i[:, None]
    t["decay"] = np.stack([np.where(rel >= 0, np.exp(g * np.maximum(rel, 0)), 0.0) * HD ** -0.5 for g in gamma], 1)
    n, c = np.arange(T, dtype=f64), np.arange(P, dtype=f64)
    chan = 2 * np.pi * (np.outer(c, c) % P) / P
    tok = 2 * np.pi * (np.outer(n, n) % T) / T
    t["dft_c"] = np.concatenate([np.cos(chan), -np.sin(chan)], 1)
    for name, f in (("dft_cos", np.cos), ("dft_sin", np.sin)):
        t[name] = (f(tok) / np.sqrt(T * P)).reshape(2, P, T).transpose(1, 0, 2)
    grid_w, axis = 64, HD
    inv = (10000.0 ** (-np.arange(0, axis, 2, dtype=np.float32) / np.float32(axis))).astype(np.float32)
    ang = np.zeros((P, T), np.float32)
    for m in range(P):
        where = (np.arange(T) // grid_w if m < HD else np.arange(T) % grid_w).astype(np.float32)
        ang[m] = where * inv[m % 32]
    t["ax_cos"], t["ax_sin"] = np.cos(ang.astype(f64)), np.sin(ang.astype(f64))
    freqs = (np.float32(10000.0) ** (-np.arange(0, HD, 2, dtype=np.float32) / np.float32(HD))).astype(np.float32)
    t["freq"] = freqs[i % 32][:, None]
    return {k: np.ascontiguousarray(v, dtype=np.float32) for k, v in t.items()}


def features(a):
    a = np.asarray(a)
    return np.moveaxis(a.reshape(a.shape[:-1] + (-1, P)), -1, 0)


def tiles_fm(w, n_tiles=2):
    k, n = w.shape
    a = w.reshape(k // P, P, n // (P * n_tiles), n_tiles, P)
    return np.ascontiguousarray(a.transpose(2, 1, 3, 0, 4)).reshape(n // (P * n_tiles), P, -1)


def tiles_tm(w):
    k, n = w.shape
    return np.ascontiguousarray(w.reshape(k // P, P, n // 256, 256).transpose(2, 1, 0, 3)).reshape(n // 256, P, -1)


def pair_up(w, ff):
    g = np.zeros((2, w.shape[0], FF_TILES * P), np.float32)
    g[0, :, :ff], g[1, :, :ff] = w[:, :ff], w[:, ff:]
    a = g.reshape(2, KT, P, FF_TILES, P)
    return np.ascontiguousarray(a.transpose(3, 2, 0, 1, 4)).reshape(FF_TILES, P, -1)


def down(w):
    g = np.zeros((FF_TILES * P, w.shape[1]), np.float32)
    g[:w.shape[0]] = w
    a = g.reshape(2, HALF, P, KT, P)
    return np.ascontiguousarray(a.transpose(0, 3, 2, 1, 4)).reshape(2, KT, P, -1)


def kernel(**inp):
    import concourse.bacc as bacc
    from concourse.bass_utils import run_bass_kernel_spmd

    inp = {k: np.asarray(v) for k, v in inp.items()}
    nc = bacc.Bacc("TRN2", target_bir_lowering=False, num_devices=1)
    arrays, io = {}, {}

    def give(name, a):
        a = np.ascontiguousarray(a)
        arrays[f"in_{name}"] = a
        io[name] = nc.dram_tensor(f"in_{name}", a.shape, mybir.dt.from_np(a.dtype), kind="ExternalInput").ap()

    tables = shape_tables()
    for name, a in tables.items():
        if name != "freq":
            give(name, a)

    def stream(a):
        return a.reshape(T, KT, P).transpose(2, 1, 0)

    give("x", stream(inp["x"][0]))
    give("mem", stream(inp["mem"][0]))
    give("ctx", stream(inp["ctx_2"][0]))
    give("pos", np.broadcast_to(inp["positions"][0].astype(np.int32), (P, T)))

    w = inp["w_in"][0]
    names = "rq rk rv rg bq bk bv ba bb bg cq ck cv c_lr cg dq df di dg".split()
    widths = [256, 256, 256, 256, 256, 256, 256, 4, 4, 256, 128, 128, 256, 16, 256, 256, 256, 256, 256]
    at = dict(zip(names, np.cumsum([0] + widths[:-1])))
    part = {n: w[:, at[n]:at[n] + wd] for n, wd in zip(names, widths)}
    give("w_in_a", tiles_fm(np.concatenate([part[n] for n in "rq rk bq bk bv cq dq ck df rv cv di".split()], 1)))
    give("w_in_g", tiles_fm(np.concatenate([part[n] for n in "rg bg cg dg".split()], 1)))
    few = np.zeros((D, P), np.float32)
    few[:, 0:4], few[:, 32:36], few[:, 64:80] = part["ba"], part["bb"], part["c_lr"]
    give("w_in_small", tiles_fm(few, 1))
    gk = np.zeros((P, P), np.float32)
    gk[64:80] = inp["gla_gk_up"][0]
    give("gk_up", gk)
    give("w_out", tiles_fm(inp["w_out"][0]))
    give("wk", tiles_fm(inp["xattn_wk"][0]))
    give("wv", tiles_tm(inp["xattn_wv"][0]))
    give("wq", tiles_fm(inp["xattn_wq"][0]))
    give("wo", tiles_fm(inp["xattn_wo"][0]))
    ff1, ff2 = inp["ffn_down"].shape[1], inp["w_ffn1_down_2"].shape[1]
    ups = {"ffn": pair_up(inp["ffn_up"][0], ff1), "a1": pair_up(inp["w_ffn1_gu_2"][0], ff2), "a2": pair_up(inp["w_ffn2_gu_2"][0], ff2),
           "b1": pair_up(inp["w_ffn1_gu_2"][1], ff2), "b2": pair_up(inp["w_ffn2_gu_2"][1], ff2)}
    downs = {"ffn": down(inp["ffn_down"][0]), "a1": down(inp["w_ffn1_down_2"][0]), "a2": down(inp["w_ffn2_down_2"][0]),
             "b1": down(inp["w_ffn1_down_2"][1]), "b2": down(inp["w_ffn2_down_2"][1])}
    for name in ups:
        for half in range(2):
            give(f"{name}_up{half}", ups[name][half * HALF:(half + 1) * HALF])
            give(f"{name}_down{half}", downs[name][half])
    give("mod", np.concatenate([tiles_tm(inp["w_mod_2"][l]) for l in range(2)]))
    ab = inp["w_in_ab_2"][0]
    give("ab_a", tiles_fm(ab[:, 0:512]))
    give("ab_u", tiles_fm(ab[:, 512:1024]))
    give("ab_v", tiles_tm(ab[:, 1024:1536]))
    give("ab_out", tiles_fm(inp["w_out_ab_2"][0]))
    qkv = inp["w_qkv_2"][0]
    give("q2", tiles_fm(qkv[:, 0:1024]))
    give("k2", tiles_fm(qkv[:, 1024:1280]))
    give("v2", tiles_tm(qkv[:, 1280:1536]))
    give("wo2", tiles_fm(inp["w_o_2"][0]))
    give("ws_t", inp["w_s_2"][0].transpose(2, 0, 1))
    give("bs_row", np.broadcast_to(inp["b_s_2"][0], (P, 4, P)))
    give("gv_row", np.broadcast_to(inp["g_v_2"][0], (P, 4, P)))
    give("b_mod", features(inp["b_mod_2"].reshape(-1)))
    give("gains", np.stack([features(inp[g][l]) for l in range(2) for g in ("g_ffn1_2", "g_mix_2", "g_ffn2_2")], 1))
    give("c_in", np.stack([features(inp["c_2"][0]), features(inp["c_ctx_2"])], 2))

    blocks, cols, width = [], {}, 0

    def block(name, a):
        nonlocal width
        full = np.zeros((P, a.shape[1]), np.float32)
        full[:a.shape[0]] = a
        blocks.append(full)
        cols[name] = width
        width += a.shape[1]

    for name in ("mix_norm_w", "mem_norm_w", "xattn_norm_w", "ffn_norm_w", "final_norm_w"):
        block(name, features(inp[name].reshape(-1)))
    block("g_final", features(inp["g_final_2"]))
    for tap in range(4):
        block(f"gdn_conv{tap}", features(inp["gdn_conv_w"][0][tap]))
    for tap in range(3):
        w_tap = np.zeros((2, FF_TILES * P), np.float32)
        w_tap[:, :ff1] = inp["ffn_conv_w"][0][tap].reshape(2, ff1)
        block(f"ff_conv{tap}", features(w_tap.reshape(-1)))
    block("gdn_dt", inp["gdn_dt_bias"].T)
    block("gdn_a_log", inp["gdn_a_log"].T)
    block("rate", np.zeros((P, 1)))
    block("gk_bias", inp["gla_gk_bias"].T)
    block("freq", tables["freq"])
    head_gain = np.ones((P, 8), np.float32)
    for j, name in enumerate(("gdn_norm_w", "gla_norm_w", "hgrn_norm_w")):
        for i in range(2):
            for tile in range(2):
                head_gain[i * HD:(i + 1) * HD, 2 + 2 * j + tile] = inp[name][0]
    block("head_gain", head_gain)
    block("g_q", inp["g_q_2"].T)
    block("g_k", inp["g_k_2"].T)
    for name, n in (("gcol", 8), ("bcol", 8), ("gam", 8), ("tailc", 4), ("att", 8)):
        block(name, np.zeros((P, n)))
    io["cols"] = cols
    give("small", np.concatenate(blocks, 1))

    io["out"] = nc.dram_tensor("out", (P, KT, T), F32, kind="ExternalOutput").ap()
    full, dn = CHUNK, HALF * P
    plan = [("w_in_a", 11, full), ("w_in_g", 4, full), ("w_in_small", 1, full // 2), ("w_out", 4, full), ("wk", 4, full), ("wv", 4, full),
            ("wq", 4, full), ("wo", 4, full)]

    def feed(name):
        return [(f"{name}_up0", HALF, full), (f"{name}_down0", KT, dn), (f"{name}_up1", HALF, full), (f"{name}_down1", KT, dn)]

    plan += feed("ffn") + [("mod", 72, full)] + feed("a1") + [("ab_a", 2, full), ("ab_u", 2, full), ("ab_v", 2, full), ("ab_out", 4, full)]
    plan += feed("a2") + feed("b1") + [("q2", 4, full), ("k2", 1, full), ("v2", 1, full), ("wo2", 4, full)] + feed("b2")
    plan = [(name, n, size, io[name]) for name, n, size in plan]
    build(nc, io, plan)
    got = run_bass_kernel_spmd(nc, [arrays], core_ids=[0]).results[0]["out"]
    return np.ascontiguousarray(got.transpose(2, 1, 0)).reshape(1, T, D)
```

```python
from contextlib import ExitStack

import numpy as np

import concourse.bass as bass
from concourse import mybir

F32 = mybir.dt.float32
F32R = mybir.dt.float32r
I32 = mybir.dt.int32
ACT = mybir.ActivationFunctionType
ALU = mybir.AluOpType
AX_X = mybir.AxisListType.X

P = 128
T = 256
D = 1024
KT = D // P
SLOTS = 3
CHUNK = 2048
EPS = 1e-6
HEADS = 4
HD = 64
FF_TILES = 22
HALF = FF_TILES // 2
LAG = 16
LEVELS = (128, 64, 32, 16)
MAGIC = 1.5 * 2.0**23
TWO_PI_A = 6.28125
TWO_PI_B = 0.0019353071693331003

RQ, RK, BQ, BK, BV, CQ, DQ, CK, DF, RV, CV, DI, RG, BG, CG, DG = 0, 2, 4, 6, 8, 10, 11, 13, 14, 16, 18, 20, 22, 24, 26, 28
Z_TILES = 30


class Job:

    def __init__(self, base, n, size, dram, first=False, mod_base=None):
        self.base, self.n, self.size, self.dram, self.first, self.mod_base = base, n, size, dram, first, mod_base

    def is_mod(self, c):
        return self.mod_base is not None and c % SLOTS == 1

    def size_at(self, c):
        return CHUNK if self.is_mod(c) else self.size


class Step:

    def __init__(self, job, c, u, i=None):
        self.job, self.chunk = job, c
        self.g = c + job.base
        self.is_mod = job.is_mod(u)
        if i is None:
            i, u3 = u // SLOTS, u % SLOTS
        else:
            u3 = u
        self.c = c if job.mod_base is None else i * (SLOTS - 1) + (1 if u3 == SLOTS - 1 else 0)
        self.m = None if job.mod_base is None else i + job.mod_base
        self.static = c if isinstance(c, int) else None
        self.slot = (job.base + u) % SLOTS
        self.bank = 2 * self.slot


def steps(eng, job, ahead=0):
    loops = max(0, job.n - ahead) // SLOTS
    done = 0
    if loops >= 2:
        peeled = 1 if job.first else 0
        for c in range(peeled * SLOTS):
            s = Step(job, c, c)
            s.looped = False
            yield s
        with eng.Fori(peeled, loops) as i:
            for u in range(SLOTS):
                s = Step(job, i * SLOTS + u, u, i)
                s.looped = True
                s.i = i
                s.u = u
                yield s
        done = loops * SLOTS
    for c in range(done, job.n):
        s = Step(job, c, c)
        s.looped = False
        yield s


def build(nc, io, plan):
    jobs = {}
    sizes = []
    mod_chunks = 0
    for name, n, size, dram, mixed in plan:
        job = jobs[name] = Job(len(sizes), n, size, dram, first=name in ("w_in_a", "w_out", "ffn_up0"), mod_base=mod_chunks if mixed else None)
        mod_chunks += sum(job.is_mod(c) for c in range(n))
        sizes += [job.size_at(c) for c in range(n)]
    total = len(sizes)

    with ExitStack() as ctx:
        def sb(name, shape, dt=F32, scope=ctx):
            return scope.enter_context(nc.sbuf_tensor(name, shape, dt))

        def sem(name):
            return ctx.enter_context(nc.semaphore(name))

        psum = ctx.enter_context(nc.psum_tensor("psum", [P, 8, 512], F32))

        raw = sb("raw", [P, SLOTS, CHUNK])
        w_hi = sb("w_hi", [P, SLOTS, CHUNK], F32R)
        w_lo = sb("w_lo", [P, SLOTS, CHUNK], F32R)
        xc = sb("xc", [P, KT, 2 * T])
        xn_hi = sb("xn_hi", [P, KT, 2 * T], F32R)
        xn_lo = sb("xn_lo", [P, KT, 2 * T], F32R)
        small = sb("small", [P, io["small"].shape[1]])
        ident = sb("ident", [P, P])
        ones = sb("ones", [P, P])
        rot = sb("rot", [P, P])
        row_sums = sb("row_sums", [P, 2])
        zeros = sb("zeros", [P, T + P], mybir.dt.bfloat16)
        work = sb("work", [P, 8192])
        nrm = work[:, 0:KT * 2 * T].rearrange("p (k t) -> p k t", k=KT)
        rstd = sb("rstd", [P, 2 * T])
        mean = sb("mean", [P, 2 * T])
        mods = sb("mods", [P, 144, 2])
        gains = sb("gains", [P, 6, KT])
        scales = sb("scales", [P, 6, KT, 2])
        b_mod = sb("b_mod", [P, 144])
        c_in = sb("c_in", [P, KT, 2])
        c4 = sb("c4", [P, KT, 4], F32R)
        X = slice(0, T)
        C = slice(T, 2 * T)
        XC = slice(0, 2 * T)

        cols = io["cols"]

        def col(name, k=0):
            return small[:, cols[name] + k:cols[name] + k + 1]

        raw_landed = [sem(f"raw_landed{s}") for s in range(SLOTS)]
        tables_in = sem("tables_in")
        start_in = sem("start_in")
        hi_ready = sem("hi_ready")
        lo_ready = sem("lo_ready")
        chunk_done = sem("chunk_done")
        evacuated = sem("evacuated")

        def load(sp, s):
            if s.looped or s.g >= SLOTS:
                sp.wait_ge(lo_ready, s.g + (1 - SLOTS))
            src = io["mod"][s.m] if s.is_mod else s.job.dram[s.c]
            sp.dma_start(raw[:, s.slot, 0:CHUNK if s.is_mod else s.job.size], src).then_inc(raw_landed[s.slot], 16)

        def split_hi(act, s, ahead=2):
            if not s.looped and s.g + ahead >= total:
                return
            slot = (s.slot + ahead) % SLOTS
            size = s.job.size_at(s.u + ahead) if s.looped else sizes[s.g + ahead]
            g = s.g + ahead
            turn = (s.i + (s.job.base + s.u + ahead) // SLOTS) if s.looped else g // SLOTS
            act.wait_ge(raw_landed[slot], turn * 16 + 16)
            if s.looped or g >= SLOTS:
                act.wait_ge(chunk_done, s.g + (ahead + 1 - SLOTS))
            act.activation(w_hi[:, slot, 0:size], raw[:, slot, 0:size], ACT.Copy).then_inc(hi_ready, 1)

        def split_lo(dve, s, ahead=2):
            if not s.looped and s.g + ahead >= total:
                return
            slot = (s.slot + ahead) % SLOTS
            size = s.job.size_at(s.u + ahead) if s.looped else sizes[s.g + ahead]
            dve.wait_ge(hi_ready, s.g + (ahead + 1))
            dve.tensor_tensor(w_lo[:, slot, 0:size], raw[:, slot, 0:size], w_hi[:, slot, 0:size].bitcast(F32),
                              ALU.subtract).then_inc(lo_ready, 1)

        def first_splits(eng, split):
            for c in range(2):
                s = Step(Job(0, total, 0, None), c - 2, c - 2)
                s.g = c - 2
                s.slot = (c - 2) % SLOTS
                s.looped = False
                split(eng, s)

        def bank_free(pe, s):
            if s.looped or s.g >= SLOTS:
                pe.wait_ge(evacuated, s.g + (1 - SLOTS))

        def three_passes(pe, out, lhs, rhs, first, last, group=False):
            (lh, ll), (rh, rl) = lhs, rhs
            pe.matmul(out, lh, rh, start=first, stop=False, skip_group_check=group)
            pe.matmul(out, lh, rl, start=False, stop=False, skip_group_check=group)
            return pe.matmul(out, ll, rh, start=False, stop=last, skip_group_check=group)

        def pe_feature_major(pe, job, act_hi, act_lo, span, n_tiles=2, k_tiles=KT, before_k=None):
            for s in steps(pe, job):
                bank_free(pe, s)
                if s.is_mod:
                    mod_pe(pe, s)
                    continue
                pe.wait_ge(lo_ready, s.g + 1)
                for n in range(n_tiles):
                    for k in range(k_tiles):
                        if before_k is not None and n == 0:
                            before_k(s, k)
                        w = slice((n * k_tiles + k) * P, (n * k_tiles + k + 1) * P)
                        mm = three_passes(pe, psum[:, s.bank + n, 0:span.stop - span.start],
                                          (w_hi[:, s.slot, w], w_lo[:, s.slot, w]),
                                          (act_hi[:, k, span], act_lo[:, k, span]), k == 0, k == k_tiles - 1)
                mm.then_inc(chunk_done, 1)

        def pe_token_major(pe, job, span):
            for s in steps(pe, job):
                bank_free(pe, s)
                if s.is_mod:
                    mod_pe(pe, s)
                    continue
                pe.wait_ge(lo_ready, s.g + 1)
                for tt in range((span.stop - span.start) // P):
                    tok = slice(span.start + tt * P, span.start + (tt + 1) * P)
                    for k in range(KT):
                        w = slice(k * 256, (k + 1) * 256)
                        mm = three_passes(pe, psum[:, s.bank + tt // 2, (tt % 2) * 256:(tt % 2) * 256 + 256],
                                          (xn_hi[:, k, tok], xn_lo[:, k, tok]),
                                          (w_hi[:, s.slot, w], w_lo[:, s.slot, w]), k == 0, k == KT - 1)
                mm.then_inc(chunk_done, 1)

        n_sq, n_added, n_sum, n_mean, n_guess, n_rstd, n_scaled, n_hi, n_lo = [sem(x) for x in (
            "norm_squares", "norm_squares_added", "norm_sums", "norm_mean", "norm_guess", "norm_rstd", "norm_scaled", "norm_hi", "norm_lo")]

        class Norm:
            made, scaled, split, squared = 0, 0, 0, 0

            def __init__(self, span, scale, shift=None, out=None, tiles=1):
                self.tiles = tiles
                self.squared_base = Norm.squared
                Norm.squared += KT // tiles
                self.j, self.span, self.scale, self.shift, self.out = Norm.made, span, scale, shift, out
                self.w = span.stop - span.start
                self.halves = self.w // T
                self.scaled_base, self.split_base = Norm.scaled, Norm.split
                Norm.made += 1
                Norm.scaled += KT * self.halves
                Norm.split += 0 if out is not None else KT * self.halves

            def act_squares(self, act):
                for k in range(0, KT, self.tiles):
                    act.activation(nrm[:, k:k + self.tiles, 0:self.w], xc[:, k:k + self.tiles, self.span], ACT.Square).then_inc(n_sq, 1)

            def act_squares_after(self, act):
                def evac(s):
                    k = s.c * self.tiles
                    tile = bass.ds(k, self.tiles) if s.looped else slice(k, k + self.tiles)
                    act.wait_ge(evacuated, s.g + 1)
                    act.activation(nrm[:, tile, 0:self.w], xc[:, tile, self.span], ACT.Square).then_inc(n_sq, 1)
                return evac

            def pool(self, pool):
                for k in range(1, KT):
                    pool.wait_ge(n_sq, self.squared_base + k // self.tiles + 1)
                    if k > 1 or self.j:
                        pool.wait_ge(n_added, self.j * (KT - 1) + k - 1)
                    pool.tensor_tensor(nrm[:, 0, 0:self.w], nrm[:, 0, 0:self.w], nrm[:, k, 0:self.w], ALU.add).then_inc(n_added, 1)

            def pe(self, pe):
                pe.wait_ge(n_added, (self.j + 1) * (KT - 1))
                pe.matmul(psum[:, 6, 0:self.w], ones[:, :], nrm[:, 0, 0:self.w], start=True, stop=True).then_inc(n_sum, 1)

            def act_rest(self, act):
                act.wait_ge(n_mean, self.j + 1)
                act.activation(rstd[:, 0:self.w], mean[:, 0:self.w], ACT.Abs_reciprocal_sqrt).then_inc(n_guess, 1)
                if self.out is not None:
                    return
                for k in range(KT):
                    act.wait_ge(n_scaled, self.scaled_base + (k + 1) * self.halves)
                    for h in range(self.halves):
                        t, o = slice(h * T, (h + 1) * T), slice(self.span.start + h * T, self.span.start + (h + 1) * T)
                        if self.shift is None:
                            act.activation(xn_hi[:, k, o], nrm[:, k, t], ACT.Copy).then_inc(n_hi, 1)
                        else:
                            act.activation(xn_hi[:, k, o], nrm[:, k, t], ACT.Identity, bias=self.shift(k, h)).then_inc(n_hi, 1)

            def dve(self, dve):
                m, r, j3 = mean[:, 0:self.w], rstd[:, 0:self.w], 3 * self.j
                tmp = work[:, 7168:7168 + self.w]
                dve.wait_ge(n_sum, self.j + 1)
                dve.tensor_scalar(m, psum[:, 6, 0:self.w], 1.0 / D, EPS, ALU.mult, ALU.add).then_inc(n_mean, 1)
                dve.wait_ge(n_guess, self.j + 1)
                dve.scalar_tensor_tensor(tmp, r, -0.5, r, ALU.mult, ALU.mult).then_inc(n_rstd, 1)
                dve.wait_ge(n_rstd, j3 + 1)
                dve.tensor_tensor(tmp, tmp, m, ALU.mult).then_inc(n_rstd, 1)
                dve.wait_ge(n_rstd, j3 + 2)
                dve.scalar_tensor_tensor(r, tmp, 1.5, r, ALU.add, ALU.mult).then_inc(n_rstd, 1)
                dve.wait_ge(n_rstd, j3 + 3)

                def low(k):
                    dve.wait_ge(n_hi, self.split_base + (k + 1) * self.halves)
                    for h in range(self.halves):
                        t, o = slice(h * T, (h + 1) * T), slice(self.span.start + h * T, self.span.start + (h + 1) * T)
                        if self.shift is None:
                            dve.tensor_tensor(xn_lo[:, k, o], nrm[:, k, t], xn_hi[:, k, o].bitcast(F32), ALU.subtract).then_inc(n_lo, 1)
                        else:
                            dve.scalar_tensor_tensor(xn_lo[:, k, o], nrm[:, k, t], self.shift(k, h), xn_hi[:, k, o].bitcast(F32),
                                                     ALU.add, ALU.subtract).then_inc(n_lo, 1)

                for k in range(KT):
                    for h in range(self.halves):
                        t, o = slice(h * T, (h + 1) * T), slice(self.span.start + h * T, self.span.start + (h + 1) * T)
                        dst = nrm[:, k, t] if self.out is None else self.out[:, k, t]
                        dve.scalar_tensor_tensor(dst, xc[:, k, o], self.scale(k, h), r[:, t], ALU.mult, ALU.mult).then_inc(n_scaled, 1)
                    if self.out is None and k:
                        low(k - 1)
                if self.out is None:
                    low(KT - 1)

            def ready(self, pe, k):
                pe.wait_ge(n_lo, self.split_base + (k + 1) * self.halves)

        AT = {
            "ret_act": dict(sines=2),
            "ret_dve": dict(angle=6, rotated=11, v_tok=12, decayed=14, out=15),
            "ret_pe": dict(turned=1, v_tok=2, scores=3, out=4),
            "gdn_act": dict(taps=1, softplus=4, rate=5, beta=6, silu=7, squares=8, rsqrt=9, tail=10, col_decays=11,
                            ratio=12, q_decay=13),
            "gdn_dve": dict(cleared=1, conv=4, rows=7, tok=8, spread=10, cums=11, cum_rows=12, beta_rows=13, tail=14,
                            log_ratio=16, sums=17, unit=22, tokens=24, strict=31, products=38, u0=39,
                            s1=40, rest=42, u1=43, out=44),
            "gdn_pe": dict(tok=1, cums=2, cum_rows=3, beta_rows=4, sums=5, tokens=6, kk=7, u0=8, s1=9, w=10, u1=11,
                           out=12),
            "gat_act": dict(u=1, ln=4, key=5),
            "gat_dve": dict(u=1, log_f=3, scaled=4, tok=6, out=7),
            "gat_pe": dict(gk=1, tok=2, zero=3, out=4),
            "post_act": dict(squares=1, rsqrt=2),
            "post_dve": dict(mean=1, unit=4, scaled=13),
            "post_pe": dict(sums=1),
        }
        stage_sem = {name: sem(name) for name in AT}

        class order:
            def __init__(self, eng, name):
                self.eng, self.name, self.n = eng, name, 0

            def __call__(self, ins, result=None):
                self.n += 1
                ins.then_inc(stage_sem[self.name], 1)
                if result is not None:
                    assert AT[self.name][result] == self.n, (self.name, result, self.n)
                self.eng.wait_ge(stage_sem[self.name], self.n)

        def need(eng, name, result):
            eng.wait_ge(stage_sem[name], AT[name][result])

        def bank(b):
            return psum[:, b, :]

        def area(at, n, w=P):
            return work[:, at:at + n * w].rearrange("p (n t) -> p n t", t=w)

        mix = ExitStack()
        z = sb("z", [P, Z_TILES, T], scope=mix)
        zs = sb("zs", [P, T], scope=mix)
        headones = sb("headones", [P, P], scope=mix)
        lagsel = sb("lagsel", [P, 2, P], scope=mix)
        triu = sb("triu", [P, P], scope=mix)
        triu_strict = sb("triu_strict", [P, P], scope=mix)
        second_half = sb("second_half", [P, 7, P], scope=mix)
        decay = sb("decay", [P, HEADS, T], scope=mix)
        gk_up = sb("gk_up", [P, P], scope=mix)
        pos = sb("pos", [P, T], I32, scope=mix)
        gt = sb("gt", [P, 2, P], scope=mix)
        s1 = sb("s1", [P, 2, HD], scope=mix)
        MIX = ["headones", "lagsel", "triu", "triu_strict", "second_half", "decay", "gk_up", "pos"]
        MIX_T = dict(headones=headones, lagsel=lagsel, triu=triu, triu_strict=triu_strict, second_half=second_half,
                     decay=decay, gk_up=gk_up, pos=pos)

        def load_mixer_tables(sp):
            for name in MIX:
                sp.dma_start(MIX_T[name][:], io[name]).then_inc(tables_in, 16)

        ret_a = work[:, 10 * T:16 * T].rearrange("p (h n) -> p h n", h=HEADS)
        ret_v = area(8 * T, 2, T)

        def retention_dve(dve):
            o = order(dve, "ret_dve")
            ang, kk_, sn = work[:, 0:T], work[:, T:2 * T], work[:, 2 * T:3 * T]
            dve.wait_ge(tables_in, 16 * len(MIX))
            o(dve.tensor_copy(ang, pos[:, :]))
            o(dve.tensor_scalar(ang, ang, col("freq"), None, ALU.mult))
            o(dve.tensor_scalar(kk_, ang, 1.0 / (2 * np.pi), MAGIC, ALU.mult, ALU.add))
            o(dve.tensor_scalar(kk_, kk_, MAGIC, None, ALU.subtract))
            o(dve.scalar_tensor_tensor(ang, kk_, -TWO_PI_A, ang, ALU.mult, ALU.add))
            o(dve.scalar_tensor_tensor(ang, kk_, -TWO_PI_B, ang, ALU.mult, ALU.add), "angle")
            need(dve, "ret_act", "sines")
            o(dve.tensor_tensor(kk_, sn, sn, ALU.mult))
            o(dve.tensor_scalar(kk_, kk_, -2.0, 1.0, ALU.mult, ALU.add))
            qk = z[:, RQ:RQ + 4, :]
            turned = psum[:, 0:2, :].rearrange("p b (t n) -> p (b t) n", n=T)
            part = area(4 * T, 4, T)
            need(dve, "ret_pe", "turned")
            sines = work[:, 3 * T:4 * T].unsqueeze(1).to_broadcast([P, 4, T])
            coss = kk_.unsqueeze(1).to_broadcast([P, 4, T])
            o(dve.tensor_tensor(part, turned, sines, ALU.mult))
            o(dve.tensor_tensor(qk, qk, coss, ALU.mult))
            o(dve.tensor_tensor(qk, qk, part, ALU.add), "rotated")
            need(dve, "ret_pe", "v_tok")
            o(dve.tensor_copy(ret_v, psum[:, 2, :].rearrange("p (t n) -> p t n", n=T)), "v_tok")
            need(dve, "ret_pe", "scores")
            o(dve.tensor_tensor(ret_a[:, :, 0:T], psum[:, 3:7, 0:T], decay[:, :, :], ALU.mult))
            o(dve.tensor_tensor(ret_a[:, :, T:T + P], psum[:, 3:7, T:T + P], decay[:, :, 0:P], ALU.mult), "decayed")
            need(dve, "ret_pe", "out")
            o(dve.tensor_copy(z[:, 0:2, :], psum[:, 7, :].rearrange("p (t n) -> p t n", n=T)), "out")

        def retention_act(act):
            o = order(act, "ret_act")
            need(act, "ret_dve", "angle")
            o(act.activation(work[:, 2 * T:3 * T], work[:, 0:T], ACT.Sin, scale=0.5))
            o(act.activation(work[:, 3 * T:4 * T], work[:, 0:T], ACT.Sin), "sines")

        def retention_pe(pe):
            pe.wait_ge(evacuated, jobs["w_in_small"].base + 1)
            pe.wait_ge(tables_in, 16 * len(MIX))
            o = order(pe, "ret_pe")
            pe.matmul(bank(0), rot[:, :], z[:, RQ:RQ + 2, :], start=True, stop=True)
            o(pe.matmul(bank(1), rot[:, :], z[:, RK:RK + 2, :], start=True, stop=True), "turned")
            for tt in range(2):
                for n in range(2):
                    mm = pe.transpose(psum[:, 2, tt * T + n * P:tt * T + (n + 1) * P], z[:, RV + n, tt * P:(tt + 1) * P], ident[:, :])
            o(mm, "v_tok")
            need(pe, "ret_dve", "rotated")
            for h in range(HEADS):
                r = slice((h % 2) * HD, (h % 2) * HD + HD)
                for st in range(2):
                    mm = pe.matmul(psum[:, 3 + h, st * T:st * T + T - st * P], z[r, RK + h // 2, st * P:(st + 1) * P],
                                   z[r, RQ + h // 2, st * P:T], start=True, stop=True)
            o(mm, "scores")
            need(pe, "ret_dve", "decayed")
            for h in range(HEADS):
                r = slice((h % 2) * HD, (h % 2) * HD + HD)
                c = (h // 2) * T
                v = slice(h * HD, (h + 1) * HD)
                pe.matmul(psum[r, 7, c:c + T], ret_v[:, 0, v], ret_a[:, h, 0:T], start=True, stop=False, skip_group_check=True)
                mm = pe.matmul(psum[r, 7, c + P:c + T], ret_v[:, 1, v], ret_a[:, h, T:T + P], start=False, stop=True, skip_group_check=True)
            o(mm, "out")

        XM, XT, NT, QT, YM, BR, GR, RT = (area(i * 1024, 8) for i in range(8))
        taps = area(0, 6, T)
        ssum, unit_tmp = area(0, 4, T), area(1024, 4, T)
        g_spread, b_spread = NT, QT
        sq4 = area(4096, 4, T)
        gb = work[:, 5120:5120 + T]
        U0, U1, REST = (work[:, 5120 + i * T:5120 + (i + 1) * T] for i in range(3))
        qg = area(5120 + 3 * T, 2)
        k_tok, v_tok = z[:, 16:18, :], z[:, 2:4, :]
        gcol, bcol, gam = (small[:, cols[x]:cols[x] + 8].rearrange("p (n h) -> p n h", n=2) for x in ("gcol", "bcol", "gam"))
        tailc = small[:, cols["tailc"]:cols["tailc"] + 4]
        level_y, level_x, level_pe = sem("inverse_masked"), sem("inverse_updated"), sem("inverse_products")

        def by_head(ap):
            return ap.rearrange("p n (h d) -> p n h d", d=HD)

        def by_parity(ap, n):
            return ap[:, n * 4:n * 4 + 4, :].rearrange("p (b a) t -> p a b t", a=2)

        def two_banks(b, w=P):
            return psum[:, b:b + 2, :].rearrange("p b (n t) -> p (b n) t", t=w)

        def newton(dve, o, y, v, tmp, result=None):
            o(dve.scalar_tensor_tensor(tmp, y, -0.5, y, ALU.mult, ALU.mult))
            o(dve.tensor_tensor(tmp, tmp, v, ALU.mult))
            o(dve.scalar_tensor_tensor(y, tmp, 1.5, y, ALU.add, ALU.mult), result)

        def delta_act(act):
            o = order(act, "gdn_act")
            need(act, "ret_dve", "out")
            for k in range(6):
                mm = act.activation(taps[:, k, :], z[:, BQ + k, :], ACT.Copy, scale=col("gdn_conv3", k))
            o(mm, "taps")
            need(act, "gdn_dve", "cleared")
            o(act.activation(gb[0:4, :], zs[0:4, :], ACT.Abs, bias=col("gdn_dt")[0:4, :]))
            o(act.activation(gb[0:4, :], gb[0:4, :], ACT.Exp, scale=-1.0))
            o(act.activation(gb[0:4, :], gb[0:4, :], ACT.Ln, bias=1.0), "softplus")
            o(act.activation(col("rate")[0:4, :], col("gdn_a_log")[0:4, :], ACT.Exp), "rate")
            o(act.activation(gb[32:36, :], zs[32:36, :], ACT.Sigmoid), "beta")
            need(act, "gdn_dve", "conv")
            o(act.activation(z[:, BQ:BQ + 6, :], taps, ACT.Silu), "silu")
            o(act.activation(sq4, z[:, BQ:BQ + 4, :], ACT.Square), "squares")
            need(act, "gdn_dve", "sums")
            o(act.activation(sq4, ssum, ACT.Abs_reciprocal_sqrt), "rsqrt")
            o(act.activation(tailc, tailc, ACT.Exp), "tail")
            o(act.activation(gam, gcol, ACT.Exp), "col_decays")
            o(act.activation(RT, RT, ACT.Exp), "ratio")
            o(act.activation(GR[:, 4:8, :], GR[:, 4:8, :], ACT.Exp), "q_decay")

        def delta_dve(dve):
            o = order(dve, "gdn_dve")
            o(dve.memset(gb, 0.0), "cleared")
            need(dve, "gdn_act", "taps")
            for back in range(1, 4):
                for k in range(6):
                    mm = dve.scalar_tensor_tensor(taps[:, k, back:T], z[:, BQ + k, 0:T - back], col(f"gdn_conv{3 - back}", k),
                                                  taps[:, k, back:T], ALU.mult, ALU.add)
                o(mm, "conv" if back == 3 else None)
            need(dve, "gdn_act", "beta")
            o(dve.tensor_scalar(zs[0:4, :], zs[0:4, :], col("gdn_dt")[0:4, :], 0.0, ALU.add, ALU.max))
            o(dve.tensor_tensor(gb[0:4, :], gb[0:4, :], zs[0:4, :], ALU.add))
            o(dve.tensor_scalar(gb[0:4, :], gb[0:4, :], col("rate")[0:4, :], -1.0, ALU.mult, ALU.mult), "rows")
            need(dve, "gdn_pe", "tok")
            o(dve.tensor_copy(gt[:, :, :], psum[:, 0, 0:2 * P].rearrange("p (n t) -> p n t", n=2)), "tok")
            for dst, c in ((g_spread, 0), (b_spread, 32)):
                o(dve.tensor_copy(dst.rearrange("p (n h) t -> p n h t", n=2),
                                  gt[:, :, c:c + 4].unsqueeze(3).to_broadcast([P, 2, HEADS, P])), "spread" if c else None)
            need(dve, "gdn_pe", "cums")
            o(dve.tensor_copy(gcol, psum[:, 1, 0:8].rearrange("p (n h) -> p n h", n=2)), "cums")
            need(dve, "gdn_pe", "cum_rows")
            o(dve.tensor_copy(GR, two_banks(2)), "cum_rows")
            need(dve, "gdn_pe", "beta_rows")
            o(dve.tensor_copy(BR, two_banks(4)), "beta_rows")
            o(dve.tensor_tensor(tailc, GR[:, 0:4, P - 1], gcol[:, 0, :], ALU.subtract), "tail")
            gc8 = small[:, cols["gcol"]:cols["gcol"] + 8].unsqueeze(2).to_broadcast([P, 8, P])
            o(dve.tensor_tensor(RT, GR, gc8, ALU.subtract))
            o(dve.tensor_scalar(RT, RT, 0.0, None, ALU.min), "log_ratio")
            need(dve, "gdn_pe", "sums")
            o(dve.tensor_scalar(ssum, two_banks(6, T), EPS, None, ALU.add), "sums")
            need(dve, "gdn_act", "rsqrt")
            newton(dve, o, sq4, ssum, unit_tmp)
            qs, ks = z[:, BQ:BQ + 2, :], z[:, BK:BK + 2, :]
            o(dve.scalar_tensor_tensor(qs, qs, HD ** -0.5, sq4[:, 0:2, :], ALU.mult, ALU.mult))
            o(dve.tensor_tensor(ks, ks, sq4[:, 2:4, :], ALU.mult), "unit")
            need(dve, "gdn_pe", "tokens")
            o(dve.tensor_copy(k_tok, psum[:, 0, :].rearrange("p (n t) -> p n t", n=2)))
            beta = gt[:, :, 32:36]
            o(dve.tensor_tensor(by_head(v_tok), by_head(psum[:, 1, :].rearrange("p (n t) -> p n t", n=2)),
                                beta.unsqueeze(3).to_broadcast([P, 2, HEADS, HD]), ALU.mult), "tokens")
            need(dve, "gdn_act", "q_decay")
            o(dve.tensor_tensor(RT, RT, triu[:, :].unsqueeze(1).to_broadcast([P, 8, P]), ALU.mult))
            o(dve.tensor_tensor(BR, BR, RT, ALU.mult))
            o(dve.tensor_tensor(BR, BR, triu_strict[:, :].unsqueeze(1).to_broadcast([P, 8, P]), ALU.mult))
            o(dve.tensor_tensor(bcol, beta, gam, ALU.mult))
            k0 = k_tok[:, 0, :].rearrange("p (h d) -> p h d", d=HD)
            o(dve.tensor_tensor(k0, k0, tailc.unsqueeze(2).to_broadcast([P, HEADS, HD]), ALU.mult))
            need(dve, "gdn_pe", "kk")
            for dst, b, factor in ((NT, 2, BR), (QT, 4, RT)):
                for n in range(2):
                    o(dve.tensor_tensor(by_parity(dst, n), psum[:, b:b + 2, n * T:(n + 1) * T].rearrange("p a (b t) -> p a b t", t=P),
                                        by_parity(factor, n), ALU.mult), "strict" if b == 2 and n else None)
            for h in range(HEADS):
                r = slice((h % 2) * HD, (h % 2) * HD + HD)
                o(dve.tensor_tensor(qg[r, h // 2, :], z[r, BQ + h // 2, P:T], GR[r, 4 + h, :], ALU.mult))
            o(dve.tensor_copy(XM, ident[:, :].unsqueeze(1).to_broadcast([P, 8, P])), "products")
            dve.tensor_copy(XT, ident[:, :].unsqueeze(1).to_broadcast([P, 8, P])).then_inc(level_x, 1)
            with dve.Fori(0, 7) as i:
                dve.wait_ge(level_pe, i * 2 + 1)
                dve.tensor_tensor(YM, two_banks(0), second_half[:, bass.ds(i, 1), :].to_broadcast([P, 8, P]), ALU.mult).then_inc(level_y, 1)
                dve.wait_ge(level_pe, i * 2 + 2)
                dve.tensor_tensor(XT, XT, two_banks(4), ALU.subtract).then_inc(level_x, 1)
                dve.tensor_tensor(XM, XM, two_banks(2), ALU.subtract).then_inc(level_x, 1)
                dve.wait_ge(level_x, i * 2 + 3)
            need(dve, "gdn_pe", "u0")
            o(dve.tensor_copy(U0, psum[:, 6, 0:T]), "u0")
            need(dve, "gdn_pe", "s1")
            o(dve.tensor_copy(s1[:, :, :], psum[:, 7, 0:P].rearrange("p (n d) -> p n d", d=HD)), "s1")
            need(dve, "gdn_pe", "w")
            o(dve.tensor_tensor(REST.rearrange("p (b a d) -> p a b d", a=2, d=HD), psum[:, 0:2, 0:P].rearrange("p a (b d) -> p a b d", d=HD),
                                bcol[:, 1, :].rearrange("p (b a) -> p a b", a=2).unsqueeze(3).to_broadcast([P, 2, 2, HD]), ALU.mult))
            o(dve.tensor_tensor(REST, v_tok[:, 1, :], REST, ALU.subtract), "rest")
            need(dve, "gdn_pe", "u1")
            o(dve.tensor_copy(U1, psum[:, 1, 0:T]), "u1")
            need(dve, "gdn_pe", "out")
            o(dve.tensor_copy(z[:, 2:4, :], psum[:, 2, :].rearrange("p (n t) -> p n t", n=2)), "out")

        def delta_pe(pe):
            o = order(pe, "gdn_pe")
            heads4 = [(h, slice((h % 2) * HD, (h % 2) * HD + HD), slice(h * HD, (h + 1) * HD)) for h in range(HEADS)]
            need(pe, "gdn_dve", "rows")
            need(pe, "gdn_act", "beta")
            for n in range(2):
                mm = pe.transpose(psum[:, 0, n * P:(n + 1) * P], gb[:, n * P:(n + 1) * P], ident[:, :])
            o(mm, "tok")
            need(pe, "gdn_dve", "tok")
            for n in range(2):
                mm = pe.matmul(psum[:, 1, n * 4:n * 4 + 4], triu[:, :], gt[:, n, 0:4], start=True, stop=True)
            o(mm, "cums")
            need(pe, "gdn_dve", "spread")
            for nh in range(8):
                mm = pe.matmul(two_banks(2)[:, nh, :], g_spread[:, nh, :], triu[:, :], start=True, stop=True)
            o(mm, "cum_rows")
            for nh in range(8):
                mm = pe.matmul(two_banks(4)[:, nh, :], b_spread[:, nh, :], ident[:, :], start=True, stop=True)
            o(mm, "beta_rows")
            need(pe, "gdn_act", "squares")
            need(pe, "ret_dve", "out")
            for i in range(2):
                mm = pe.matmul(bank(6 + i), headones[:, :], sq4[:, 2 * i:2 * i + 2, :], start=True, stop=True)
            o(mm, "sums")
            need(pe, "gdn_dve", "unit")
            for b, tile in ((0, BK), (1, BV)):
                for n in range(2):
                    for i in range(2):
                        mm = pe.transpose(psum[:, b, n * T + i * P:n * T + (i + 1) * P], z[:, tile + i, n * P:(n + 1) * P], ident[:, :])
            o(mm, "tokens")
            for b, tile in ((2, BK), (4, BQ)):
                for n in range(2):
                    for h, r, _ in heads4:
                        mm = pe.matmul(psum[:, b + h % 2, (n * 2 + h // 2) * P:(n * 2 + h // 2 + 1) * P], z[r, BK + h // 2, n * P:(n + 1) * P],
                                       z[r, tile + h // 2, n * P:(n + 1) * P], start=True, stop=True)
            o(mm, "kk")
            need(pe, "gdn_dve", "products")
            with pe.Fori(0, 7) as i:
                pe.wait_ge(level_x, i * 2 + 1)
                for nh in range(8):
                    mm = pe.matmul(two_banks(0)[:, nh, :], NT[:, nh, :], XM[:, nh, :], start=True, stop=True)
                mm.then_inc(level_pe, 1)
                pe.wait_ge(level_y, i + 1)
                for nh in range(8):
                    pe.matmul(two_banks(4)[:, nh, :], YM[:, nh, :], XT[:, nh, :], start=True, stop=True)
                    mm = pe.matmul(two_banks(2)[:, nh, :], XT[:, nh, :], YM[:, nh, :], start=True, stop=True)
                mm.then_inc(level_pe, 1)
            pe.wait_ge(level_x, 15)
            for h, _, f in heads4:
                mm = pe.matmul(psum[:, 6, f], XT[:, h, :], v_tok[:, 0, f], start=True, stop=True)
            o(mm, "u0")
            need(pe, "gdn_dve", "u0")
            for h, r, f in heads4:
                mm = pe.matmul(psum[r, 7, (h // 2) * HD:(h // 2) * HD + HD], k_tok[:, 0, f], U0[:, f], start=True, stop=True)
            o(mm, "s1")
            need(pe, "gdn_dve", "s1")
            for h, r, f in heads4:
                mm = pe.matmul(psum[:, h % 2, (h // 2) * HD:(h // 2) * HD + HD], z[r, BK + h // 2, P:T], s1[r, h // 2, :], start=True, stop=True)
            o(mm, "w")
            need(pe, "gdn_dve", "rest")
            for h, _, f in heads4:
                mm = pe.matmul(psum[:, 1, f], XT[:, 4 + h, :], REST[:, f], start=True, stop=True)
            o(mm, "u1")
            need(pe, "gdn_dve", "u1")
            for h, r, f in heads4:
                c = (h // 2) * T
                pe.matmul(psum[r, 2, c:c + P], U0[:, f], QT[:, h, :], start=True, stop=True)
                pe.matmul(psum[r, 2, c + P:c + T], U1[:, f], QT[:, 4 + h, :], start=True, stop=False)
                mm = pe.matmul(psum[r, 2, c + P:c + T], s1[r, h // 2, :], qg[r, h // 2, :], start=False, stop=True)
            o(mm, "out")

        Q3, K3, V4, O4 = z[:, CQ:CQ + 3, :], z[:, CK:CK + 3, :], z[:, CV:CV + 4, :], z[:, 4:8, :]
        U3, C3, E3 = area(0, 3, T), area(768, 3, T), area(1536, 3, T)
        QK = [area(2304, 3, T), area(3072, 3, T)]
        A8 = area(3840, 8, T + P)
        resets = area(6912, 4, T)
        toks = [z[:, 16:18, :], z[:, 8:10, :]]
        LE = [area(1536, 3, T), area(0, 3, T)]
        LTMP = [area(3840, 4, T), area(4864, 4, T)]
        lv_cum, lv_exp, lv_qk, lv_pe = sem("level_cum"), sem("level_decays"), sem("level_scaled"), sem("level_scores")
        copied = sem("scores_copied")
        lag_diff, lag_exp, lag_p, lag_bc, lag_tmp, lag_acc = (sem(x) for x in (
            "lag_diff", "lag_decays", "lag_products", "lag_spread", "lag_values", "lag_added"))

        def halves_of(ap, L, side):
            return ap.rearrange("p g (b s l) -> p (g b) s l", s=2, l=L)[:, :, side, :]

        def gated_dve(dve):
            o = order(dve, "gat_dve")
            o(dve.tensor_copy(U3[:, 1:3, :], z[:, DF:DF + 2, :]), "u")
            need(dve, "gat_act", "ln")
            o(dve.scalar_tensor_tensor(U3, U3, 0.0, E3, ALU.min, ALU.subtract))
            o(dve.tensor_scalar(U3[:, 0, :], U3[:, 0, :], 1.0 / 16.0, None, ALU.mult), "log_f")
            o(dve.tensor_scalar(z[:, CQ, :], z[:, CQ, :], (HD // 2) ** -0.5, None, ALU.mult), "scaled")
            need(dve, "gat_pe", "tok")
            for i in range(2):
                o(dve.tensor_copy(toks[i], psum[:, 1 + i, :].rearrange("p (n t) -> p n t", n=2)), "tok" if i else None)
            for i, L in enumerate(LEVELS):
                dve.memset(resets[:, i, :], 1.0).then_inc(lv_cum, 1)
                dve.wait_ge(lv_cum, 2 * i + 1)
                dve.memset(resets[:, i, :].rearrange("p (b l) -> p b l", l=L)[:, :, 0], 0.0).then_inc(lv_cum, 1)
            dve.wait_ge(lv_cum, 8)
            need(dve, "gat_act", "key")
            for i, L in enumerate(LEVELS):
                if i:
                    dve.wait_ge(lv_exp, 2 * i)
                for g in range(3):
                    mm = dve.tensor_tensor_scan(C3[:, g, :], resets[:, i, :], U3[:, g, :], 0.0, ALU.mult, ALU.add)
                mm.then_inc(lv_cum, 1)
                dve.wait_ge(lv_cum, 8 + 2 * i + 1)
                left = halves_of(C3, L, 0)
                dve.tensor_tensor(halves_of(E3, L, 0), left[:, :, L - 1:L].to_broadcast([P, left.shape[1], L]), left,
                                  ALU.subtract).then_inc(lv_cum, 1)
                dve.wait_ge(lv_exp, 2 * i + 2)
                if i >= 2:
                    dve.wait_ge(lv_pe, i - 1)
                for side, src in ((0, K3), (1, Q3)):
                    dve.tensor_tensor(halves_of(QK[i % 2], L, side), halves_of(src, L, side), halves_of(E3, L, side),
                                      ALU.mult).then_inc(lv_qk, 1)
            dve.wait_ge(lv_pe, len(LEVELS))
            for j in range(4, 8):
                dve.tensor_copy(A8[:, j, :], psum[:, j, 0:T + P]).then_inc(copied, 1)
            need(dve, "gat_pe", "out")
            o(dve.tensor_copy(O4, two_banks(0, T)), "out")
            for lag in range(LAG + 1):
                if lag < LAG:
                    w = LAG - lag
                    lp = QK[lag % 2].rearrange("p g t -> p (g t)")[:, 0:48 * w].rearrange("p (b l) -> p b l", l=w)
                    q = Q3.rearrange("p g (b l) -> p (g b) l", l=LAG)[:, :, lag:LAG]
                    k = K3.rearrange("p g (b l) -> p (g b) l", l=LAG)[:, :, 0:w]
                    if lag >= 2:
                        dve.wait_ge(lag_bc, lag - 1)
                    if lag == 0:
                        dve.tensor_tensor(lp, q, k, ALU.mult).then_inc(lag_p, 2)
                    else:
                        dve.tensor_tensor(lp, q, k, ALU.mult).then_inc(lag_p, 1)
                        dve.wait_ge(lag_p, 2 * lag + 1)
                        dve.wait_ge(lag_exp, lag)
                        le = LE[lag % 2].rearrange("p g t -> p (g t)")[:, 0:48 * w].rearrange("p (b l) -> p b l", l=w)
                        dve.tensor_tensor(lp, lp, le, ALU.mult).then_inc(lag_p, 1)
                if lag:
                    d = lag - 1
                    w = LAG - d
                    dve.wait_ge(lag_bc, d + 1)
                    if d >= 2:
                        dve.wait_ge(lag_acc, d - 1)
                    got = two_banks(2 * (d % 2), T)[:, :, 0:LAG * w].rearrange("p o (b l) -> p o b l", l=w)
                    tmp = LTMP[d % 2][:, :, 0:LAG * w].rearrange("p o (b l) -> p o b l", l=w)
                    v = V4.rearrange("p o (b l) -> p o b l", l=LAG)[:, :, :, 0:w]
                    dve.tensor_tensor(tmp, got, v, ALU.mult).then_inc(lag_tmp, 1)

        def gated_pool(pool):
            pool.wait_ge(lv_qk, 2 * len(LEVELS))
            for d in range(1, LAG + 2):
                if d < LAG:
                    w = LAG - d
                    le = LE[d % 2].rearrange("p g t -> p (g t)")[:, 0:48 * w].rearrange("p (b l) -> p b l", l=w)
                    c = C3.rearrange("p g (b l) -> p (g b) l", l=LAG)
                    if d >= 3:
                        pool.wait_ge(lag_p, 2 * (d - 2) + 2)
                    pool.tensor_tensor(le, c[:, :, d:LAG], c[:, :, 0:w], ALU.subtract).then_inc(lag_diff, 1)
                if d >= 2:
                    e = d - 2
                    w = LAG - e
                    tmp = LTMP[e % 2][:, :, 0:LAG * w].rearrange("p o (b l) -> p o b l", l=w)
                    acc = O4.rearrange("p o (b l) -> p o b l", l=LAG)[:, :, :, e:LAG]
                    pool.wait_ge(lag_tmp, e + 1)
                    if e:
                        pool.wait_ge(lag_acc, e)
                    pool.tensor_tensor(acc, acc, tmp, ALU.add).then_inc(lag_acc, 1)

        def gated_act(act):
            o = order(act, "gat_act")
            need(act, "gdn_dve", "out")
            need(act, "gat_pe", "gk")
            o(act.activation(U3[:, 0, :], psum[:, 0, 0:T], ACT.Identity, bias=col("gk_bias")), "u")
            need(act, "gat_dve", "u")
            o(act.activation(E3, U3, ACT.Abs))
            o(act.activation(E3, E3, ACT.Exp, scale=-1.0))
            o(act.activation(E3, E3, ACT.Ln, bias=1.0), "ln")
            o(act.activation(K3[:, 1:3, :], K3[:, 1:3, :], ACT.Sigmoid, scale=-1.0), "key")
            for i, L in enumerate(LEVELS):
                act.wait_ge(lv_cum, 8 + 2 * i + 2)
                act.activation(halves_of(E3, L, 0), halves_of(E3, L, 0), ACT.Exp).then_inc(lv_exp, 1)
                if i:
                    act.wait_ge(lv_qk, 2 * i)
                act.activation(halves_of(E3, L, 1), halves_of(C3, L, 1), ACT.Exp).then_inc(lv_exp, 1)
            act.wait_ge(lv_pe, len(LEVELS))
            for j in range(4):
                act.activation(A8[:, j, :], psum[:, j, 0:T + P], ACT.Copy).then_inc(copied, 1)
            for d in range(1, LAG):
                w = LAG - d
                le = LE[d % 2].rearrange("p g t -> p (g t)")[:, 0:48 * w]
                act.wait_ge(lag_diff, d)
                act.activation(le, le, ACT.Exp).then_inc(lag_exp, 1)

        def gated_pe(pe):
            o = order(pe, "gat_pe")
            need(pe, "gdn_dve", "out")
            o(pe.matmul(psum[:, 0, 0:T], gk_up[64:80, :], zs[64:80, :], start=True, stop=True), "gk")
            for b, tile in ((1, CV), (2, DI)):
                for n in range(2):
                    for i in range(2):
                        mm = pe.transpose(psum[:, b, n * T + i * P:n * T + (i + 1) * P], z[:, tile + i, n * P:(n + 1) * P], ident[:, :])
            o(mm, "tok")
            need(pe, "gat_dve", "tok")
            need(pe, "gat_act", "u")
            for j in range(8):
                mm = pe.matmul(psum[:, j, 0:T + P], zeros[:, 0:P], zeros[:, 0:T + P], start=True, stop=False, skip_group_check=True)
            o(mm, "zero")
            heads8 = [(j, 0, slice(32 * j, 32 * j + 32)) if j < 4 else (j, 1 + (j - 4) // 2, slice(HD * (j % 2), HD * (j % 2) + HD))
                      for j in range(8)]
            for i, L in enumerate(LEVELS):
                pe.wait_ge(lv_qk, 2 * i + 2)
                for j, tile, r in heads8:
                    for s0 in range(0, T, 2 * L):
                        st, at = s0 // P, s0 % P
                        c = s0 + L + (P if st else 0)
                        mm = pe.matmul(psum[at:at + L, j, c:c + L], QK[i % 2][r, tile, s0:s0 + L], QK[i % 2][r, tile, s0 + L:s0 + 2 * L],
                                       start=False, stop=(i == len(LEVELS) - 1), skip_group_check=True)
                mm.then_inc(lv_pe, 1)
            pe.wait_ge(copied, 8)
            for j in range(8):
                tok, f = toks[j // 4], slice((j % 4) * HD, (j % 4) * HD + HD)
                r, out = slice(HD * (j % 2), HD * (j % 2) + HD), two_banks(0, T)[:, j // 2, :]
                pe.matmul(out[r, :], tok[:, 0, f], A8[:, j, 0:T], start=True, stop=False, skip_group_check=True)
                mm = pe.matmul(out[r, P:T], tok[:, 1, f], A8[:, j, T:T + P], start=False, stop=True, skip_group_check=True)
            o(mm, "out")
            need(pe, "gat_dve", "out")
            for d in range(LAG):
                w = LAG - d
                pe.wait_ge(lag_p, 2 * d + 2)
                if d >= 2:
                    pe.wait_ge(lag_tmp, d - 1)
                lp = QK[d % 2].rearrange("p g t -> p (g t)")
                for out in range(4):
                    tile, sel = (0, lagsel[:, out, :]) if out < 2 else (out - 1, headones[:, :])
                    mm = pe.matmul(two_banks(2 * (d % 2), T)[:, out, 0:LAG * w], sel, lp[:, tile * LAG * w:(tile + 1) * LAG * w],
                                   start=True, stop=True, skip_group_check=True)
                mm.then_inc(lag_bc, 1)

        post_hi, post_lo = sem("mixed_hi"), sem("mixed_lo")
        OSQ, OSUM, OTMP = (area(i * 2048, 8, T) for i in range(3))

        def post_act(act):
            o = order(act, "post_act")
            act.wait_ge(lag_acc, LAG)
            o(act.activation(OSQ, z[:, 0:8, :], ACT.Square), "squares")
            need(act, "post_dve", "mean")
            o(act.activation(OSQ, OSUM, ACT.Abs_reciprocal_sqrt), "rsqrt")
            need(act, "post_dve", "scaled")
            act.activation(xn_hi[:, :, X], z[:, 0:8, :], ACT.Copy).then_inc(post_hi, 1)

        def post_pe(pe):
            o = order(pe, "post_pe")
            need(pe, "post_act", "squares")
            for i in range(4):
                mm = pe.matmul(bank(4 + i), headones[:, :], OSQ[:, 2 * i:2 * i + 2, :], start=True, stop=True)
            o(mm, "sums")

        def post_dve(dve):
            o = order(dve, "post_dve")
            need(dve, "post_pe", "sums")
            o(dve.tensor_scalar(OSUM, psum[:, 4:8, :].rearrange("p b (n t) -> p (b n) t", t=T), 1.0 / HD, EPS, ALU.mult, ALU.add), "mean")
            need(dve, "post_act", "rsqrt")
            newton(dve, o, OSQ, OSUM, OTMP, "unit")
            for k in range(8):
                o(dve.scalar_tensor_tensor(z[:, k, :], z[:, k, :], col("head_gain", k), z[:, RG + k, :], ALU.mult, ALU.mult))
            o(dve.tensor_tensor(z[:, 0:8, :], z[:, 0:8, :], OSQ, ALU.mult), "scaled")
            dve.wait_ge(post_hi, 1)
            dve.tensor_tensor(xn_lo[:, :, X], z[:, 0:8, :], xn_hi[:, :, X].bitcast(F32), ALU.subtract).then_inc(post_lo, 1)

        at_scores, at_max, at_exp, at_norm, at_turn, at_pt, at_out, at_hi, at_lo, at_self = (sem(x) for x in (
            "att_scores", "att_max", "att_probs", "att_scaled", "att_turned", "att_turned_out", "att_out", "att_hi",
            "att_lo", "att_small"))
        at_col = small[:, cols["att"]:cols["att"] + 8]
        PROB = [work[:, i * 512:(i + 1) * 512] for i in range(2)]
        PT = [area(1024 + i * 1024, 4, T) for i in range(2)]

        class Attention:
            units, heads_before = 0, 0

            def __init__(self, heads, parts, keys, q, k, v):
                self.heads, self.parts, self.keys, self.q, self.k, self.v = heads, parts, keys, q, k, v
                self.scale = (parts * P) ** -0.5
                self.u0, self.h0 = Attention.units, Attention.heads_before
                Attention.units += 2 * heads
                Attention.heads_before += heads

            def pe(self, pe):
                key_tiles = self.keys // P

                def scores(u):
                    h, tt = u // 2, u % 2
                    if u >= 2:
                        pe.wait_ge(at_exp, self.u0 + u - 1)
                    for i in range(self.parts):
                        mm = pe.matmul(psum[:, u % 2, 0:self.keys], self.q(h, i)[:, tt * P:(tt + 1) * P], self.k(h, i),
                                       start=(i == 0), stop=(i == self.parts - 1))
                    mm.then_inc(at_scores, 1)

                scores(0)
                for u in range(2 * self.heads):
                    h, tt = u // 2, u % 2
                    if u + 1 < 2 * self.heads:
                        scores(u + 1)
                    pe.wait_ge(at_norm, self.u0 + u + 1)
                    if u >= 2:
                        pe.wait_ge(at_pt, self.u0 + u - 1)
                    for j in range(key_tiles):
                        mm = pe.transpose(psum[:, 2 + u % 2, j * P:(j + 1) * P], PROB[u % 2][:, j * P:(j + 1) * P], ident[:, :])
                    mm.then_inc(at_turn, 1)
                    if tt:
                        pe.wait_ge(at_pt, self.u0 + u + 1)
                        if h >= 2:
                            pe.wait_ge(at_lo, self.h0 + h - 1)
                        for i in range(self.parts):
                            for j in range(key_tiles):
                                mm = pe.matmul(psum[:, 4 + h % 2, i * T:(i + 1) * T], self.v(h, j)[:, i * P:(i + 1) * P],
                                               PT[h % 2][:, j, :], start=(j == 0), stop=(j == key_tiles - 1))
                        mm.then_inc(at_out, 1)

            def act(self, act):
                def turned(u):
                    h, tt = u // 2, u % 2
                    act.wait_ge(at_turn, self.u0 + u + 1)
                    if h >= 2 and tt == 0:
                        act.wait_ge(at_out, self.h0 + h - 1)
                    act.activation(PT[h % 2][:, 0:self.keys // P, tt * P:(tt + 1) * P],
                                   psum[:, 2 + u % 2, 0:self.keys].rearrange("p (j t) -> p j t", t=P), ACT.Copy).then_inc(at_pt, 1)

                def out_hi(h):
                    act.wait_ge(at_out, self.h0 + h + 1)
                    act.activation(xn_hi[:, self.parts * h:self.parts * (h + 1), X],
                                   psum[:, 4 + h % 2, 0:self.parts * T].rearrange("p (i t) -> p i t", t=T), ACT.Copy).then_inc(at_hi, 1)

                for u in range(2 * self.heads):
                    act.wait_ge(at_max, self.u0 + u + 1)
                    if u >= 2:
                        act.wait_ge(at_turn, self.u0 + u - 1)
                    act.activation(PROB[u % 2][:, 0:self.keys], psum[:, u % 2, 0:self.keys], ACT.Exp, scale=self.scale,
                                   bias=at_col[:, u % 2:u % 2 + 1], accum_out=at_col[:, 2 + u % 2:3 + u % 2]).then_inc(at_exp, 1)
                    if u:
                        turned(u - 1)
                    if u >= 3 and u % 2:
                        out_hi((u - 3) // 2)
                turned(2 * self.heads - 1)
                out_hi(self.heads - 1)

            def dve(self, dve):
                def out_lo(h):
                    dve.wait_ge(at_hi, self.h0 + h + 1)
                    o = xn_hi[:, self.parts * h:self.parts * (h + 1), X].bitcast(F32)
                    dve.tensor_tensor(xn_lo[:, self.parts * h:self.parts * (h + 1), X],
                                      psum[:, 4 + h % 2, 0:self.parts * T].rearrange("p (i t) -> p i t", t=T), o,
                                      ALU.subtract).then_inc(at_lo, 1)

                for u in range(2 * self.heads):
                    n = 2 * (self.u0 + u)
                    dve.wait_ge(at_scores, self.u0 + u + 1)
                    top, bias = at_col[:, 4:5], at_col[:, u % 2:u % 2 + 1]
                    dve.tensor_reduce(top, psum[:, u % 2, 0:self.keys], AX_X, ALU.max).then_inc(at_self, 1)
                    dve.wait_ge(at_self, n + 1)
                    dve.tensor_scalar(bias, top, -self.scale, None, ALU.mult).then_inc(at_max, 1)
                    dve.wait_ge(at_exp, self.u0 + u + 1)
                    dve.reciprocal(at_col[:, 5:6], at_col[:, 2 + u % 2:3 + u % 2]).then_inc(at_self, 1)
                    dve.wait_ge(at_self, n + 2)
                    dve.tensor_scalar(PROB[u % 2][:, 0:self.keys], PROB[u % 2][:, 0:self.keys], at_col[:, 5:6], None, ALU.mult).then_inc(at_norm, 1)
                    if u >= 3 and u % 2:
                        out_lo((u - 3) // 2)
                out_lo(self.heads - 1)

        def run_act(act, job, evac, splits=True, counts=False):
            for s in steps(act, job, 2):
                if splits or s.is_mod:
                    split_hi(act, s)
                if counts:
                    act.wait_ge(evacuated, job.base)
                if s.is_mod and counts:
                    mod_rows(act, s, lambda out, got: act.activation(out, got, ACT.Copy))
                elif evac is not None and not s.is_mod:
                    evac(s)

        def run_dve(dve, job, evac, splits=True):
            for s in steps(dve, job, 2):
                if splits or s.is_mod:
                    split_lo(dve, s)
                if evac is not None:
                    dve.wait_ge(evacuated, job.base)
                if s.is_mod and evac is not None:
                    mod_rows(dve, s, dve.tensor_copy)
                elif evac is not None and not s.is_mod:
                    evac(s)

        def pairs_of(s, dst, w=2):
            at = s.c * w
            return dst[:, bass.ds(at, w), :] if s.looped else dst[:, at:at + w, :]

        def act_copy_to(act, dst, func=ACT.Copy, w=T):
            def evac(s):
                act.wait_ge(chunk_done, s.g + 1)
                act.activation(pairs_of(s, dst), psum[:, s.bank:s.bank + 2, 0:w], func).then_inc(evacuated, 1)
            return evac

        def act_tokens_to(act, dst, func=ACT.Copy):
            tiles = dst.shape[1]

            def evac(s):
                act.wait_ge(chunk_done, s.g + 1)
                at = s.c * 256
                out = dst[:, :, bass.ds(at, 256)] if s.looped else dst[:, :, at:at + 256]
                got = psum[:, s.bank:s.bank + 2, :].rearrange("p b (n f) -> p (b n) f", f=256)[:, 0:tiles, :]
                act.activation(out, got, func).then_inc(evacuated, 1)
            return evac

        def dve_add_gated(dve, tiles, gate, halves):
            def evac(s):
                dve.wait_ge(chunk_done, s.g + 1)
                for n in range(tiles):
                    k = s.c * tiles + n
                    tile = bass.ds(k, 1) if s.looped else slice(k, k + 1)
                    for h in range(halves):
                        t = slice(h * T, (h + 1) * T)
                        x, got = xc[:, tile, t], psum[:, s.bank + n:s.bank + n + 1, t]
                        if gate is None:
                            mm = dve.tensor_tensor(x, x, got, ALU.add)
                        else:
                            mm = dve.scalar_tensor_tensor(x, got, gate[:, tile, h], x, ALU.mult, ALU.add)
                mm.then_inc(evacuated, 1)
            return evac

        ff_gate, ff_hi, ff_lo, ff_conv, ff_tap = (sem(x) for x in (
            "ff_gate", "ff_hi", "ff_lo", "ff_convolved", "ff_newest_tap"))
        later = ExitStack()
        mix.close()
        h_hi = sb("h_hi", [P, HALF, 2 * T], F32R, scope=later)
        h_lo = sb("h_lo", [P, HALF, 2 * T], F32R, scope=later)
        fbuf = [work[:, 4096 + i * 1024:4096 + (i + 1) * 1024].rearrange("p (n t) -> p n t", n=2) for i in range(SLOTS)]

        class Feed:
            chunks = 0

            def __init__(self, name, norm, w, gate, conv=None):
                self.name, self.norm, self.w, self.gate, self.conv = name, norm, w, gate, conv
                self.bases = [Feed.chunks, Feed.chunks + HALF]
                Feed.chunks += FF_TILES

            def pe(self, pe):
                for half in range(2):
                    base = self.bases[half]
                    up, down = jobs[f"{self.name}_up{half}"], jobs[f"{self.name}_down{half}"]

                    def norm_k(s, k):
                        if s.looped and s.u == 0 or s.static == 0:
                            self.norm.ready(pe, k)

                    pe_feature_major(pe, up, xn_hi, xn_lo, slice(0, self.w), before_k=norm_k if half == 0 else None)
                    if up is jobs["b1_up1"]:
                        mod_last_turn(pe)

                    def hidden_k(s, k):
                        if (s.looped and s.u == 0 or s.static == 0) and k in (0, HALF - 1):
                            pe.wait_ge(ff_lo, base + (HALF - 1 if k == 0 else HALF))

                    pe_feature_major(pe, down, h_hi, h_lo, slice(0, self.w), n_tiles=1, k_tiles=HALF, before_k=hidden_k)

            def act(self, act, then):
                for half in range(2):
                    base, job = self.bases[half], jobs[f"{self.name}_up{half}"]

                    def evac(s):
                        b = fbuf[s.slot]
                        n = s.c + base
                        act.wait_ge(chunk_done, s.g + 1)
                        if s.looped or n >= 2:
                            act.wait_ge(ff_lo, n - 1)
                        if self.conv is None:
                            act.activation(b[:, 0, 0:self.w], psum[:, s.bank, 0:self.w], ACT.Silu).then_inc(ff_gate, 1)
                        else:
                            k = s.c + half * HALF
                            for i in range(2):
                                tap = small[:, bass.ds(k + (cols["ff_conv2"] + i * FF_TILES), 1)] if s.looped else col("ff_conv2", k + i * FF_TILES)
                                mm = act.activation(b[:, i, 0:T], psum[:, s.bank + i, 0:T], ACT.Copy, scale=tap)
                            mm.then_inc(ff_tap, 1)
                            split_hi(act, s)
                            act.wait_ge(ff_conv, n * 2 + 2)
                            act.activation(b[:, 0, 0:T], b[:, 0, 0:T], ACT.Silu).then_inc(ff_gate, 1)
                        act.wait_ge(evacuated, s.g + 1)
                        out = h_hi[:, bass.ds(s.c, 1), 0:self.w] if s.looped else h_hi[:, s.c:s.c + 1, 0:self.w]
                        act.activation(out, b[:, 1:2, 0:self.w], ACT.Copy).then_inc(ff_hi, 1)

                    run_act(act, job, evac, splits=self.conv is None)
                    run_act(act, jobs[f"{self.name}_down{half}"], then.act_squares_after(act) if half else None)

            def dve(self, dve):
                for half in range(2):
                    base, job = self.bases[half], jobs[f"{self.name}_up{half}"]

                    def evac(s):
                        b = fbuf[s.slot]
                        n = s.c + base
                        if self.conv is not None:
                            dve.wait_ge(ff_tap, n + 1)
                            k = s.c + half * HALF
                            for back in (1, 2):
                                for i in range(2):
                                    name = f"ff_conv{2 - back}"
                                    tap = small[:, bass.ds(k + (cols[name] + i * FF_TILES), 1)] if s.looped else col(name, k + i * FF_TILES)
                                    mm = dve.scalar_tensor_tensor(b[:, i, back:T], psum[:, s.bank + i, 0:T - back], tap, b[:, i, back:T],
                                                                  ALU.mult, ALU.add)
                                mm.then_inc(ff_conv, 1)
                                dve.wait_ge(ff_conv, n * 2 + back)
                            up = b[:, 1, 0:T]
                            split_lo(dve, s)
                        else:
                            up = psum[:, s.bank + 1, 0:self.w]
                        dve.wait_ge(ff_gate, n + 1)
                        dve.tensor_tensor(b[:, 1, 0:self.w], b[:, 0, 0:self.w], up, ALU.mult).then_inc(evacuated, 1)

                    run_dve(dve, job, evac, splits=self.conv is None)
                    run_dve(dve, jobs[f"{self.name}_down{half}"], dve_add_gated(dve, 1, self.gate, self.w // T))

            def pool(self, pool):
                for half in range(2):
                    base, job = self.bases[half], jobs[f"{self.name}_up{half}"]
                    for s in steps(pool, job, 2):
                        if s.is_mod:
                            continue
                        n = s.c + base
                        b = fbuf[s.slot]
                        pool.wait_ge(ff_hi, n + 1)
                        lo = h_lo[:, bass.ds(s.c, 1), 0:self.w] if s.looped else h_lo[:, s.c:s.c + 1, 0:self.w]
                        hi = h_hi[:, bass.ds(s.c, 1), 0:self.w] if s.looped else h_hi[:, s.c:s.c + 1, 0:self.w]
                        pool.tensor_tensor(lo, b[:, 1:2, 0:self.w], hi.bitcast(F32), ALU.subtract).then_inc(ff_lo, 1)
        mrow = work[:, 7680:7936]
        mod_act, mod_dve, mod_turned = sem("mod_inputs"), sem("mod_prepared"), sem("mod_turned")
        MOD_TAKEN = (17, 37, 59, 72)

        def mod_turn(pe, m):
            at = m * 4
            for n in range(2):
                out = psum[:, 7, bass.ds(at + n * 2, 2)] if not isinstance(at, int) else psum[:, 7, at + n * 2:at + n * 2 + 2]
                mm = pe.matmul(out, mrow[:, n * P:(n + 1) * P], row_sums[:, :], start=True, stop=True)
            mm.then_inc(mod_turned, 1)

        def mod_pe(pe, s):
            if s.looped or s.m > 0:
                pe.wait_ge(evacuated, s.g - 1)
                mod_turn(pe, s.m - 1)
            else:
                pe.wait_ge(mod_dve, 2)
            pe.wait_ge(lo_ready, s.g + 1)
            for k in range(KT):
                w = slice(k * 256, (k + 1) * 256)
                pe.matmul(psum[0:4, s.bank, 0:256], c4[:, k, :], w_hi[:, s.slot, w], start=(k == 0), stop=False)
                mm = pe.matmul(psum[0:4, s.bank, 0:256], c4[:, k, :], w_lo[:, s.slot, w], start=False, stop=(k == KT - 1))
            mm.then_inc(chunk_done, 1)

        def mod_last_turn(pe):
            pe.wait_ge(evacuated, jobs["b1_up1"].base + jobs["b1_up1"].n)
            mod_turn(pe, mod_chunks - 1)

        def mod_rows(eng, s, copy):
            eng.wait_ge(chunk_done, s.g + 1)
            if s.looped or s.m > 0:
                eng.wait_ge(mod_turned, s.m)
            copy(mrow[0:4, :], psum[0:4, s.bank, 0:256]).then_inc(evacuated, 1)

        def mod_scalar(act):
            act.wait_ge(start_in, 16 * len(START))
            act.activation(c_in[:, :, :], c_in[:, :, :], ACT.Silu).then_inc(mod_act, 1)
            act.wait_ge(mod_act, 1)
            act.activation(c4[:, :, :].rearrange("p k (w l) -> p k w l", l=2)[:, :, :, 0], c_in[:, :, :], ACT.Copy).then_inc(mod_act, 1)

        def mod_vector(dve):
            dve.memset(mrow, 0.0).then_inc(mod_dve, 1)
            dve.wait_ge(mod_act, 2)
            hl = c4[:, :, :].rearrange("p k (w l) -> p k w l", l=2)
            dve.tensor_tensor(hl[:, :, :, 1], c_in[:, :, :], hl[:, :, :, 0].bitcast(F32), ALU.subtract).then_inc(mod_dve, 1)

        mod_ready = [0]

        def mod_columns(dve, feed, norms):
            if feed == 0:
                mod_ready[0] = 2
            m0, m1 = (0,) + MOD_TAKEN[:-1], MOD_TAKEN
            a, b = m0[feed], m1[feed]
            dve.wait_ge(mod_turned, b)
            dve.tensor_tensor(mods[:, 2 * a:2 * b, :], psum[:, 7, 4 * a:4 * b].rearrange("p (n w) -> p n w", w=2),
                              b_mod[:, 2 * a:2 * b].unsqueeze(2).to_broadcast([P, 2 * (b - a), 2]), ALU.add).then_inc(mod_dve, 1)
            mod_ready[0] += 1
            dve.wait_ge(mod_dve, mod_ready[0])
            for ln in norms:
                at = (ln // 3) * 72 + (ln % 3) * 24
                dve.scalar_tensor_tensor(scales[:, ln, :, :], mods[:, at + 8:at + 16, :], 1.0,
                                         gains[:, ln, :].unsqueeze(2).to_broadcast([P, KT, 2]), ALU.add, ALU.mult).then_inc(mod_dve, 1)
                mod_ready[0] += 1
                if ln % 3 != 1:
                    dve.tensor_scalar(mods[:, at + 16:at + 24, :], mods[:, at + 16:at + 24, :], 0.5, None, ALU.mult).then_inc(mod_dve, 1)
                    mod_ready[0] += 1
            dve.wait_ge(mod_dve, mod_ready[0])

        def modulated(ln, span, tiles=1):
            at = (ln // 3) * 72 + (ln % 3) * 24
            return Norm(span, lambda k, h: scales[:, ln, k, h:h + 1], lambda k, h: mods[:, at + k, h:h + 1], tiles=tiles)

        def gate_of(ln):
            at = (ln // 3) * 72 + (ln % 3) * 24 + 16
            return mods[:, at:at + KT, :]

        later.close()
        l0 = ExitStack()
        a_t, u_t, v_t = (sb(n, [P, 4, 2 * T], scope=l0) for n in ("a_t", "u_t", "v_t"))
        dft_c = sb("dft_c", [P, 2 * P], scope=l0)
        dft_cos = sb("dft_cos", [P, 2, T], scope=l0)
        dft_sin = sb("dft_sin", [P, 2, T], scope=l0)
        ws_t = sb("ws_t", [P, 4, P], scope=l0)
        bs_row = sb("bs_row", [P, 4, P], scope=l0)
        gv_row = sb("gv_row", [P, 4, P], scope=l0)
        L0_TABLES = dict(dft_c=dft_c, dft_cos=dft_cos, dft_sin=dft_sin, ws_t=ws_t, bs_row=bs_row, gv_row=gv_row)
        o_t = area(0, KT, 2 * T)
        mid = [area(4096 + i * 512, 2, T) for i in range(2)]
        vsq = work[:, 5120:7168].rearrange("p (n f) -> p n f", f=P)
        vst = work[:, 7168:7184]
        vst2, vst3 = work[:, 7184:7200], work[:, 7200:7216]
        l0_tables_in, f_mid, f_mid_out, f_sum, f_sum_out, g_dve, g_act, g_pe, o_hi, o_lo = (sem(x) for x in (
            "l0_tables_in", "fourier_channels", "fourier_channels_out", "fourier_tokens", "fourier_tokens_out", "gating_dve",
            "gating_rsqrt", "gating_mixed", "branch_hi", "branch_lo"))

        def branch_pe(pe, norm):
            def norm_k(s, k):
                if s.c == 0:
                    norm.ready(pe, k)
            pe_feature_major(pe, jobs["ab_a"], xn_hi, xn_lo, XC, before_k=norm_k)
            pe_feature_major(pe, jobs["ab_u"], xn_hi, xn_lo, XC)
            pe_token_major(pe, jobs["ab_v"], XC)
            pe.wait_ge(evacuated, jobs["ab_v"].base + 2)
            pe.wait_ge(l0_tables_in, 16 * len(L0_TABLES))

            def channels(j):
                q, g = j // 4, j % 4
                if j >= 2:
                    pe.wait_ge(f_mid_out, j - 1)
                for nt in range(2):
                    mm = pe.matmul(psum[:, j % 2, nt * T:(nt + 1) * T], a_t[:, g, q * T + nt * P:q * T + (nt + 1) * P], dft_c[:, :],
                                   start=True, stop=True)
                mm.then_inc(f_mid, 1)

            channels(0)
            for j in range(8):
                if j + 1 < 8:
                    channels(j + 1)
                pe.wait_ge(f_mid_out, j + 1)
                if j >= 2:
                    pe.wait_ge(f_sum_out, j - 1)
                for nt in range(2):
                    pe.matmul(psum[:, 2 + j % 2, 0:T], mid[j % 2][:, nt, 0:P], dft_cos[:, nt, :], start=(nt == 0), stop=False)
                    mm = pe.matmul(psum[:, 2 + j % 2, 0:T], mid[j % 2][:, nt, P:T], dft_sin[:, nt, :], start=False, stop=(nt == 1))
                mm.then_inc(f_sum, 1)
            pe.wait_ge(g_dve, 8)
            for tt in range(4):
                for g in range(4):
                    mm = pe.matmul(psum[:, 4 + g, tt * P:(tt + 1) * P], v_t[:, tt, g * P:(g + 1) * P], ws_t[:, g, :], start=True, stop=True)
            mm.then_inc(g_pe, 1)
            pe.wait_ge(o_lo, 2)
            pe_feature_major(pe, jobs["ab_out"], xn_hi, xn_lo, XC)

        def branch_act(act, norm, then):
            for name in L0_TABLES:
                act.dma_start(L0_TABLES[name][:], io[name]).then_inc(l0_tables_in, 16)
            norm.act_rest(act)
            run_act(act, jobs["ab_a"], act_copy_to(act, a_t, w=2 * T), counts=True)
            run_act(act, jobs["ab_u"], act_copy_to(act, u_t, ACT.Gelu_apprx_tanh, w=2 * T), counts=True)
            run_act(act, jobs["ab_v"], act_tokens_to(act, v_t, ACT.Gelu_apprx_tanh), counts=True)
            act.wait_ge(g_dve, 3)
            act.activation(vst2, vst, ACT.Abs_reciprocal_sqrt).then_inc(g_act, 1)
            for j in range(8):
                act.wait_ge(f_mid, j + 1)
                if j >= 2:
                    act.wait_ge(f_sum, j - 1)
                act.activation(mid[j % 2], psum[:, j % 2, :].rearrange("p (n t) -> p n t", n=2), ACT.Copy).then_inc(f_mid_out, 1)
            act.wait_ge(f_sum_out, 8)
            act.activation(xn_hi[:, 0:4, :], o_t[:, 0:4, :], ACT.Copy).then_inc(o_hi, 1)
            act.wait_ge(g_dve, 10)
            act.activation(xn_hi[:, 4:8, :], o_t[:, 4:8, :], ACT.Copy).then_inc(o_hi, 1)
            run_act(act, jobs["ab_out"], then.act_squares_after(act))

        def branch_dve(dve, norm):
            norm.dve(dve)
            for name in ("ab_a", "ab_u", "ab_v"):
                run_dve(dve, jobs[name], None)
            n = 0

            def o(ins):
                nonlocal n
                n += 1
                ins.then_inc(g_dve, 1)
                dve.wait_ge(g_dve, n)
            v = v_t[:, :, :].rearrange("p n (g f) -> p (n g) f", f=P)
            dve.wait_ge(evacuated, jobs["ab_v"].base + 2)
            dve.wait_ge(l0_tables_in, 16 * len(L0_TABLES))
            o(dve.tensor_tensor(vsq, v, v, ALU.mult))
            o(dve.tensor_reduce(vst3, vsq, AX_X, ALU.add))
            o(dve.tensor_scalar(vst, vst3, 1.0 / P, EPS, ALU.mult, ALU.add))
            dve.wait_ge(g_act, 1)
            o(dve.scalar_tensor_tensor(vst3, vst2, -0.5, vst2, ALU.mult, ALU.mult))
            o(dve.tensor_tensor(vst3, vst3, vst, ALU.mult))
            o(dve.scalar_tensor_tensor(vst2, vst3, 1.5, vst2, ALU.add, ALU.mult))
            o(dve.tensor_tensor(v, v, vst2.unsqueeze(2).to_broadcast([P, 16, P]), ALU.mult))
            gv = gv_row[:, :, :].unsqueeze(1).to_broadcast([P, 4, 4, P])
            v4 = v_t[:, :, :].rearrange("p n (g f) -> p n g f", f=P)
            o(dve.tensor_tensor(v4, v4, gv, ALU.mult))
            for j in range(8):
                dve.wait_ge(f_sum, j + 1)
                dve.tensor_copy(o_t[:, j % 4, (j // 4) * T:(j // 4 + 1) * T], psum[:, 2 + j % 2, 0:T]).then_inc(f_sum_out, 1)
            dve.wait_ge(g_pe, 1)
            gated = o_t[:, 4:8, :].rearrange("p g (n t) -> p g n t", t=P)
            bs = bs_row[:, :, :].unsqueeze(2).to_broadcast([P, 4, 4, P])
            o(dve.tensor_tensor(gated, psum[:, 4:8, :].rearrange("p g (n t) -> p g n t", t=P), bs, ALU.add))
            o(dve.tensor_tensor(o_t[:, 4:8, :], o_t[:, 4:8, :], u_t[:, :, :], ALU.mult))
            for i in range(2):
                dve.wait_ge(o_hi, i + 1)
                k = slice(4 * i, 4 * i + 4)
                dve.tensor_tensor(xn_lo[:, k, :], o_t[:, k, :], xn_hi[:, k, :].bitcast(F32), ALU.subtract).then_inc(o_lo, 1)
            run_dve(dve, jobs["ab_out"], dve_add_gated(dve, 2, gate_of(1), 2))

        l0.close()
        l1 = ctx.enter_context(ExitStack())
        qk12 = sb("qk12", [P, 12, T], scope=l1)
        qk_tmp = sb("qk_tmp", [P, 12, T], scope=l1)
        v2 = sb("v2", [P, 4, T], scope=l1)
        ax_cos, ax_sin = sb("ax_cos", [P, T], scope=l1), sb("ax_sin", [P, T], scope=l1)
        ax_in, r_act, r_dve, r_pe = sem("axial_in"), sem("rope_act"), sem("rope_dve"), sem("rope_pe")
        qk_mean, qk_rstd = work[:, 0:12 * T].rearrange("p (n t) -> p n t", t=T), work[:, 12 * T:24 * T].rearrange("p (n t) -> p n t", t=T)
        kx = qk12[:, 8:12, :].rearrange("p (h w) t -> p h w t", w=2)[:, :, 0, :]
        k_all = qk12[:, 8:12, :].rearrange("p (h w) t -> p h (w t)", w=2)

        first = Norm(X, lambda k, h: col("mix_norm_w", k))
        memory = Norm(C, lambda k, h: col("mem_norm_w", k), tiles=2)
        cross = Norm(X, lambda k, h: col("xattn_norm_w", k), tiles=2)
        ffn = Norm(X, lambda k, h: col("ffn_norm_w", k), tiles=2)
        between = Norm(X, lambda k, h: col("final_norm_w", k), out=xc[:, :, X])
        n20, n21 = modulated(0, XC), modulated(1, XC)
        n22, n23, n24 = modulated(2, XC, 2), modulated(3, XC), modulated(4, XC)
        n25 = modulated(5, X, 2)
        last = Norm(X, lambda k, h: col("g_final", k), out=nrm)
        feed0 = Feed("ffn", ffn, T, None, conv=True)
        feed1 = Feed("a1", n20, 2 * T, gate_of(0))
        feed2 = Feed("a2", n22, 2 * T, gate_of(2))
        feed3 = Feed("b1", n23, 2 * T, gate_of(3))
        feed4 = Feed("b2", n25, T, gate_of(5))
        k1, v1, q1 = z[:, 0:8, :], z[:, 8:16, :].rearrange("p (n a) t -> p n (a t)", n=2), z[:, 16:24, :]
        att1 = Attention(4, 2, T, lambda h, i: q1[:, 2 * h + i, :], lambda h, i: k1[:, 2 * h + i, :], lambda h, j: v1[:, j, h * T:(h + 1) * T])
        att2 = Attention(8, 1, 2 * T, lambda h, i: qk12[:, h, :], lambda h, i: k_all[:, h // 4, :], lambda h, j: v2[:, j, (h // 4) * P:(h // 4 + 1) * P])
        START = dict(small=small, ident=ident, ones=ones, rot=rot, row_sums=row_sums, gains=gains, b_mod=b_mod, c_in=c_in)
        residual_in, mem_in, ctx_in, out_in, set_up = sem("residual_in"), sem("mem_in"), sem("ctx_in"), sem("out_stored"), sem("constants_set")

        block = ctx.enter_context(nc.Block())

        @block.sync
        def _(sp):
            sp.dma_start(xc[:, :, X], io["x"]).then_inc(residual_in, 16)
            for name in START:
                sp.dma_start(START[name][:], io[name]).then_inc(start_in, 16)
            for n, (name, *_) in enumerate(plan):
                for s in steps(sp, jobs[name]):
                    load(sp, s)
                    if n == 0 and s.static == SLOTS - 1:
                        sp.dma_start(xc[:, :, C], io["mem"]).then_inc(mem_in, 16)
                if n == 0:
                    load_mixer_tables(sp)
            sp.wait_ge(n_scaled, last.scaled_base + KT)
            sp.dma_start(io["out"], nrm[:, :, X]).then_inc(out_in, 16)
            sp.wait_ge(out_in, 16)

        @block.tensor
        def _(pe):
            pe.wait_ge(start_in, 16 * len(START))
            pe.wait_ge(set_up, 2)
            first.pe(pe)
            first.ready(pe, KT - 1)
            pe_feature_major(pe, jobs["w_in_a"], xn_hi, xn_lo, X)
            memory.pe(pe)
            pe_feature_major(pe, jobs["w_in_g"], xn_hi, xn_lo, X)
            pe_feature_major(pe, jobs["w_in_small"], xn_hi, xn_lo, X, n_tiles=1)
            retention_pe(pe)
            delta_pe(pe)
            gated_pe(pe)
            post_pe(pe)
            pe.wait_ge(post_lo, 1)
            pe_feature_major(pe, jobs["w_out"], xn_hi, xn_lo, X)
            memory.ready(pe, KT - 1)
            pe_feature_major(pe, jobs["wk"], xn_hi, xn_lo, C)
            cross.pe(pe)
            pe_token_major(pe, jobs["wv"], C)
            cross.ready(pe, KT - 1)
            pe_feature_major(pe, jobs["wq"], xn_hi, xn_lo, X)
            pe.wait_ge(evacuated, jobs["wq"].base + jobs["wq"].n)
            att1.pe(pe)
            pe.wait_ge(at_lo, att1.heads)
            pe_feature_major(pe, jobs["wo"], xn_hi, xn_lo, X)
            ffn.pe(pe)
            feed0.pe(pe)
            between.pe(pe)
            n20.pe(pe)
            feed1.pe(pe)
            n21.pe(pe)
            branch_pe(pe, n21)
            n22.pe(pe)
            feed2.pe(pe)
            n23.pe(pe)
            feed3.pe(pe)
            n24.pe(pe)
            n24.ready(pe, KT - 1)
            pe_feature_major(pe, jobs["q2"], xn_hi, xn_lo, X)
            pe_feature_major(pe, jobs["k2"], xn_hi, xn_lo, XC)
            pe_token_major(pe, jobs["v2"], XC)
            pe.wait_ge(r_act, 1)
            for i in range(6):
                mm = pe.matmul(bank(i), ones[:, :], qk_tmp[:, 2 * i:2 * i + 2, :], start=True, stop=True)
            mm.then_inc(r_pe, 1)
            pe.wait_ge(r_dve, 6)
            for i in range(4):
                pe.matmul(bank(i), rot[:, :], qk12[:, 2 * i:2 * i + 2, :], start=True, stop=True)
            pe.matmul(bank(4), rot[:, :], kx, start=True, stop=True).then_inc(r_pe, 1)
            pe.wait_ge(r_dve, 11)
            att2.pe(pe)
            pe.wait_ge(at_lo, att1.heads + att2.heads)
            pe_feature_major(pe, jobs["wo2"], xn_hi, xn_lo, X)
            n25.pe(pe)
            feed4.pe(pe)
            last.pe(pe)

        @block.scalar
        def _(act):
            act.wait_ge(residual_in, 16)
            first.act_squares(act)
            first_splits(act, split_hi)
            first.act_rest(act)
            run_act(act, jobs["w_in_a"], act_copy_to(act, z), counts=True)
            act.wait_ge(mem_in, 16)
            memory.act_squares(act)
            memory.act_rest(act)
            act.wait_ge(n_scaled, memory.scaled_base + KT)
            act.dma_start(xc[:, :, C], io["ctx"]).then_inc(ctx_in, 16)
            run_act(act, jobs["w_in_g"], act_copy_to(act, z[:, RG:RG + 8, :], ACT.Silu), counts=True)

            def small_rows(s):
                act.wait_ge(chunk_done, s.g + 1)
                act.activation(zs[:, :], psum[:, s.bank, 0:T], ACT.Copy).then_inc(evacuated, 1)
            run_act(act, jobs["w_in_small"], small_rows, counts=True)
            mod_scalar(act)
            retention_act(act)
            delta_act(act)
            gated_act(act)
            post_act(act)
            run_act(act, jobs["w_out"], cross.act_squares_after(act))
            run_act(act, jobs["wk"], act_copy_to(act, k1), counts=True)
            cross.act_rest(act)
            run_act(act, jobs["wv"], act_tokens_to(act, v1), counts=True)
            run_act(act, jobs["wq"], act_copy_to(act, q1), counts=True)
            att1.act(act)
            run_act(act, jobs["wo"], ffn.act_squares_after(act))
            ffn.act_rest(act)
            feed0.act(act, between)
            between.act_rest(act)
            act.wait_ge(ctx_in, 16)
            act.wait_ge(n_scaled, between.scaled_base + KT)
            n20.act_squares(act)
            n20.act_rest(act)
            feed1.act(act, n21)
            branch_act(act, n21, n22)
            n22.act_rest(act)
            feed2.act(act, n23)
            n23.act_rest(act)
            feed3.act(act, n24)
            act.dma_start(ax_cos[:, :], io["ax_cos"]).then_inc(ax_in, 16)
            act.dma_start(ax_sin[:, :], io["ax_sin"]).then_inc(ax_in, 16)
            n24.act_rest(act)
            run_act(act, jobs["q2"], act_copy_to(act, qk12[:, 0:8, :]), counts=True)

            def keys(s):
                act.wait_ge(chunk_done, s.g + 1)
                act.activation(k_all, psum[:, s.bank:s.bank + 2, :], ACT.Copy).then_inc(evacuated, 1)
            run_act(act, jobs["k2"], keys, counts=True)
            run_act(act, jobs["v2"], act_tokens_to(act, v2), counts=True)
            act.wait_ge(evacuated, jobs["v2"].base + 1)
            act.activation(qk_tmp[:, :, :], qk12[:, :, :], ACT.Square).then_inc(r_act, 1)
            act.wait_ge(r_dve, 1)
            act.activation(qk_rstd, qk_mean, ACT.Abs_reciprocal_sqrt).then_inc(r_act, 1)
            act.wait_ge(r_dve, 11)
            att2.act(act)
            run_act(act, jobs["wo2"], n25.act_squares_after(act))
            n25.act_rest(act)
            feed4.act(act, last)
            last.act_rest(act)

        @block.vector
        def _(dve):
            dve.memset(zeros[:, :], 0.0).then_inc(set_up, 1)
            dve.memset(mean[:, :], 0.0).then_inc(set_up, 1)
            dve.wait_ge(set_up, 2)
            first_splits(dve, split_lo)
            dve.wait_ge(start_in, 16 * len(START))
            first.dve(dve)
            run_dve(dve, jobs["w_in_a"], None)
            memory.dve(dve)
            for name in ("w_in_g", "w_in_small"):
                run_dve(dve, jobs[name], None)
            retention_dve(dve)
            delta_dve(dve)
            gated_dve(dve)
            post_dve(dve)
            mod_vector(dve)
            run_dve(dve, jobs["w_out"], dve_add_gated(dve, 2, None, 1))
            run_dve(dve, jobs["wk"], None)
            cross.dve(dve)
            run_dve(dve, jobs["wv"], None)
            run_dve(dve, jobs["wq"], None)
            att1.dve(dve)
            run_dve(dve, jobs["wo"], dve_add_gated(dve, 2, None, 1))
            ffn.dve(dve)
            feed0.dve(dve)
            between.dve(dve)
            mod_columns(dve, 0, (0,))
            n20.dve(dve)
            feed1.dve(dve)
            mod_columns(dve, 1, (1, 2))
            branch_dve(dve, n21)
            n22.dve(dve)
            feed2.dve(dve)
            mod_columns(dve, 2, (3,))
            n23.dve(dve)
            feed3.dve(dve)
            mod_columns(dve, 3, (4, 5))
            n24.dve(dve)
            for name in ("q2", "k2", "v2"):
                run_dve(dve, jobs[name], None)
            n = 0

            def o(ins):
                nonlocal n
                n += 1
                ins.then_inc(r_dve, 1)
                dve.wait_ge(r_dve, n)
            flat = lambda ap: ap.rearrange("p n t -> p (n t)")
            dve.wait_ge(r_pe, 1)
            o(dve.tensor_scalar(flat(qk_mean), psum[:, 0:6, :].rearrange("p b t -> p (b t)"), 1.0 / P, EPS, ALU.mult, ALU.add))
            dve.wait_ge(r_act, 2)
            y, tmp = flat(qk_rstd), flat(qk_tmp[:, :, :])
            o(dve.scalar_tensor_tensor(tmp, y, -0.5, y, ALU.mult, ALU.mult))
            o(dve.tensor_tensor(tmp, tmp, flat(qk_mean), ALU.mult))
            o(dve.scalar_tensor_tensor(y, tmp, 1.5, y, ALU.add, ALU.mult))
            o(dve.scalar_tensor_tensor(qk12[:, 0:8, :], qk12[:, 0:8, :], col("g_q"), qk_rstd[:, 0:8, :], ALU.mult, ALU.mult))
            o(dve.scalar_tensor_tensor(qk12[:, 8:12, :], qk12[:, 8:12, :], col("g_k"), qk_rstd[:, 8:12, :], ALU.mult, ALU.mult))
            dve.wait_ge(r_pe, 2)
            dve.wait_ge(ax_in, 32)
            o(dve.tensor_tensor(qk_tmp[:, 0:10, :], psum[:, 0:5, :].rearrange("p b (n t) -> p (b n) t", t=T),
                                ax_sin[:, :].unsqueeze(1).to_broadcast([P, 10, T]), ALU.mult))
            o(dve.tensor_tensor(qk12[:, 0:8, :], qk12[:, 0:8, :], ax_cos[:, :].unsqueeze(1).to_broadcast([P, 8, T]), ALU.mult))
            o(dve.tensor_tensor(qk12[:, 0:8, :], qk12[:, 0:8, :], qk_tmp[:, 0:8, :], ALU.add))
            o(dve.tensor_tensor(kx, kx, ax_cos[:, :].unsqueeze(1).to_broadcast([P, 2, T]), ALU.mult))
            o(dve.tensor_tensor(kx, kx, qk_tmp[:, 8:10, :], ALU.add))
            att2.dve(dve)
            run_dve(dve, jobs["wo2"], dve_add_gated(dve, 2, gate_of(4), 1))
            n25.dve(dve)
            feed4.dve(dve)
            last.dve(dve)

        @block.gpsimd
        def _(pool):
            first.pool(pool)
            memory.pool(pool)
            gated_pool(pool)
            cross.pool(pool)
            ffn.pool(pool)
            feed0.pool(pool)
            between.pool(pool)
            n20.pool(pool)
            feed1.pool(pool)
            n21.pool(pool)
            n22.pool(pool)
            feed2.pool(pool)
            n23.pool(pool)
            feed3.pool(pool)
            n24.pool(pool)
            n25.pool(pool)
            feed4.pool(pool)
            last.pool(pool)


def shape_tables():
    f64 = np.float64
    i = np.arange(P)
    t = {}
    t["ident"] = np.eye(P)
    t["ones"] = np.ones((P, P))
    rot = np.zeros((P, P))
    for m in range(P):
        if m % 64 < 32:
            rot[m + 32, m] = -1.0
        else:
            rot[m - 32, m] = 1.0
    t["rot"] = rot
    t["row_sums"] = (i[:, None] // 2 == np.arange(2)[None, :]) & (i[:, None] < 4)
    t["headones"] = (i[:, None] // HD == i[None, :] // HD)
    t["lagsel"] = np.stack([i[:, None] // 32 == 2 * j + i[None, :] // HD for j in range(2)], 1)
    t["triu"] = i[:, None] <= i[None, :]
    t["triu_strict"] = i[:, None] < i[None, :]
    t["second_half"] = np.stack([(i[:, None] // (2 * L) == i[None, :] // (2 * L)) & (i[:, None] // L % 2 == 1) & (i[None, :] // L % 2 == 0)
                                 for L in (1, 2, 4, 8, 16, 32, 64)], 1)
    gamma = np.log(1.0 - np.exp2(-5.0 - np.arange(HEADS)))
    rel = np.arange(T)[None, :] - i[:, None]
    t["decay"] = np.stack([np.where(rel >= 0, np.exp(g * np.maximum(rel, 0)), 0.0) * HD ** -0.5 for g in gamma], 1)
    n, c = np.arange(T, dtype=f64), np.arange(P, dtype=f64)
    chan = 2 * np.pi * (np.outer(c, c) % P) / P
    tok = 2 * np.pi * (np.outer(n, n) % T) / T
    t["dft_c"] = np.concatenate([np.cos(chan), -np.sin(chan)], 1)
    for name, f in (("dft_cos", np.cos), ("dft_sin", np.sin)):
        t[name] = (f(tok) / np.sqrt(T * P)).reshape(2, P, T).transpose(1, 0, 2)
    grid_w, axis = 64, HD
    inv = (10000.0 ** (-np.arange(0, axis, 2, dtype=np.float32) / np.float32(axis))).astype(np.float32)
    ang = np.zeros((P, T), np.float32)
    for m in range(P):
        where = (np.arange(T) // grid_w if m < HD else np.arange(T) % grid_w).astype(np.float32)
        ang[m] = where * inv[m % 32]
    t["ax_cos"], t["ax_sin"] = np.cos(ang.astype(f64)), np.sin(ang.astype(f64))
    freqs = (np.float32(10000.0) ** (-np.arange(0, HD, 2, dtype=np.float32) / np.float32(HD))).astype(np.float32)
    t["freq"] = freqs[i % 32][:, None]
    return {k: np.ascontiguousarray(v, dtype=np.float32) for k, v in t.items()}


def features(a):
    a = np.asarray(a)
    return np.moveaxis(a.reshape(a.shape[:-1] + (-1, P)), -1, 0)


def tiles_fm(w, n_tiles=2):
    k, n = w.shape
    a = w.reshape(k // P, P, n // (P * n_tiles), n_tiles, P)
    return np.ascontiguousarray(a.transpose(2, 1, 3, 0, 4)).reshape(n // (P * n_tiles), P, -1)


def tiles_tm(w):
    k, n = w.shape
    return np.ascontiguousarray(w.reshape(k // P, P, n // 256, 256).transpose(2, 1, 0, 3)).reshape(n // 256, P, -1)


def pair_up(w, ff):
    g = np.zeros((2, w.shape[0], FF_TILES * P), np.float32)
    g[0, :, :ff], g[1, :, :ff] = w[:, :ff], w[:, ff:]
    a = g.reshape(2, KT, P, FF_TILES, P)
    return np.ascontiguousarray(a.transpose(3, 2, 0, 1, 4)).reshape(FF_TILES, P, -1)


def down(w):
    g = np.zeros((FF_TILES * P, w.shape[1]), np.float32)
    g[:w.shape[0]] = w
    a = g.reshape(2, HALF, P, KT, P)
    return np.ascontiguousarray(a.transpose(0, 3, 2, 1, 4)).reshape(2, KT, P, -1)


def kernel(**inp):
    import concourse.bacc as bacc
    from concourse.bass_utils import run_bass_kernel_spmd

    inp = {k: np.asarray(v) for k, v in inp.items()}
    nc = bacc.Bacc("TRN2", target_bir_lowering=False, num_devices=1)
    arrays, io = {}, {}

    def give(name, a):
        a = np.ascontiguousarray(a)
        arrays[f"in_{name}"] = a
        io[name] = nc.dram_tensor(f"in_{name}", a.shape, mybir.dt.from_np(a.dtype), kind="ExternalInput").ap()

    tables = shape_tables()
    for name, a in tables.items():
        if name != "freq":
            give(name, a)

    def stream(a):
        return a.reshape(T, KT, P).transpose(2, 1, 0)

    give("x", stream(inp["x"][0]))
    give("mem", stream(inp["mem"][0]))
    give("ctx", stream(inp["ctx_2"][0]))
    give("pos", np.broadcast_to(inp["positions"][0].astype(np.int32), (P, T)))

    w = inp["w_in"][0]
    names = "rq rk rv rg bq bk bv ba bb bg cq ck cv c_lr cg dq df di dg".split()
    widths = [256, 256, 256, 256, 256, 256, 256, 4, 4, 256, 128, 128, 256, 16, 256, 256, 256, 256, 256]
    at = dict(zip(names, np.cumsum([0] + widths[:-1])))
    part = {n: w[:, at[n]:at[n] + wd] for n, wd in zip(names, widths)}
    give("w_in_a", tiles_fm(np.concatenate([part[n] for n in "rq rk bq bk bv cq dq ck df rv cv di".split()], 1)))
    give("w_in_g", tiles_fm(np.concatenate([part[n] for n in "rg bg cg dg".split()], 1)))
    few = np.zeros((D, P), np.float32)
    few[:, 0:4], few[:, 32:36], few[:, 64:80] = part["ba"], part["bb"], part["c_lr"]
    give("w_in_small", tiles_fm(few, 1))
    gk = np.zeros((P, P), np.float32)
    gk[64:80] = inp["gla_gk_up"][0]
    give("gk_up", gk)
    give("w_out", tiles_fm(inp["w_out"][0]))
    give("wk", tiles_fm(inp["xattn_wk"][0]))
    give("wv", tiles_tm(inp["xattn_wv"][0]))
    give("wq", tiles_fm(inp["xattn_wq"][0]))
    give("wo", tiles_fm(inp["xattn_wo"][0]))
    ff1, ff2 = inp["ffn_down"].shape[1], inp["w_ffn1_down_2"].shape[1]
    ups = {"ffn": pair_up(inp["ffn_up"][0], ff1), "a1": pair_up(inp["w_ffn1_gu_2"][0], ff2), "a2": pair_up(inp["w_ffn2_gu_2"][0], ff2),
           "b1": pair_up(inp["w_ffn1_gu_2"][1], ff2), "b2": pair_up(inp["w_ffn2_gu_2"][1], ff2)}
    downs = {"ffn": down(inp["ffn_down"][0]), "a1": down(inp["w_ffn1_down_2"][0]), "a2": down(inp["w_ffn2_down_2"][0]),
             "b1": down(inp["w_ffn1_down_2"][1]), "b2": down(inp["w_ffn2_down_2"][1])}
    for name in ups:
        for half in range(2):
            give(f"{name}_up{half}", ups[name][half * HALF:(half + 1) * HALF])
            give(f"{name}_down{half}", downs[name][half])
    give("mod", np.concatenate([tiles_tm(inp["w_mod_2"][l]) for l in range(2)]))
    ab = inp["w_in_ab_2"][0]
    give("ab_a", tiles_fm(ab[:, 0:512]))
    give("ab_u", tiles_fm(ab[:, 512:1024]))
    give("ab_v", tiles_tm(ab[:, 1024:1536]))
    give("ab_out", tiles_fm(inp["w_out_ab_2"][0]))
    qkv = inp["w_qkv_2"][0]
    give("q2", tiles_fm(qkv[:, 0:1024]))
    give("k2", tiles_fm(qkv[:, 1024:1280]))
    give("v2", tiles_tm(qkv[:, 1280:1536]))
    give("wo2", tiles_fm(inp["w_o_2"][0]))
    give("ws_t", inp["w_s_2"][0].transpose(2, 0, 1))
    give("bs_row", np.broadcast_to(inp["b_s_2"][0], (P, 4, P)))
    give("gv_row", np.broadcast_to(inp["g_v_2"][0], (P, 4, P)))
    give("b_mod", features(inp["b_mod_2"].reshape(-1)))
    give("gains", np.stack([features(inp[g][l]) for l in range(2) for g in ("g_ffn1_2", "g_mix_2", "g_ffn2_2")], 1))
    give("c_in", np.stack([features(inp["c_2"][0]), features(inp["c_ctx_2"])], 2))

    blocks, cols, width = [], {}, 0

    def block(name, a):
        nonlocal width
        full = np.zeros((P, a.shape[1]), np.float32)
        full[:a.shape[0]] = a
        blocks.append(full)
        cols[name] = width
        width += a.shape[1]

    for name in ("mix_norm_w", "mem_norm_w", "xattn_norm_w", "ffn_norm_w", "final_norm_w"):
        block(name, features(inp[name].reshape(-1)))
    block("g_final", features(inp["g_final_2"]))
    for tap in range(4):
        block(f"gdn_conv{tap}", features(inp["gdn_conv_w"][0][tap]))
    for tap in range(3):
        w_tap = np.zeros((2, FF_TILES * P), np.float32)
        w_tap[:, :ff1] = inp["ffn_conv_w"][0][tap].reshape(2, ff1)
        block(f"ff_conv{tap}", features(w_tap.reshape(-1)))
    block("gdn_dt", inp["gdn_dt_bias"].T)
    block("gdn_a_log", inp["gdn_a_log"].T)
    block("rate", np.zeros((P, 1)))
    block("gk_bias", inp["gla_gk_bias"].T)
    block("freq", tables["freq"])
    head_gain = np.ones((P, 8), np.float32)
    for j, name in enumerate(("gdn_norm_w", "gla_norm_w", "hgrn_norm_w")):
        for i in range(2):
            for tile in range(2):
                head_gain[i * HD:(i + 1) * HD, 2 + 2 * j + tile] = inp[name][0]
    block("head_gain", head_gain)
    block("g_q", inp["g_q_2"].T)
    block("g_k", inp["g_k_2"].T)
    for name, n in (("gcol", 8), ("bcol", 8), ("gam", 8), ("tailc", 4), ("att", 8)):
        block(name, np.zeros((P, n)))
    io["cols"] = cols
    give("small", np.concatenate(blocks, 1))

    io["out"] = nc.dram_tensor("out", (P, KT, T), F32, kind="ExternalOutput").ap()
    full, dn = CHUNK, HALF * P
    plan = [("w_in_a", 11, full), ("w_in_g", 4, full), ("w_in_small", 1, full // 2), ("w_out", 6, full, 2), ("wk", 6, full, 2),
            ("wv", 6, full, 2), ("wq", 6, full, 2), ("wo", 6, full, 2)]

    def feed(name, up_mods=6, down_mods=4):
        return [(f"{name}_{part}{half}", n + mods, size, mods) for half in range(2)
                for part, n, size, mods in (("up", HALF, full, up_mods), ("down", KT, dn, down_mods))]

    plan += feed("ffn", 0, 4) + feed("a1") + [("ab_a", 2, full), ("ab_u", 2, full), ("ab_v", 2, full), ("ab_out", 6, full, 2)]
    plan += feed("a2") + feed("b1", 6, 0) + [("q2", 4, full), ("k2", 1, full), ("v2", 1, full), ("wo2", 4, full)] + feed("b2", 0, 0)
    plan = [(name, n, size, io[name], bool(mods)) for name, n, size, mods in [job + (0,) * (4 - len(job)) for job in plan]]
    build(nc, io, plan)
    got = run_bass_kernel_spmd(nc, [arrays], core_ids=[0]).results[0]["out"]
    return np.ascontiguousarray(got.transpose(2, 1, 0)).reshape(1, T, D)
```

```python
from contextlib import ExitStack

import numpy as np

import concourse.bass as bass
from concourse import mybir

F32 = mybir.dt.float32
F32R = mybir.dt.float32r
I32 = mybir.dt.int32
ACT = mybir.ActivationFunctionType
ALU = mybir.AluOpType
AX_X = mybir.AxisListType.X

P = 128
T = 256
D = 1024
KT = D // P
SLOTS = 3
CHUNK = 2048
EPS = 1e-6
HEADS = 4
HD = 64
FF_TILES = 22
HALF = FF_TILES // 2
LAG = 16
LEVELS = (128, 64, 32, 16)
MAGIC = 1.5 * 2.0**23
TWO_PI_A = 6.28125
TWO_PI_B = 0.0019353071693331003

RQ, RK, BQ, BK, BV, CQ, DQ, CK, DF, RV, CV, DI, RG, BG, CG, DG = 0, 2, 4, 6, 8, 10, 11, 13, 14, 16, 18, 20, 22, 24, 26, 28
Z_TILES = 30


class Job:

    def __init__(self, base, n, size, dram, first=False, mod_at=None, mod_base=None, packed_last=None):
        self.base, self.n, self.size, self.dram, self.first, self.mod_at, self.mod_base = base, n, size, dram, first, mod_at, mod_base
        self.packed_last = packed_last

    def is_mod(self, c):
        return self.mod_at is not None and c % SLOTS == self.mod_at

    def size_at(self, c):
        if self.packed_last is not None and c == self.n - 1:
            return self.size // 2
        return CHUNK if self.is_mod(c) else self.size


class Step:

    def __init__(self, job, c, u, i=None):
        self.job, self.chunk = job, c
        self.g = c + job.base
        self.is_mod = job.is_mod(u)
        if i is None:
            i, u3 = u // SLOTS, u % SLOTS
        else:
            u3 = u
        mixed = job.mod_at is not None
        self.c = i * (SLOTS - 1) + (u3 - 1 if u3 > job.mod_at else u3) if mixed else c
        self.m = i + job.mod_base if mixed else None
        self.static = c if isinstance(c, int) else None
        self.slot = (job.base + u) % SLOTS
        self.bank = 2 * self.slot


def steps(eng, job, ahead=0):
    loops = max(0, job.n - ahead) // SLOTS
    done = 0
    if loops >= 2:
        peeled = 1 if job.first else 0
        for c in range(peeled * SLOTS):
            s = Step(job, c, c)
            s.looped = False
            yield s
        with eng.Fori(peeled, loops) as i:
            for u in range(SLOTS):
                s = Step(job, i * SLOTS + u, u, i)
                s.looped = True
                s.i = i
                s.u = u
                yield s
        done = loops * SLOTS
    for c in range(done, job.n):
        s = Step(job, c, c)
        s.looped = False
        yield s


def build(nc, io, plan):
    jobs = {}
    sizes = []
    mod_chunks = 0
    for name, n, size, dram, mod_at in plan:
        job = jobs[name] = Job(len(sizes), n, size, dram, name in ("w_in_a", "w_out", "ffn_up0"), mod_at, mod_chunks,
                               io.get(f"{name}_last"))
        mod_chunks += sum(job.is_mod(c) for c in range(n))
        sizes += [job.size_at(c) for c in range(n)]
    total = len(sizes)

    with ExitStack() as ctx:
        def sb(name, shape, dt=F32, scope=ctx):
            return scope.enter_context(nc.sbuf_tensor(name, shape, dt))

        def sem(name):
            return ctx.enter_context(nc.semaphore(name))

        psum = ctx.enter_context(nc.psum_tensor("psum", [P, 8, 512], F32))

        raw = sb("raw", [P, SLOTS, CHUNK])
        w_hi = sb("w_hi", [P, SLOTS, CHUNK], F32R)
        w_lo = sb("w_lo", [P, SLOTS, CHUNK], F32R)
        xc = sb("xc", [P, KT, 2 * T])
        xn_hi = sb("xn_hi", [P, KT, 2 * T], F32R)
        xn_lo = sb("xn_lo", [P, KT, 2 * T], F32R)
        small = sb("small", [P, io["small"].shape[1]])
        ident = sb("ident", [P, P])
        ones = sb("ones", [P, P])
        rot = sb("rot", [P, P])
        row_sums = sb("row_sums", [P, 2])
        zeros = sb("zeros", [P, T + P], mybir.dt.bfloat16)
        work = sb("work", [P, 8192])
        nrm = work[:, 0:KT * 2 * T].rearrange("p (k t) -> p k t", k=KT)
        rstd = sb("rstd", [P, 2 * T])
        mean = sb("mean", [P, 2 * T])
        mods = sb("mods", [P, 144, 2])
        gains = sb("gains", [P, 6, KT])
        scales = sb("scales", [P, 6, KT, 2])
        b_mod = sb("b_mod", [P, 144])
        c_in = sb("c_in", [P, KT, 2])
        c4 = sb("c4", [P, KT, 4], F32R)
        mrow = sb("mrow", [P, 256])
        X = slice(0, T)
        C = slice(T, 2 * T)
        XC = slice(0, 2 * T)

        cols = io["cols"]

        def col(name, k=0):
            return small[:, cols[name] + k:cols[name] + k + 1]

        raw_landed = [sem(f"raw_landed{s}") for s in range(SLOTS)]
        tables_in = sem("tables_in")
        start_in = sem("start_in")
        hi_ready = sem("hi_ready")
        lo_ready = sem("lo_ready")
        chunk_done = sem("chunk_done")
        evacuated = sem("evacuated")

        def load(sp, s):
            if s.looped or s.g >= SLOTS:
                sp.wait_ge(lo_ready, s.g + (1 - SLOTS))
            src = io["mod"][s.m] if s.is_mod else s.job.dram[s.c]
            size = CHUNK if s.is_mod else s.job.size
            if not s.looped and s.job.packed_last is not None and s.static == s.job.n - 1:
                src, size = s.job.packed_last, size // 2
            sp.dma_start(raw[:, s.slot, 0:size], src).then_inc(raw_landed[s.slot], 16)

        def split_hi(act, s, ahead=2):
            if not s.looped and s.g + ahead >= total:
                return
            slot = (s.slot + ahead) % SLOTS
            size = s.job.size_at(s.u + ahead) if s.looped else sizes[s.g + ahead]
            g = s.g + ahead
            turn = (s.i + (s.job.base + s.u + ahead) // SLOTS) if s.looped else g // SLOTS
            act.wait_ge(raw_landed[slot], turn * 16 + 16)
            if s.looped or g >= SLOTS:
                act.wait_ge(chunk_done, s.g + (ahead + 1 - SLOTS))
            act.activation(w_hi[:, slot, 0:size], raw[:, slot, 0:size], ACT.Copy).then_inc(hi_ready, 1)

        def split_lo(dve, s, ahead=2):
            if not s.looped and s.g + ahead >= total:
                return
            slot = (s.slot + ahead) % SLOTS
            size = s.job.size_at(s.u + ahead) if s.looped else sizes[s.g + ahead]
            dve.wait_ge(hi_ready, s.g + (ahead + 1))
            dve.tensor_tensor(w_lo[:, slot, 0:size], raw[:, slot, 0:size], w_hi[:, slot, 0:size].bitcast(F32),
                              ALU.subtract).then_inc(lo_ready, 1)

        def first_splits(eng, split):
            for c in range(2):
                s = Step(Job(0, total, 0, None), c - 2, c - 2)
                s.g = c - 2
                s.slot = (c - 2) % SLOTS
                s.looped = False
                split(eng, s)

        def bank_free(pe, s):
            if s.looped or s.g >= SLOTS:
                pe.wait_ge(evacuated, s.g + (1 - SLOTS))

        def three_passes(pe, out, lhs, rhs, first, last, group=False):
            (lh, ll), (rh, rl) = lhs, rhs
            pe.matmul(out, lh, rh, start=first, stop=False, skip_group_check=group)
            pe.matmul(out, lh, rl, start=False, stop=False, skip_group_check=group)
            return pe.matmul(out, ll, rh, start=False, stop=last, skip_group_check=group)

        def pe_feature_major(pe, job, act_hi, act_lo, span, n_tiles=2, k_tiles=KT, before_k=None, last_rows=P):
            for s in steps(pe, job):
                bank_free(pe, s)
                if s.is_mod:
                    mod_pe(pe, s)
                    continue
                pe.wait_ge(lo_ready, s.g + 1)
                for k in range(k_tiles):
                    if before_k is not None:
                        before_k(s, k)
                    for n in range(1 if packed(s) else n_tiles):
                        w = slice((n * k_tiles + k) * P, (n * k_tiles + k + 1) * P)
                        r = slice(0, last_rows if k == k_tiles - 1 else P)
                        mm = three_passes(pe, psum[:, s.bank + n, 0:span.stop - span.start],
                                          (w_hi[r, s.slot, w], w_lo[r, s.slot, w]),
                                          (act_hi[r, k, span], act_lo[r, k, span]), k == 0, k == k_tiles - 1)
                mm.then_inc(chunk_done, 1)

        def pe_token_major(pe, job, span):
            for s in steps(pe, job):
                bank_free(pe, s)
                if s.is_mod:
                    mod_pe(pe, s)
                    continue
                pe.wait_ge(lo_ready, s.g + 1)
                for tt in range((span.stop - span.start) // P):
                    tok = slice(span.start + tt * P, span.start + (tt + 1) * P)
                    for k in range(KT):
                        w = slice(k * 256, (k + 1) * 256)
                        mm = three_passes(pe, psum[:, s.bank + tt // 2, (tt % 2) * 256:(tt % 2) * 256 + 256],
                                          (xn_hi[:, k, tok], xn_lo[:, k, tok]),
                                          (w_hi[:, s.slot, w], w_lo[:, s.slot, w]), k == 0, k == KT - 1)
                mm.then_inc(chunk_done, 1)

        n_sq, n_added, n_sum, n_mean, n_guess, n_rstd, n_scaled, n_hi, n_lo = [sem(x) for x in (
            "norm_squares", "norm_squares_added", "norm_sums", "norm_mean", "norm_guess", "norm_rstd", "norm_scaled", "norm_hi", "norm_lo")]

        class Norm:
            made, scaled, split, squared, added = 0, 0, 0, 0, 0

            def __init__(self, span, scale, shift=None, out=None, tiles=1, direct=None, pool_low=False):
                self.pool_low = pool_low
                self.direct = direct or tiles
                self.tiles = tiles
                self.squared_base = Norm.squared
                Norm.squared += KT // tiles
                self.added_base = Norm.added
                Norm.added += KT - self.direct - 1
                self.j, self.span, self.scale, self.shift, self.out = Norm.made, span, scale, shift, out
                self.w = span.stop - span.start
                self.halves = self.w // T
                self.scaled_base, self.split_base = Norm.scaled, Norm.split
                Norm.made += 1
                Norm.scaled += KT * self.halves
                Norm.split += 0 if out is not None else KT * self.halves

            def act_squares(self, act):
                for k in range(0, KT, self.tiles):
                    act.activation(nrm[:, k:k + self.tiles, 0:self.w], xc[:, k:k + self.tiles, self.span], ACT.Square).then_inc(n_sq, 1)

            def act_squares_after(self, act):
                def evac(s):
                    k = s.c * self.tiles
                    tile = bass.ds(k, self.tiles) if s.looped else slice(k, k + self.tiles)
                    act.wait_ge(evacuated, s.g + 1)
                    act.activation(nrm[:, tile, 0:self.w], xc[:, tile, self.span], ACT.Square).then_inc(n_sq, 1)
                return evac

            def pool(self, pool):
                for k in range(1, KT - self.direct):
                    pool.wait_ge(n_sq, self.squared_base + k // self.tiles + 1)
                    if k > 1 or self.added_base:
                        pool.wait_ge(n_added, self.added_base + k - 1)
                    pool.tensor_tensor(nrm[:, 0, 0:self.w], nrm[:, 0, 0:self.w], nrm[:, k, 0:self.w], ALU.add).then_inc(n_added, 1)

            def pe(self, pe):
                pe.wait_ge(n_added, self.added_base + KT - self.direct - 1)
                pe.matmul(psum[:, 6, 0:self.w], ones[:, :], nrm[:, 0, 0:self.w], start=True, stop=False)
                for k in range(KT - self.direct, KT):
                    pe.wait_ge(n_sq, self.squared_base + k // self.tiles + 1)
                    mm = pe.matmul(psum[:, 6, 0:self.w], ones[:, :], nrm[:, k, 0:self.w], start=False, stop=(k == KT - 1))
                mm.then_inc(n_sum, 1)

            def act_rest(self, act):
                act.activation(col("tables", self.j), col("freq"), ACT.Abs_reciprocal_sqrt)
                act.wait_ge(n_mean, self.j + 1)
                act.activation(rstd[:, 0:self.w], mean[:, 0:self.w], ACT.Abs_reciprocal_sqrt).then_inc(n_guess, 1)
                if self.out is not None:
                    return
                for k in range(KT):
                    act.wait_ge(n_scaled, self.scaled_base + (k + 1) * self.halves)
                    for h in range(self.halves):
                        t, o = slice(h * T, (h + 1) * T), slice(self.span.start + h * T, self.span.start + (h + 1) * T)
                        if self.shift is None:
                            act.activation(xn_hi[:, k, o], nrm[:, k, t], ACT.Copy).then_inc(n_hi, 1)
                        else:
                            act.activation(xn_hi[:, k, o], nrm[:, k, t], ACT.Identity, bias=self.shift(k, h)).then_inc(n_hi, 1)

            def dve(self, dve):
                m, r, j3 = mean[:, 0:self.w], rstd[:, 0:self.w], 3 * self.j
                tmp = work[:, 7168:7168 + self.w]
                dve.wait_ge(n_sum, self.j + 1)
                dve.tensor_scalar(m, psum[:, 6, 0:self.w], 1.0 / D, EPS, ALU.mult, ALU.add).then_inc(n_mean, 1)
                dve.wait_ge(n_guess, self.j + 1)
                dve.scalar_tensor_tensor(tmp, r, -0.5, r, ALU.mult, ALU.mult).then_inc(n_rstd, 1)
                dve.wait_ge(n_rstd, j3 + 1)
                dve.tensor_tensor(tmp, tmp, m, ALU.mult).then_inc(n_rstd, 1)
                dve.wait_ge(n_rstd, j3 + 2)
                dve.scalar_tensor_tensor(r, tmp, 1.5, r, ALU.add, ALU.mult).then_inc(n_rstd, 1)
                dve.wait_ge(n_rstd, j3 + 3)

                def low(k):
                    dve.wait_ge(n_hi, self.split_base + (k + 1) * self.halves)
                    for h in range(self.halves):
                        t, o = slice(h * T, (h + 1) * T), slice(self.span.start + h * T, self.span.start + (h + 1) * T)
                        if self.shift is None:
                            dve.tensor_tensor(xn_lo[:, k, o], nrm[:, k, t], xn_hi[:, k, o].bitcast(F32), ALU.subtract).then_inc(n_lo, 1)
                        else:
                            dve.scalar_tensor_tensor(xn_lo[:, k, o], nrm[:, k, t], self.shift(k, h), xn_hi[:, k, o].bitcast(F32),
                                                     ALU.add, ALU.subtract).then_inc(n_lo, 1)

                for k in range(KT):
                    for h in range(self.halves):
                        t, o = slice(h * T, (h + 1) * T), slice(self.span.start + h * T, self.span.start + (h + 1) * T)
                        dst = nrm[:, k, t] if self.out is None else self.out[:, k, t]
                        dve.scalar_tensor_tensor(dst, xc[:, k, o], self.scale(k, h), r[:, t], ALU.mult, ALU.mult).then_inc(n_scaled, 1)
                    if self.out is None and k and not self.pool_low:
                        low(k - 1)
                if self.out is None and not self.pool_low:
                    low(KT - 1)

            def pool_lows(self, pool):
                for k in range(KT):
                    pool.wait_ge(n_hi, self.split_base + k + 1)
                    pool.tensor_tensor(xn_lo[:, k, self.span], nrm[:, k, 0:self.w], xn_hi[:, k, self.span].bitcast(F32),
                                       ALU.subtract).then_inc(n_lo, 1)

            def ready(self, pe, k):
                pe.wait_ge(n_lo, self.split_base + (k + 1) * self.halves)

            def ready_at_first(self, pe):
                def before_k(s, k):
                    if (s.u if s.looped else s.static) == (1 if s.job.mod_at == 0 else 0):
                        self.ready(pe, k)
                return before_k

        AT = {
            "ret_act": dict(sines=2),
            "ret_dve": dict(angle=6, rotated=11, v_tok=12, decayed=14, out=15),
            "ret_pe": dict(turned=1, v_tok=2, scores=3, out=4),
            "gdn_act": dict(taps=1, softplus=4, rate=5, beta=6, silu=7, squares=8, beta_rows=9, rsqrt=10,
                            q_decay=11, tail=12, col_decays=13, ratio=14),
            "gdn_dve": dict(cleared=1, conv=4, rows=7, tok=8, spread=10, cums=11, difference=12, tail=13,
                            sums=14, unit=19, log_ratio=20, tokens=22, strict=29, u0=36,
                            s1=37, rest=39, u1=40, out=41),
            "gdn_pe": dict(tok=1, cums=2, cum_rows=3, beta_rows=4, sums=5, tokens=6, kk=7, u0=8, s1=9, w=10, u1=11,
                           out=12),
            "gat_act": dict(u=1, ln=4, key=5),
            "gat_dve": dict(u=1, log_f=3, scaled=4, tok=6, out=7),
            "gat_pe": dict(gk=1, tok=2, zero=3, out=4),
        }
        stage_sem = {name: sem(name) for name in AT}

        class order:
            def __init__(self, eng, name):
                self.eng, self.name, self.n = eng, name, 0

            def __call__(self, ins, result=None):
                self.n += 1
                ins.then_inc(stage_sem[self.name], 1)
                if result is not None:
                    assert AT[self.name][result] == self.n, (self.name, result, self.n)
                self.eng.wait_ge(stage_sem[self.name], self.n)

        def need(eng, name, result):
            eng.wait_ge(stage_sem[name], AT[name][result])

        def bank(b):
            return psum[:, b, :]

        def area(at, n, w=P):
            return work[:, at:at + n * w].rearrange("p (n t) -> p n t", t=w)

        mix = ExitStack()
        z = sb("z", [P, Z_TILES, T], scope=mix)
        zs = sb("zs", [P, T], scope=mix)
        headones = sb("headones", [P, P], scope=mix)
        lagsel = sb("lagsel", [P, 2, P], scope=mix)
        triu = sb("triu", [P, P], scope=mix)
        tril_strict = sb("tril_strict", [P, P], scope=mix)
        second_half = sb("second_half", [P, 7, P], scope=mix)
        decay = sb("decay", [P, HEADS, T], scope=mix)
        gk_up = sb("gk_up", [P, P], scope=mix)
        pos = sb("pos", [P, T], I32, scope=mix)
        gt = sb("gt", [P, 2, P], scope=mix)
        s1 = sb("s1", [P, 2, HD], scope=mix)
        MIX = dict(headones=headones, lagsel=lagsel, triu=triu, tril_strict=tril_strict, second_half=second_half,
                   decay=decay, gk_up=gk_up, pos=pos)

        def load_mixer_tables(sp):
            for name in MIX:
                sp.dma_start(MIX[name][:], io[name]).then_inc(tables_in, 16)

        UP = 16 * T
        ret_a = work[:, UP + 10 * T:UP + 16 * T].rearrange("p (h n) -> p h n", h=HEADS)
        ret_v = area(UP + 8 * T, 2, T)

        def retention_dve_angles(dve, o):
            ang, kk_, sn = (work[:, UP + i * T:UP + (i + 1) * T] for i in range(3))
            dve.wait_ge(tables_in, 16 * len(MIX))
            o(dve.tensor_copy(ang, pos[:, :]))
            o(dve.tensor_scalar(ang, ang, col("freq"), None, ALU.mult))
            o(dve.tensor_scalar(kk_, ang, 1.0 / (2 * np.pi), MAGIC, ALU.mult, ALU.add))
            o(dve.tensor_scalar(kk_, kk_, MAGIC, None, ALU.subtract))
            o(dve.scalar_tensor_tensor(ang, kk_, -TWO_PI_A, ang, ALU.mult, ALU.add))
            o(dve.scalar_tensor_tensor(ang, kk_, -TWO_PI_B, ang, ALU.mult, ALU.add), "angle")
            need(dve, "ret_act", "sines")
            o(dve.tensor_tensor(kk_, sn, sn, ALU.mult))
            o(dve.tensor_scalar(kk_, kk_, -2.0, 1.0, ALU.mult, ALU.add))

        def retention_dve(dve, o, delta_first):
            kk_ = work[:, UP + T:UP + 2 * T]
            qk = z[:, RQ:RQ + 4, :]
            turned = psum[:, 0:2, :].rearrange("p b (t n) -> p (b t) n", n=T)
            part = area(UP + 4 * T, 4, T)
            need(dve, "ret_pe", "turned")
            sines = work[:, UP + 3 * T:UP + 4 * T].unsqueeze(1).to_broadcast([P, 4, T])
            coss = kk_.unsqueeze(1).to_broadcast([P, 4, T])
            o(dve.tensor_tensor(part, turned, sines, ALU.mult))
            o(dve.tensor_tensor(qk, qk, coss, ALU.mult))
            o(dve.tensor_tensor(qk, qk, part, ALU.add), "rotated")
            need(dve, "ret_pe", "v_tok")
            o(dve.tensor_copy(ret_v, psum[:, 2, :].rearrange("p (t n) -> p t n", n=T)), "v_tok")
            delta_first()
            need(dve, "ret_pe", "scores")
            o(dve.tensor_tensor(ret_a[:, :, 0:T], psum[:, 3:7, 0:T], decay[:, :, :], ALU.mult))
            o(dve.tensor_tensor(ret_a[:, :, T:T + P], psum[:, 3:7, T:T + P], decay[:, :, 0:P], ALU.mult), "decayed")
            need(dve, "ret_pe", "out")
            o(dve.tensor_copy(z[:, 0:2, :], psum[:, 7, :].rearrange("p (t n) -> p t n", n=T)), "out")

        def retention_act(act):
            o = order(act, "ret_act")
            need(act, "ret_dve", "angle")
            o(act.activation(work[:, UP + 2 * T:UP + 3 * T], work[:, UP:UP + T], ACT.Sin, scale=0.5))
            o(act.activation(work[:, UP + 3 * T:UP + 4 * T], work[:, UP:UP + T], ACT.Sin), "sines")

        def retention_pe(pe):
            pe.wait_ge(evacuated, jobs["w_in_g"].base + jobs["w_in_g"].n)
            pe.wait_ge(tables_in, 16 * len(MIX))
            o = order(pe, "ret_pe")
            pe.matmul(bank(0), rot[:, :], z[:, RQ:RQ + 2, :], start=True, stop=True)
            o(pe.matmul(bank(1), rot[:, :], z[:, RK:RK + 2, :], start=True, stop=True), "turned")
            for tt in range(2):
                for n in range(2):
                    mm = pe.transpose(psum[:, 2, tt * T + n * P:tt * T + (n + 1) * P], z[:, RV + n, tt * P:(tt + 1) * P], ident[:, :])
            o(mm, "v_tok")
            need(pe, "ret_dve", "rotated")
            for h in range(HEADS):
                r = slice((h % 2) * HD, (h % 2) * HD + HD)
                for st in range(2):
                    mm = pe.matmul(psum[:, 3 + h, st * T:st * T + T - st * P], z[r, RK + h // 2, st * P:(st + 1) * P],
                                   z[r, RQ + h // 2, st * P:T], start=True, stop=True)
            o(mm, "scores")
            need(pe, "ret_dve", "decayed")
            for h in range(HEADS):
                r = slice((h % 2) * HD, (h % 2) * HD + HD)
                c = (h // 2) * T
                v = slice(h * HD, (h + 1) * HD)
                pe.matmul(psum[r, 7, c:c + T], ret_v[:, 0, v], ret_a[:, h, 0:T], start=True, stop=False, skip_group_check=True)
                mm = pe.matmul(psum[r, 7, c + P:c + T], ret_v[:, 1, v], ret_a[:, h, T:T + P], start=False, stop=True, skip_group_check=True)
            o(mm, "out")

        XM, XT, NT, QT, YM, BR, GR, RT = (area(i * 1024, 8) for i in range(8))
        taps = area(0, 6, T)
        ssum, unit_tmp = area(0, 4, T), area(1024, 4, T)
        g_spread, b_spread = NT, QT
        sq4 = area(4096, 4, T)
        gb = work[:, 6 * T:7 * T]
        U0, U1, REST = (work[:, 5120 + i * T:5120 + (i + 1) * T] for i in range(3))
        qg = area(5120 + 3 * T, 2)
        k_tok, v_tok = z[:, 16:18, :], z[:, 2:4, :]
        gcol, bcol, gam = (small[:, cols[x]:cols[x] + 8].rearrange("p (n h) -> p n h", n=2) for x in ("gcol", "bcol", "gam"))
        tailc = small[:, cols["tailc"]:cols["tailc"] + 4]
        level_y, level_x, level_pe = sem("inverse_masked"), sem("inverse_updated"), sem("inverse_products")

        def by_head(ap):
            return ap.rearrange("p n (h d) -> p n h d", d=HD)

        def by_parity(ap, n):
            return ap[:, n * 4:n * 4 + 4, :].rearrange("p (b a) t -> p a b t", a=2)

        def one_bank(b, w=P):
            return psum[:, b, :].rearrange("p (n t) -> p n t", t=w)

        def two_banks(b, w=P):
            return psum[:, b:b + 2, :].rearrange("p b (n t) -> p (b n) t", t=w)

        def newton(dve, o, y, v, tmp, result=None):
            o(dve.scalar_tensor_tensor(tmp, y, -0.5, y, ALU.mult, ALU.mult))
            o(dve.tensor_tensor(tmp, tmp, v, ALU.mult))
            o(dve.scalar_tensor_tensor(y, tmp, 1.5, y, ALU.add, ALU.mult), result)

        def delta_act(act):
            o = order(act, "gdn_act")
            act.wait_ge(n_lo, memory.split_base + KT)
            for k in range(6):
                mm = act.activation(taps[:, k, :], z[:, BQ + k, :], ACT.Copy, scale=col("gdn_conv3", k))
            o(mm, "taps")
            need(act, "gdn_dve", "cleared")
            o(act.activation(gb[0:4, :], zs[0:4, :], ACT.Abs, bias=col("gdn_dt")[0:4, :]))
            o(act.activation(gb[0:4, :], gb[0:4, :], ACT.Exp, scale=-1.0))
            o(act.activation(gb[0:4, :], gb[0:4, :], ACT.Ln, bias=1.0), "softplus")
            o(act.activation(col("rate")[0:4, :], col("gdn_a_log")[0:4, :], ACT.Exp), "rate")
            o(act.activation(gb[32:36, :], zs[32:36, :], ACT.Sigmoid), "beta")
            need(act, "gdn_dve", "conv")
            o(act.activation(z[:, BQ:BQ + 6, :], taps, ACT.Silu), "silu")
            need(act, "ret_dve", "out")
            o(act.activation(sq4, z[:, BQ:BQ + 4, :], ACT.Square), "squares")
            need(act, "gdn_pe", "beta_rows")
            o(act.activation(BR, two_banks(4), ACT.Copy), "beta_rows")
            need(act, "gdn_dve", "sums")
            o(act.activation(sq4, ssum, ACT.Abs_reciprocal_sqrt), "rsqrt")
            o(act.activation(GR[:, 4:8, :], one_bank(3), ACT.Exp), "q_decay")
            o(act.activation(tailc, tailc, ACT.Exp), "tail")
            o(act.activation(gam, gcol, ACT.Exp), "col_decays")
            need(act, "gdn_dve", "log_ratio")
            o(act.activation(RT, RT, ACT.Exp), "ratio")

        def delta_dve_first(dve, o):
            dve.wait_ge(n_lo, memory.split_base + KT)
            o(dve.memset(gb, 0.0), "cleared")
            need(dve, "gdn_act", "taps")
            for back in range(1, 4):
                for k in range(6):
                    mm = dve.scalar_tensor_tensor(taps[:, k, back:T], z[:, BQ + k, 0:T - back], col(f"gdn_conv{3 - back}", k),
                                                  taps[:, k, back:T], ALU.mult, ALU.add)
                o(mm, "conv" if back == 3 else None)
            need(dve, "gdn_act", "beta")
            o(dve.tensor_scalar(zs[0:4, :], zs[0:4, :], col("gdn_dt")[0:4, :], 0.0, ALU.add, ALU.max))
            o(dve.tensor_tensor(gb[0:4, :], gb[0:4, :], zs[0:4, :], ALU.add))
            o(dve.tensor_scalar(gb[0:4, :], gb[0:4, :], col("rate")[0:4, :], -1.0, ALU.mult, ALU.mult), "rows")

        def delta_dve(dve, o, gated_copy, gated_log):
            need(dve, "gdn_pe", "tok")
            o(dve.tensor_copy(gt[:, :, :], psum[:, 0, 0:2 * P].rearrange("p (n t) -> p n t", n=2)), "tok")
            spread_to = [P, 2, HEADS, P]
            o(dve.tensor_copy(g_spread.rearrange("p (n h) t -> p n h t", n=2), gt[:, :, 0:4].unsqueeze(3).to_broadcast(spread_to)))
            o(dve.tensor_tensor(b_spread.rearrange("p (n h) t -> p n h t", n=2), tril_strict[:, :].unsqueeze(1).unsqueeze(1).to_broadcast(spread_to),
                                gt[:, :, 32:36].unsqueeze(3).to_broadcast(spread_to), ALU.mult), "spread")
            need(dve, "gdn_pe", "cums")
            o(dve.tensor_copy(gcol, psum[:, 1, 0:8].rearrange("p (n h) -> p n h", n=2)), "cums")
            need(dve, "gdn_pe", "cum_rows")
            gc8 = small[:, cols["gcol"]:cols["gcol"] + 8].unsqueeze(2).to_broadcast([P, 8, P])
            o(dve.tensor_tensor(RT, two_banks(2), gc8, ALU.subtract), "difference")
            o(dve.tensor_tensor(tailc, one_bank(2)[:, :, P - 1], gcol[:, 0, :], ALU.subtract), "tail")
            need(dve, "gdn_pe", "sums")
            o(dve.tensor_scalar(ssum, two_banks(6, T), EPS, None, ALU.add), "sums")
            need(dve, "gdn_act", "rsqrt")
            newton(dve, o, sq4, ssum, unit_tmp)
            qs, ks = z[:, BQ:BQ + 2, :], z[:, BK:BK + 2, :]
            o(dve.scalar_tensor_tensor(qs, qs, HD ** -0.5, sq4[:, 0:2, :], ALU.mult, ALU.mult))
            o(dve.tensor_tensor(ks, ks, sq4[:, 2:4, :], ALU.mult), "unit")
            o(dve.tensor_scalar(RT, RT, 0.0, None, ALU.min), "log_ratio")
            need(dve, "gdn_pe", "tokens")
            o(dve.tensor_copy(k_tok, psum[:, 0, :].rearrange("p (n t) -> p n t", n=2)))
            beta = gt[:, :, 32:36]
            o(dve.tensor_tensor(by_head(v_tok), by_head(psum[:, 1, :].rearrange("p (n t) -> p n t", n=2)),
                                beta.unsqueeze(3).to_broadcast([P, 2, HEADS, HD]), ALU.mult), "tokens")
            need(dve, "gdn_act", "ratio")
            o(dve.tensor_tensor(RT, RT, triu[:, :].unsqueeze(1).to_broadcast([P, 8, P]), ALU.mult))
            o(dve.tensor_tensor(BR, BR, RT, ALU.mult))
            o(dve.tensor_tensor(bcol, beta, gam, ALU.mult))
            k0 = k_tok[:, 0, :].rearrange("p (h d) -> p h d", d=HD)
            o(dve.tensor_tensor(k0, k0, tailc.unsqueeze(2).to_broadcast([P, HEADS, HD]), ALU.mult))
            o(dve.tensor_copy(XM, ident[:, :].unsqueeze(1).to_broadcast([P, 8, P])))
            dve.tensor_copy(XT, ident[:, :].unsqueeze(1).to_broadcast([P, 8, P])).then_inc(level_x, 4)
            need(dve, "gdn_pe", "kk")
            for dst, b, factor in ((NT, 2, BR), (QT, 4, RT)):
                for n in range(2):
                    o(dve.tensor_tensor(by_parity(dst, n), psum[:, b:b + 2, n * T:(n + 1) * T].rearrange("p a (b t) -> p a b t", t=P),
                                        by_parity(factor, n), ALU.mult), "strict" if b == 2 and n else None)
            for h in range(HEADS):
                r = slice((h % 2) * HD, (h % 2) * HD + HD)
                o(dve.tensor_tensor(qg[r, h // 2, :], z[r, BQ + h // 2, P:T], GR[r, 4 + h, :], ALU.mult))
            gated_copy()
            with dve.Fori(0, 7) as i:
                for a in range(2):
                    four = slice(4 * a, 4 * a + 4)
                    dve.wait_ge(level_pe, i * 4 + (a + 1))
                    dve.tensor_tensor(YM[:, four, :], one_bank(a), second_half[:, bass.ds(i, 1), :].to_broadcast([P, 4, P]), ALU.mult).then_inc(level_y, 1)
                for a in range(2):
                    four = slice(4 * a, 4 * a + 4)
                    dve.wait_ge(level_pe, i * 4 + (a + 3))
                    dve.tensor_tensor(XM[:, four, :], XM[:, four, :], one_bank(2 + a), ALU.subtract).then_inc(level_x, 1)
                    dve.tensor_tensor(XT[:, four, :], XT[:, four, :], one_bank(4 + a), ALU.subtract).then_inc(level_x, 1)
            gated_log()
            need(dve, "gdn_pe", "u0")
            o(dve.tensor_copy(U0, psum[:, 6, 0:T]), "u0")
            need(dve, "gdn_pe", "s1")
            o(dve.tensor_copy(s1[:, :, :], psum[:, 7, 0:P].rearrange("p (n d) -> p n d", d=HD)), "s1")
            need(dve, "gdn_pe", "w")
            o(dve.tensor_tensor(REST.rearrange("p (b a d) -> p a b d", a=2, d=HD), psum[:, 0:2, 0:P].rearrange("p a (b d) -> p a b d", d=HD),
                                bcol[:, 1, :].rearrange("p (b a) -> p a b", a=2).unsqueeze(3).to_broadcast([P, 2, 2, HD]), ALU.mult))
            o(dve.tensor_tensor(REST, v_tok[:, 1, :], REST, ALU.subtract), "rest")
            need(dve, "gdn_pe", "u1")
            o(dve.tensor_copy(U1, psum[:, 1, 0:T]), "u1")
            need(dve, "gdn_pe", "out")
            o(dve.tensor_copy(z[:, 2:4, :], psum[:, 2, :].rearrange("p (n t) -> p n t", n=2)), "out")

        def delta_pe(pe, gated_first):
            o = order(pe, "gdn_pe")
            heads4 = [(h, slice((h % 2) * HD, (h % 2) * HD + HD), slice(h * HD, (h + 1) * HD)) for h in range(HEADS)]
            need(pe, "gdn_dve", "rows")
            need(pe, "gdn_act", "beta")
            for n in range(2):
                mm = pe.transpose(psum[:, 0, n * P:(n + 1) * P], gb[:, n * P:(n + 1) * P], ident[:, :])
            o(mm, "tok")
            need(pe, "gdn_dve", "tok")
            for n in range(2):
                mm = pe.matmul(psum[:, 1, n * 4:n * 4 + 4], triu[:, :], gt[:, n, 0:4], start=True, stop=True)
            o(mm, "cums")
            need(pe, "gdn_dve", "spread")
            for nh in range(8):
                mm = pe.matmul(two_banks(2)[:, nh, :], g_spread[:, nh, :], triu[:, :], start=True, stop=True)
            o(mm, "cum_rows")
            for nh in range(8):
                mm = pe.matmul(two_banks(4)[:, nh, :], b_spread[:, nh, :], ident[:, :], start=True, stop=True)
            o(mm, "beta_rows")
            need(pe, "gdn_act", "squares")
            for i in range(2):
                mm = pe.matmul(bank(6 + i), headones[:, :], sq4[:, 2 * i:2 * i + 2, :], start=True, stop=True)
            o(mm, "sums")
            need(pe, "gdn_dve", "unit")
            for b, tile in ((0, BK), (1, BV)):
                for n in range(2):
                    for i in range(2):
                        mm = pe.transpose(psum[:, b, n * T + i * P:n * T + (i + 1) * P], z[:, tile + i, n * P:(n + 1) * P], ident[:, :])
            o(mm, "tokens")
            need(pe, "gdn_act", "q_decay")
            for b, tile in ((2, BK), (4, BQ)):
                for n in range(2):
                    for h, r, _ in heads4:
                        mm = pe.matmul(psum[:, b + h % 2, (n * 2 + h // 2) * P:(n * 2 + h // 2 + 1) * P], z[r, BK + h // 2, n * P:(n + 1) * P],
                                       z[r, tile + h // 2, n * P:(n + 1) * P], start=True, stop=True)
            o(mm, "kk")
            gated_first()
            need(pe, "gdn_dve", "strict")
            with pe.Fori(0, 7) as i:
                for a in range(2):
                    pe.wait_ge(level_x, i * 4 + (2 * a + 1))
                    for nh in range(4 * a, 4 * a + 4):
                        mm = pe.matmul(two_banks(0)[:, nh, :], NT[:, nh, :], XM[:, nh, :], start=True, stop=True)
                    mm.then_inc(level_pe, 1)
                for a in range(2):
                    pe.wait_ge(level_x, i * 4 + (2 * a + 2))
                    pe.wait_ge(level_y, i * 2 + (a + 1))
                    for nh in range(4 * a, 4 * a + 4):
                        pe.matmul(two_banks(2)[:, nh, :], XT[:, nh, :], YM[:, nh, :], start=True, stop=True)
                        mm = pe.matmul(two_banks(4)[:, nh, :], YM[:, nh, :], XT[:, nh, :], start=True, stop=True)
                    mm.then_inc(level_pe, 1)
            pe.wait_ge(level_x, 32)
            for h, _, f in heads4:
                mm = pe.matmul(psum[:, 6, f], XT[:, h, :], v_tok[:, 0, f], start=True, stop=True)
            o(mm, "u0")
            need(pe, "gdn_dve", "u0")
            need(pe, "gat_act", "u")
            for h, r, f in heads4:
                mm = pe.matmul(psum[r, 7, (h // 2) * HD:(h // 2) * HD + HD], k_tok[:, 0, f], U0[:, f], start=True, stop=True)
            o(mm, "s1")
            need(pe, "gdn_dve", "s1")
            for h, r, f in heads4:
                mm = pe.matmul(psum[:, h % 2, (h // 2) * HD:(h // 2) * HD + HD], z[r, BK + h // 2, P:T], s1[r, h // 2, :], start=True, stop=True)
            o(mm, "w")
            need(pe, "gdn_dve", "rest")
            for h, _, f in heads4:
                mm = pe.matmul(psum[:, 1, f], XT[:, 4 + h, :], REST[:, f], start=True, stop=True)
            o(mm, "u1")
            need(pe, "gdn_dve", "u1")
            for h, r, f in heads4:
                c = (h // 2) * T
                pe.matmul(psum[r, 2, c:c + P], U0[:, f], QT[:, h, :], start=True, stop=True)
                pe.matmul(psum[r, 2, c + P:c + T], U1[:, f], QT[:, 4 + h, :], start=True, stop=False)
                mm = pe.matmul(psum[r, 2, c + P:c + T], s1[r, h // 2, :], qg[r, h // 2, :], start=False, stop=True)
            o(mm, "out")

        Q3, K3, V4, O4 = z[:, CQ:CQ + 3, :], z[:, CK:CK + 3, :], z[:, CV:CV + 4, :], z[:, 4:8, :]
        C3, E3 = area(768, 3, T), area(1536, 3, T)
        U3, SOFT = xc[:, 0:3, C], xc[:, 3:6, C]
        QK = [area(2304, 3, T), area(3072, 3, T)]
        A8 = area(3840, 8, T + P)
        resets = [x[:, i * T:(i + 1) * T] for x in (rstd, mean) for i in range(2)]
        toks = [z[:, 16:18, :], z[:, 8:10, :]]
        LE = [area(1536, 3, T), area(0, 3, T)]
        LTMP = [area(3840, 4, T), area(4864, 4, T)]
        lv_cum, lv_exp, lv_qk, lv_pe = sem("level_cum"), sem("level_decays"), sem("level_scaled"), sem("level_scores")
        copied, resets_set = sem("scores_copied"), sem("resets_set")
        lag_diff, lag_exp, lag_p, lag_bc, lag_tmp, lag_acc = (sem(x) for x in (
            "lag_diff", "lag_decays", "lag_products", "lag_spread", "lag_values", "lag_added"))

        def halves_of(ap, L, side):
            return ap.rearrange("p g (b s l) -> p (g b) s l", s=2, l=L)[:, :, side, :]

        def gated_gates(dve, o):
            need(dve, "gat_act", "ln")
            o(dve.scalar_tensor_tensor(U3, U3, 0.0, SOFT, ALU.min, ALU.subtract))
            o(dve.tensor_scalar(U3[:, 0, :], U3[:, 0, :], 1.0 / 16.0, None, ALU.mult), "log_f")
            o(dve.tensor_scalar(z[:, CQ, :], z[:, CQ, :], (HD // 2) ** -0.5, None, ALU.mult), "scaled")

        def gated_dve(dve, o):
            need(dve, "gat_pe", "tok")
            for i in range(2):
                o(dve.tensor_copy(toks[i], psum[:, 1 + i, :].rearrange("p (n t) -> p n t", n=2)), "tok" if i else None)
            dve.wait_ge(resets_set, 8)
            need(dve, "gat_act", "key")
            for i, L in enumerate(LEVELS):
                if i:
                    dve.wait_ge(lv_exp, 2 * i)
                for g in range(3):
                    mm = dve.tensor_tensor_scan(C3[:, g, :], resets[i], U3[:, g, :], 0.0, ALU.mult, ALU.add)
                mm.then_inc(lv_cum, 1)
                dve.wait_ge(lv_cum, 2 * i + 1)
                left = halves_of(C3, L, 0)
                dve.tensor_tensor(halves_of(E3, L, 0), left[:, :, L - 1:L].to_broadcast([P, left.shape[1], L]), left,
                                  ALU.subtract).then_inc(lv_cum, 1)
                dve.wait_ge(lv_exp, 2 * i + 2)
                if i >= 2:
                    dve.wait_ge(lv_pe, i - 1)
                for side, src in ((0, K3), (1, Q3)):
                    dve.tensor_tensor(halves_of(QK[i % 2], L, side), halves_of(src, L, side), halves_of(E3, L, side),
                                      ALU.mult).then_inc(lv_qk, 1)
            dve.wait_ge(lv_pe, len(LEVELS))
            for j in range(4, 8):
                dve.tensor_copy(A8[:, j, :], psum[:, j, 0:T + P]).then_inc(copied, 1)
            need(dve, "gat_pe", "out")
            o(dve.tensor_copy(O4, two_banks(0, T)), "out")
            for lag in range(LAG + 1):
                if lag < LAG:
                    w = LAG - lag
                    lp = QK[lag % 2].rearrange("p g t -> p (g t)")[:, 0:48 * w].rearrange("p (b l) -> p b l", l=w)
                    q = Q3.rearrange("p g (b l) -> p (g b) l", l=LAG)[:, :, lag:LAG]
                    k = K3.rearrange("p g (b l) -> p (g b) l", l=LAG)[:, :, 0:w]
                    if lag >= 2:
                        dve.wait_ge(lag_bc, lag - 1)
                    if lag == 0:
                        dve.tensor_tensor(lp, q, k, ALU.mult).then_inc(lag_p, 2)
                    else:
                        dve.tensor_tensor(lp, q, k, ALU.mult).then_inc(lag_p, 1)
                        dve.wait_ge(lag_p, 2 * lag + 1)
                        dve.wait_ge(lag_exp, lag)
                        le = LE[lag % 2].rearrange("p g t -> p (g t)")[:, 0:48 * w].rearrange("p (b l) -> p b l", l=w)
                        dve.tensor_tensor(lp, lp, le, ALU.mult).then_inc(lag_p, 1)
                if lag:
                    d = lag - 1
                    w = LAG - d
                    dve.wait_ge(lag_bc, d + 1)
                    if d >= 2:
                        dve.wait_ge(lag_acc, d - 1)
                    got = two_banks(2 * (d % 2), T)[:, :, 0:LAG * w].rearrange("p o (b l) -> p o b l", l=w)
                    tmp = LTMP[d % 2][:, :, 0:LAG * w].rearrange("p o (b l) -> p o b l", l=w)
                    v = V4.rearrange("p o (b l) -> p o b l", l=LAG)[:, :, :, 0:w]
                    dve.tensor_tensor(tmp, got, v, ALU.mult).then_inc(lag_tmp, 1)

        def gated_pool_first(pool):
            pool.wait_ge(n_lo, memory.split_base + KT)
            for i, L in enumerate(LEVELS):
                pool.memset(resets[i], 1.0).then_inc(resets_set, 1)
                pool.wait_ge(resets_set, 2 * i + 1)
                pool.memset(resets[i].rearrange("p (b l) -> p b l", l=L)[:, :, 0], 0.0).then_inc(resets_set, 1)

        def gated_pool(pool):
            pool.wait_ge(lv_qk, 2 * len(LEVELS))
            for d in range(1, LAG + 2):
                if d < LAG:
                    w = LAG - d
                    le = LE[d % 2].rearrange("p g t -> p (g t)")[:, 0:48 * w].rearrange("p (b l) -> p b l", l=w)
                    c = C3.rearrange("p g (b l) -> p (g b) l", l=LAG)
                    if d >= 3:
                        pool.wait_ge(lag_p, 2 * (d - 2) + 2)
                    pool.tensor_tensor(le, c[:, :, d:LAG], c[:, :, 0:w], ALU.subtract).then_inc(lag_diff, 1)
                if d >= 2:
                    e = d - 2
                    w = LAG - e
                    tmp = LTMP[e % 2][:, :, 0:LAG * w].rearrange("p o (b l) -> p o b l", l=w)
                    acc = O4.rearrange("p o (b l) -> p o b l", l=LAG)[:, :, :, e:LAG]
                    pool.wait_ge(lag_tmp, e + 1)
                    if e:
                        pool.wait_ge(lag_acc, e)
                    pool.tensor_tensor(acc, acc, tmp, ALU.add).then_inc(lag_acc, 1)

        def gated_act_first(act):
            o = order(act, "gat_act")
            need(act, "gat_pe", "gk")
            act.wait_ge(n_scaled, memory.scaled_base + KT)
            o(act.activation(U3[:, 0, :], psum[:, 7, 0:T], ACT.Identity, bias=col("gk_bias")), "u")
            need(act, "gat_dve", "u")
            o(act.activation(SOFT, U3, ACT.Abs))
            o(act.activation(SOFT, SOFT, ACT.Exp, scale=-1.0))
            o(act.activation(SOFT, SOFT, ACT.Ln, bias=1.0), "ln")
            o(act.activation(K3[:, 1:3, :], K3[:, 1:3, :], ACT.Sigmoid, scale=-1.0), "key")

        def gated_act(act):
            for i, L in enumerate(LEVELS):
                act.wait_ge(lv_cum, 2 * i + 2)
                act.activation(halves_of(E3, L, 0), halves_of(E3, L, 0), ACT.Exp).then_inc(lv_exp, 1)
                if i:
                    act.wait_ge(lv_qk, 2 * i)
                act.activation(halves_of(E3, L, 1), halves_of(C3, L, 1), ACT.Exp).then_inc(lv_exp, 1)
            act.wait_ge(lv_pe, len(LEVELS))
            for j in range(4):
                act.activation(A8[:, j, :], psum[:, j, 0:T + P], ACT.Copy).then_inc(copied, 1)
            for d in range(1, LAG):
                w = LAG - d
                le = LE[d % 2].rearrange("p g t -> p (g t)")[:, 0:48 * w]
                act.wait_ge(lag_diff, d)
                act.activation(le, le, ACT.Exp).then_inc(lag_exp, 1)

        def gated_pe(pe, o):
            need(pe, "gdn_dve", "out")
            for b, tile in ((1, CV), (2, DI)):
                for n in range(2):
                    for i in range(2):
                        mm = pe.transpose(psum[:, b, n * T + i * P:n * T + (i + 1) * P], z[:, tile + i, n * P:(n + 1) * P], ident[:, :])
            o(mm, "tok")
            need(pe, "gat_dve", "tok")
            need(pe, "gat_act", "u")
            for j in range(8):
                mm = pe.matmul(psum[:, j, 0:T + P], zeros[:, 0:P], zeros[:, 0:T + P], start=True, stop=False, skip_group_check=True)
            o(mm, "zero")
            heads8 = [(j, 0, slice(32 * j, 32 * j + 32)) if j < 4 else (j, 1 + (j - 4) // 2, slice(HD * (j % 2), HD * (j % 2) + HD))
                      for j in range(8)]
            for i, L in enumerate(LEVELS):
                pe.wait_ge(lv_qk, 2 * i + 2)
                for j, tile, r in heads8:
                    for s0 in range(0, T, 2 * L):
                        st, at = s0 // P, s0 % P
                        c = s0 + L + (P if st else 0)
                        mm = pe.matmul(psum[at:at + L, j, c:c + L], QK[i % 2][r, tile, s0:s0 + L], QK[i % 2][r, tile, s0 + L:s0 + 2 * L],
                                       start=False, stop=(i == len(LEVELS) - 1), skip_group_check=True)
                mm.then_inc(lv_pe, 1)
            pe.wait_ge(copied, 8)
            for j in range(8):
                tok, f = toks[j // 4], slice((j % 4) * HD, (j % 4) * HD + HD)
                r, out = slice(HD * (j % 2), HD * (j % 2) + HD), two_banks(0, T)[:, j // 2, :]
                pe.matmul(out[r, :], tok[:, 0, f], A8[:, j, 0:T], start=True, stop=False, skip_group_check=True)
                mm = pe.matmul(out[r, P:T], tok[:, 1, f], A8[:, j, T:T + P], start=False, stop=True, skip_group_check=True)
            o(mm, "out")
            need(pe, "gat_dve", "out")
            for d in range(LAG):
                w = LAG - d
                pe.wait_ge(lag_p, 2 * d + 2)
                if d >= 2:
                    pe.wait_ge(lag_tmp, d - 1)
                lp = QK[d % 2].rearrange("p g t -> p (g t)")
                for out in range(4):
                    tile, sel = (0, lagsel[:, out, :]) if out < 2 else (out - 1, headones[:, :])
                    mm = pe.matmul(two_banks(2 * (d % 2), T)[:, out, 0:LAG * w], sel, lp[:, tile * LAG * w:(tile + 1) * LAG * w],
                                   start=True, stop=True, skip_group_check=True)
                mm.then_inc(lag_bc, 1)

        ctx_in = sem("ctx_in")
        post_hi, post_lo = sem("mixed_hi"), sem("mixed_lo")
        OSQ, OSUM, OTMP = (area(i * 2048, 8, T) for i in range(3))

        post_sq, post_sum, post_mean, post_guess, post_step, post_gated, post_scaled = (sem(x) for x in (
            "mixed_squares", "mixed_sums", "mixed_mean", "mixed_guess", "mixed_newton", "mixed_gated", "mixed_scaled"))

        def pair(i):
            return slice(2 * i, 2 * i + 2)

        def post_act(act):
            act.wait_ge(lag_acc, LAG)
            act.dma_start(xc[:, :, C], io["ctx"]).then_inc(ctx_in, 16)
            for i in range(4):
                act.activation(OSQ[:, pair(i), :], z[:, pair(i), :], ACT.Square).then_inc(post_sq, 1)
            for i in range(6):
                if i < 4:
                    act.wait_ge(post_mean, i + 1)
                    act.activation(OSQ[:, pair(i), :], OSUM[:, pair(i), :], ACT.Abs_reciprocal_sqrt).then_inc(post_guess, 1)
                if i >= 2:
                    j = i - 2
                    act.wait_ge(post_scaled, j + 1)
                    act.activation(xn_hi[:, pair(j), X], z[:, pair(j), :], ACT.Copy).then_inc(post_hi, 1)

        def post_pe(pe):
            for i in range(4):
                pe.wait_ge(post_sq, i + 1)
                pe.matmul(bank(4 + i), headones[:, :], OSQ[:, pair(i), :], start=True, stop=True).then_inc(post_sum, 1)

        def post_dve(dve):
            for i in range(4):
                dve.wait_ge(post_sq, i + 1)
                for k in range(2 * i, 2 * i + 2):
                    dve.scalar_tensor_tensor(z[:, k, :], z[:, k, :], col("head_gain", k), z[:, RG + k, :], ALU.mult, ALU.mult).then_inc(post_gated, 1)

            def low(i):
                dve.wait_ge(post_hi, i + 1)
                dve.tensor_tensor(xn_lo[:, pair(i), X], z[:, pair(i), :], xn_hi[:, pair(i), X].bitcast(F32), ALU.subtract).then_inc(post_lo, 1)

            def mean_of(i):
                dve.wait_ge(post_sum, i + 1)
                dve.tensor_scalar(OSUM[:, pair(i), :], one_bank(4 + i, T), 1.0 / HD, EPS, ALU.mult, ALU.add).then_inc(post_mean, 1)

            mean_of(0)
            for i in range(4):
                if i < 3:
                    mean_of(i + 1)
                y, v, tmp = OSQ[:, pair(i), :], OSUM[:, pair(i), :], OTMP[:, pair(i), :]
                dve.wait_ge(post_guess, i + 1)
                dve.scalar_tensor_tensor(tmp, y, -0.5, y, ALU.mult, ALU.mult).then_inc(post_step, 1)
                dve.wait_ge(post_mean, i + 1)
                dve.wait_ge(post_step, 3 * i + 1)
                dve.tensor_tensor(tmp, tmp, v, ALU.mult).then_inc(post_step, 1)
                dve.wait_ge(post_step, 3 * i + 2)
                dve.scalar_tensor_tensor(y, tmp, 1.5, y, ALU.add, ALU.mult).then_inc(post_step, 1)
                dve.wait_ge(post_step, 3 * i + 3)
                dve.wait_ge(post_gated, 2 * i + 2)
                dve.tensor_tensor(z[:, pair(i), :], z[:, pair(i), :], y, ALU.mult).then_inc(post_scaled, 1)
                if i:
                    low(i - 1)
            low(3)

        at_scores, at_max, at_exp, at_norm, at_turn, at_pt, at_out, at_hi, at_lo, at_top, at_inverse = (sem(x) for x in (
            "att_scores", "att_max", "att_probs", "att_scaled", "att_turned", "att_turned_out", "att_out", "att_hi",
            "att_lo", "att_row_max", "att_inverse_sum"))
        at_col = small[:, cols["att"]:cols["att"] + 8]
        SCORES = (0, 1, 6)
        PROB = [work[:, i * 512:(i + 1) * 512] for i in range(2)]
        PT = [area(1024 + i * 1024, 4, T) for i in range(2)]

        class Attention:
            units, heads_before = 0, 0

            def __init__(self, heads, parts, keys, q, k, v):
                self.heads, self.parts, self.keys, self.q, self.k, self.v = heads, parts, keys, q, k, v
                self.scale = (parts * P) ** -0.5
                self.u0, self.h0 = Attention.units, Attention.heads_before
                Attention.units += 2 * heads
                Attention.heads_before += heads

            def pe(self, pe):
                key_tiles = self.keys // P

                def scores(u):
                    h, tt = u // 2, u % 2
                    if u >= 3:
                        pe.wait_ge(at_exp, self.u0 + u - 2)
                    for i in range(self.parts):
                        mm = pe.matmul(psum[:, SCORES[u % 3], 0:self.keys], self.q(h, i)[:, tt * P:(tt + 1) * P], self.k(h, i),
                                       start=(i == 0), stop=(i == self.parts - 1))
                    mm.then_inc(at_scores, 1)

                scores(0)
                scores(1)
                for u in range(2 * self.heads):
                    h, tt = u // 2, u % 2
                    if u + 2 < 2 * self.heads:
                        scores(u + 2)
                    pe.wait_ge(at_norm, self.u0 + u + 1)
                    if u >= 2:
                        pe.wait_ge(at_pt, self.u0 + u - 1)
                    for j in range(key_tiles):
                        mm = pe.transpose(psum[:, 2 + u % 2, j * P:(j + 1) * P], PROB[u % 2][:, j * P:(j + 1) * P], ident[:, :])
                    mm.then_inc(at_turn, 1)
                    if tt:
                        pe.wait_ge(at_pt, self.u0 + u + 1)
                        if h >= 2:
                            pe.wait_ge(at_lo, self.h0 + h - 1)
                        for i in range(self.parts):
                            for j in range(key_tiles):
                                mm = pe.matmul(psum[:, 4 + h % 2, i * T:(i + 1) * T], self.v(h, j)[:, i * P:(i + 1) * P],
                                               PT[h % 2][:, j, :], start=(j == 0), stop=(j == key_tiles - 1))
                        mm.then_inc(at_out, 1)

            def act(self, act):
                def turned(u):
                    h, tt = u // 2, u % 2
                    act.wait_ge(at_turn, self.u0 + u + 1)
                    if h >= 2 and tt == 0:
                        act.wait_ge(at_out, self.h0 + h - 1)
                    act.activation(PT[h % 2][:, 0:self.keys // P, tt * P:(tt + 1) * P],
                                   psum[:, 2 + u % 2, 0:self.keys].rearrange("p (j t) -> p j t", t=P), ACT.Copy).then_inc(at_pt, 1)

                def out_hi(h):
                    act.wait_ge(at_out, self.h0 + h + 1)
                    act.activation(xn_hi[:, self.parts * h:self.parts * (h + 1), X],
                                   psum[:, 4 + h % 2, 0:self.parts * T].rearrange("p (i t) -> p i t", t=T), ACT.Copy).then_inc(at_hi, 1)

                for u in range(2 * self.heads):
                    act.wait_ge(at_max, self.u0 + u + 1)
                    if u >= 2:
                        act.wait_ge(at_turn, self.u0 + u - 1)
                    act.activation(PROB[u % 2][:, 0:self.keys], psum[:, SCORES[u % 3], 0:self.keys], ACT.Exp, scale=self.scale,
                                   bias=at_col[:, u % 2:u % 2 + 1], accum_out=at_col[:, 2 + u % 2:3 + u % 2]).then_inc(at_exp, 1)
                    if u:
                        turned(u - 1)
                    if u >= 3 and u % 2:
                        out_hi((u - 3) // 2)
                turned(2 * self.heads - 1)
                out_hi(self.heads - 1)

            def dve(self, dve):
                def out_lo(h):
                    dve.wait_ge(at_hi, self.h0 + h + 1)
                    o = xn_hi[:, self.parts * h:self.parts * (h + 1), X].bitcast(F32)
                    dve.tensor_tensor(xn_lo[:, self.parts * h:self.parts * (h + 1), X],
                                      psum[:, 4 + h % 2, 0:self.parts * T].rearrange("p (i t) -> p i t", t=T), o,
                                      ALU.subtract).then_inc(at_lo, 1)

                def row_max(u):
                    dve.wait_ge(at_scores, self.u0 + u + 1)
                    top, bias = at_col[:, 4 + u % 2:5 + u % 2], at_col[:, u % 2:u % 2 + 1]
                    dve.tensor_reduce(top, psum[:, SCORES[u % 3], 0:self.keys], AX_X, ALU.max).then_inc(at_top, 1)
                    dve.wait_ge(at_top, self.u0 + u + 1)
                    dve.tensor_scalar(bias, top, -self.scale, None, ALU.mult).then_inc(at_max, 1)

                row_max(0)
                for u in range(2 * self.heads):
                    if u + 1 < 2 * self.heads:
                        row_max(u + 1)
                    dve.wait_ge(at_exp, self.u0 + u + 1)
                    inverse = at_col[:, 6 + u % 2:7 + u % 2]
                    dve.reciprocal(inverse, at_col[:, 2 + u % 2:3 + u % 2]).then_inc(at_inverse, 1)
                    dve.wait_ge(at_inverse, self.u0 + u + 1)
                    dve.tensor_scalar(PROB[u % 2][:, 0:self.keys], PROB[u % 2][:, 0:self.keys], inverse, None, ALU.mult).then_inc(at_norm, 1)
                    if u >= 3 and u % 2:
                        out_lo((u - 3) // 2)
                out_lo(self.heads - 1)

        def run_act(act, job, evac, splits=True, counts=False):
            for s in steps(act, job, 2):
                if splits or s.is_mod:
                    split_hi(act, s)
                if counts:
                    act.wait_ge(evacuated, job.base if job.mod_at is None else s.g)
                if evac is not None and not s.is_mod:
                    evac(s)

        def run_dve(dve, job, evac, splits=True):
            for s in steps(dve, job, 2):
                if splits or s.is_mod:
                    split_lo(dve, s)
                if s.is_mod:
                    dve.wait_ge(evacuated, s.g)
                    mod_rows(dve, s)
                elif evac is not None:
                    dve.wait_ge(evacuated, job.base)
                    evac(s)

        def pairs_of(s, dst, w=2):
            at = s.c * w
            return dst[:, bass.ds(at, w), :] if s.looped else dst[:, at:at + w, :]

        def act_copy_to(act, dst, func=ACT.Copy, w=T):
            def evac(s):
                act.wait_ge(chunk_done, s.g + 1)
                act.activation(pairs_of(s, dst), psum[:, s.bank:s.bank + 2, 0:w], func).then_inc(evacuated, 1)
            return evac

        def act_tokens_to(act, dst, func=ACT.Copy):
            tiles = dst.shape[1]

            def evac(s):
                act.wait_ge(chunk_done, s.g + 1)
                at = s.c * 256
                out = dst[:, :, bass.ds(at, 256)] if s.looped else dst[:, :, at:at + 256]
                got = psum[:, s.bank:s.bank + 2, :].rearrange("p b (n f) -> p (b n) f", f=256)[:, 0:tiles, :]
                act.activation(out, got, func).then_inc(evacuated, 1)
            return evac

        def dve_add_gated(dve, tiles, gate, halves):
            def evac(s):
                dve.wait_ge(chunk_done, s.g + 1)
                for n in range(tiles):
                    k = s.c * tiles + n
                    tile = bass.ds(k, 1) if s.looped else slice(k, k + 1)
                    for h in range(halves):
                        t = slice(h * T, (h + 1) * T)
                        x, got = xc[:, tile, t], psum[:, s.bank + n:s.bank + n + 1, t]
                        if gate is None:
                            mm = dve.tensor_tensor(x, x, got, ALU.add)
                        else:
                            mm = dve.scalar_tensor_tensor(x, got, gate[:, tile, h], x, ALU.mult, ALU.add)
                mm.then_inc(evacuated, 1)
            return evac

        ff_gate, ff_hi, ff_lo, ff_conv, ff_tap = (sem(x) for x in (
            "ff_gate", "ff_hi", "ff_lo", "ff_convolved", "ff_newest_tap"))
        later = ExitStack()
        mix.close()
        h_hi = sb("h_hi", [P, HALF, 2 * T], F32R, scope=later)
        h_lo = sb("h_lo", [P, HALF, 2 * T], F32R, scope=later)
        fbuf = [work[:, 4096 + i * 1024:4096 + (i + 1) * 1024].rearrange("p (n t) -> p n t", n=2) for i in range(SLOTS)]

        def packed(s):
            return s.job.packed_last is not None and not s.looped and s.static == s.job.n - 1

        class Feed:
            chunks = 0

            def __init__(self, name, norm, w, gate, conv=None):
                self.name, self.norm, self.w, self.gate, self.conv = name, norm, w, gate, conv
                self.bases = [Feed.chunks, Feed.chunks + HALF]
                Feed.chunks += FF_TILES

            def pe(self, pe):
                for half in range(2):
                    base = self.bases[half]
                    up, down = jobs[f"{self.name}_up{half}"], jobs[f"{self.name}_down{half}"]

                    norm_k = self.norm.ready_at_first(pe)
                    pe_feature_major(pe, up, xn_hi, xn_lo, slice(0, self.w), before_k=norm_k if half == 0 else None)

                    def hidden_k(s, k):
                        if (s.u if s.looped else s.static) == 0 and k in (0, HALF - 1):
                            pe.wait_ge(ff_lo, base + (HALF - 1 if k == 0 else HALF))

                    pe_feature_major(pe, down, h_hi, h_lo, slice(0, self.w), n_tiles=1, k_tiles=HALF, before_k=hidden_k,
                                     last_rows=HD if up.packed_last is not None else P)

            def act(self, act, then):
                for half in range(2):
                    base, job = self.bases[half], jobs[f"{self.name}_up{half}"]

                    def evac(s):
                        b = fbuf[s.slot]
                        n = s.c + base
                        r = slice(0, HD if packed(s) else P)
                        act.wait_ge(chunk_done, s.g + 1)
                        if s.looped or n >= 2:
                            act.wait_ge(ff_lo, n - 1)
                        if self.conv is None:
                            act.activation(b[r, 0, 0:self.w], psum[r, s.bank, 0:self.w], ACT.Silu).then_inc(ff_gate, 1)
                        else:
                            k = s.c + half * HALF
                            for i in range(2):
                                tap = small[:, bass.ds(k + (cols["ff_conv2"] + i * FF_TILES), 1)] if s.looped else col("ff_conv2", k + i * FF_TILES)
                                act.activation(b[:, i, 0:T], psum[:, s.bank + i, 0:T], ACT.Copy, scale=tap).then_inc(ff_tap, 1)
                            split_hi(act, s)
                            act.wait_ge(ff_conv, n * 4 + 2)
                            act.activation(b[:, 0, 0:T], b[:, 0, 0:T], ACT.Silu).then_inc(ff_gate, 1)
                        act.wait_ge(evacuated, s.g + 1)
                        out = h_hi[:, bass.ds(s.c, 1), 0:self.w] if s.looped else h_hi[r, s.c:s.c + 1, 0:self.w]
                        act.activation(out, b[r, 1:2, 0:self.w], ACT.Copy).then_inc(ff_hi, 1)

                    run_act(act, job, evac, splits=self.conv is None)
                    run_act(act, jobs[f"{self.name}_down{half}"], then.act_squares_after(act) if half else None)

            def dve(self, dve):
                for half in range(2):
                    base, job = self.bases[half], jobs[f"{self.name}_up{half}"]

                    def evac(s):
                        b = fbuf[s.slot]
                        n = s.c + base
                        if self.conv is not None:
                            k = s.c + half * HALF
                            for i in range(2):
                                dve.wait_ge(ff_tap, n * 2 + (i + 1))
                                for back in (1, 2):
                                    name = f"ff_conv{2 - back}"
                                    tap = small[:, bass.ds(k + (cols[name] + i * FF_TILES), 1)] if s.looped else col(name, k + i * FF_TILES)
                                    if back == 2:
                                        dve.wait_ge(ff_conv, n * 4 + (2 * i + 1))
                                    dve.scalar_tensor_tensor(b[:, i, back:T], psum[:, s.bank + i, 0:T - back], tap, b[:, i, back:T],
                                                             ALU.mult, ALU.add).then_inc(ff_conv, 1)
                            up = b[:, 1, 0:T]
                        else:
                            up = psum[:, s.bank + 1, 0:self.w]
                        dve.wait_ge(ff_gate, n + 1)
                        if self.conv is not None:
                            dve.wait_ge(ff_conv, n * 4 + 4)
                        r, up_r = (slice(0, HD), slice(HD, P)) if packed(s) else (slice(0, P), slice(0, P))
                        if packed(s):
                            up = psum[:, s.bank, 0:self.w]
                        dve.tensor_tensor(b[r, 1, 0:self.w], b[r, 0, 0:self.w], up[up_r], ALU.mult).then_inc(evacuated, 1)
                        if self.conv is not None:
                            split_lo(dve, s)

                    run_dve(dve, job, evac, splits=self.conv is None)
                    run_dve(dve, jobs[f"{self.name}_down{half}"], dve_add_gated(dve, 1, self.gate, self.w // T))

            def pool(self, pool):
                for half in range(2):
                    base, job = self.bases[half], jobs[f"{self.name}_up{half}"]
                    for s in steps(pool, job, 2):
                        if s.is_mod:
                            continue
                        n = s.c + base
                        b = fbuf[s.slot]
                        pool.wait_ge(ff_hi, n + 1)
                        r = slice(0, HD if packed(s) else P)
                        lo = h_lo[:, bass.ds(s.c, 1), 0:self.w] if s.looped else h_lo[r, s.c:s.c + 1, 0:self.w]
                        hi = h_hi[:, bass.ds(s.c, 1), 0:self.w] if s.looped else h_hi[r, s.c:s.c + 1, 0:self.w]
                        pool.tensor_tensor(lo, b[r, 1:2, 0:self.w], hi.bitcast(F32), ALU.subtract).then_inc(ff_lo, 1)

        mod_act, mod_dve, mod_turned = (sem(x) for x in ("mod_inputs", "mod_prepared", "mod_turned"))
        MOD_TAKEN = (17, 37, 38, 58, 70, 72)
        MOD_READ = (3, 6, 10, 11, 14, 16)

        def mod_turn(pe, m):
            at = m * 4
            for n in range(2):
                out = psum[:, 7, bass.ds(at + n * 2, 2)] if not isinstance(at, int) else psum[:, 7, at + n * 2:at + n * 2 + 2]
                mm = pe.matmul(out, mrow[:, n * P:(n + 1) * P], row_sums[:, :], start=True, stop=True)
            mm.then_inc(mod_turned, 1)

        def mod_pe(pe, s):
            if s.looped or s.m > 0:
                pe.wait_ge(evacuated, s.g - 1)
                mod_turn(pe, s.m - 1)
            else:
                pe.wait_ge(mod_dve, 2)
            pe.wait_ge(lo_ready, s.g + 1)
            for k in range(KT):
                w = slice(k * 256, (k + 1) * 256)
                pe.matmul(psum[0:4, s.bank, 0:256], c4[:, k, :], w_hi[:, s.slot, w], start=(k == 0), stop=False)
                mm = pe.matmul(psum[0:4, s.bank, 0:256], c4[:, k, :], w_lo[:, s.slot, w], start=False, stop=(k == KT - 1))
            mm.then_inc(chunk_done, 1)

        def mod_last_turn(pe):
            pe.wait_ge(evacuated, jobs["k2"].base + 1)
            mod_turn(pe, mod_chunks - 1)

        def mod_rows(dve, s):
            dve.wait_ge(chunk_done, s.g + 1)
            if s.looped or s.m > 0:
                dve.wait_ge(mod_turned, s.m)
            dve.tensor_copy(mrow[0:4, :], psum[0:4, s.bank, 0:256]).then_inc(evacuated, 1)

        def mod_scalar(act):
            act.wait_ge(start_in, 16 * len(START))
            act.activation(c_in[:, :, :], c_in[:, :, :], ACT.Silu).then_inc(mod_act, 1)
            act.wait_ge(mod_act, 1)
            act.activation(c4[:, :, :].rearrange("p k (w l) -> p k w l", l=2)[:, :, :, 0], c_in[:, :, :], ACT.Copy).then_inc(mod_act, 1)

        def mod_vector(dve):
            dve.memset(mrow[:, :], 0.0).then_inc(mod_dve, 1)
            dve.wait_ge(mod_act, 2)
            hl = c4[:, :, :].rearrange("p k (w l) -> p k w l", l=2)
            dve.tensor_tensor(hl[:, :, :, 1], c_in[:, :, :], hl[:, :, :, 0].bitcast(F32), ALU.subtract).then_inc(mod_dve, 1)

        mod_ready = [2]

        def mod_columns(dve, call, norms):
            a, b = ((0,) + MOD_TAKEN)[call:call + 2]
            dve.wait_ge(mod_turned, b)
            dve.tensor_tensor(mods[:, 2 * a:2 * b, :], psum[:, 7, 4 * a:4 * b].rearrange("p (n w) -> p n w", w=2),
                              b_mod[:, 2 * a:2 * b].unsqueeze(2).to_broadcast([P, 2 * (b - a), 2]), ALU.add).then_inc(mod_dve, 1)
            mod_ready[0] += 1
            assert mod_ready[0] == MOD_READ[call]
            dve.wait_ge(mod_dve, mod_ready[0])
            for ln in norms:
                at = (ln // 3) * 72 + (ln % 3) * 24
                dve.scalar_tensor_tensor(scales[:, ln, :, :], mods[:, at + 8:at + 16, :], 1.0,
                                         gains[:, ln, :].unsqueeze(2).to_broadcast([P, KT, 2]), ALU.add, ALU.mult).then_inc(mod_dve, 1)
                mod_ready[0] += 1
                if ln % 3 != 1:
                    dve.tensor_scalar(mods[:, at + 16:at + 24, :], mods[:, at + 16:at + 24, :], 0.5, None, ALU.mult).then_inc(mod_dve, 1)
                    mod_ready[0] += 1
            dve.wait_ge(mod_dve, mod_ready[0])

        def modulated(ln, span, tiles=1, direct=None):
            at = (ln // 3) * 72 + (ln % 3) * 24
            return Norm(span, lambda k, h: scales[:, ln, k, h:h + 1], lambda k, h: mods[:, at + k, h:h + 1], tiles=tiles, direct=direct)

        def gate_of(ln):
            at = (ln // 3) * 72 + (ln % 3) * 24 + 16
            return mods[:, at:at + KT, :]

        later.close()
        l0 = ExitStack()
        a_t, u_t, v_t = (sb(n, [P, 4, 2 * T], scope=l0) for n in ("a_t", "u_t", "v_t"))
        dft_c = sb("dft_c", [P, 2 * P], scope=l0)
        dft_cos = sb("dft_cos", [P, 2, T], scope=l0)
        dft_sin = sb("dft_sin", [P, 2, T], scope=l0)
        ws_t = sb("ws_t", [P, 4, P], scope=l0)
        bs_row = sb("bs_row", [P, 4, P], scope=l0)
        gv_row = sb("gv_row", [P, 4, P], scope=l0)
        L0_TABLES = dict(dft_c=dft_c, dft_cos=dft_cos, dft_sin=dft_sin, ws_t=ws_t, bs_row=bs_row, gv_row=gv_row)
        o_t = area(0, KT, 2 * T)
        mid = [area(4096 + i * 512, 2, T) for i in range(2)]
        vsq = work[:, 5120:7168].rearrange("p (n f) -> p n f", f=P)
        vst = work[:, 7168:7184]
        vst2, vst3 = work[:, 7184:7200], work[:, 7200:7216]
        l0_tables_in, f_mid, f_mid_out, f_sum, f_sum_out, g_dve, g_act, g_pe, o_hi, o_lo = (sem(x) for x in (
            "l0_tables_in", "fourier_channels", "fourier_channels_out", "fourier_tokens", "fourier_tokens_out", "gating_dve",
            "gating_rsqrt", "gating_mixed", "branch_hi", "branch_lo"))

        def branch_pe(pe, norm):
            pe_feature_major(pe, jobs["ab_a"], xn_hi, xn_lo, XC, before_k=norm.ready_at_first(pe))
            pe_feature_major(pe, jobs["ab_u"], xn_hi, xn_lo, XC)
            pe_token_major(pe, jobs["ab_v"], XC)
            pe.wait_ge(evacuated, jobs["ab_v"].base + 2)
            pe.wait_ge(l0_tables_in, 16 * len(L0_TABLES))

            def channels(j):
                q, g = j // 4, j % 4
                if j >= 2:
                    pe.wait_ge(f_mid_out, j - 1)
                for nt in range(2):
                    mm = pe.matmul(psum[:, j % 2, nt * T:(nt + 1) * T], a_t[:, g, q * T + nt * P:q * T + (nt + 1) * P], dft_c[:, :],
                                   start=True, stop=True)
                mm.then_inc(f_mid, 1)

            channels(0)
            for j in range(8):
                if j + 1 < 8:
                    channels(j + 1)
                pe.wait_ge(f_mid_out, j + 1)
                if j >= 2:
                    pe.wait_ge(f_sum_out, j - 1)
                for nt in range(2):
                    pe.matmul(psum[:, 2 + j % 2, 0:T], mid[j % 2][:, nt, 0:P], dft_cos[:, nt, :], start=(nt == 0), stop=False)
                    mm = pe.matmul(psum[:, 2 + j % 2, 0:T], mid[j % 2][:, nt, P:T], dft_sin[:, nt, :], start=False, stop=(nt == 1))
                mm.then_inc(f_sum, 1)
            pe.wait_ge(g_dve, 8)
            for tt in range(4):
                for g in range(4):
                    mm = pe.matmul(psum[:, 4 + g, tt * P:(tt + 1) * P], v_t[:, tt, g * P:(g + 1) * P], ws_t[:, g, :], start=True, stop=True)
            mm.then_inc(g_pe, 1)
            pe.wait_ge(g_dve, 12)

            def branches_k(s, k):
                if s.static == 0 and k in (0, 4, 6):
                    pe.wait_ge(o_lo, max(1, k // 2))
            pe_feature_major(pe, jobs["ab_out"], xn_hi, xn_lo, XC, before_k=branches_k)

        def branch_act(act, norm, then):
            for name in L0_TABLES:
                act.dma_start(L0_TABLES[name][:], io[name]).then_inc(l0_tables_in, 16)
            norm.act_rest(act)
            run_act(act, jobs["ab_a"], act_copy_to(act, a_t, w=2 * T), counts=True)
            run_act(act, jobs["ab_u"], act_copy_to(act, u_t, ACT.Gelu_apprx_tanh, w=2 * T), counts=True)
            run_act(act, jobs["ab_v"], act_tokens_to(act, v_t, ACT.Gelu_apprx_tanh), counts=True)
            act.wait_ge(g_dve, 3)
            act.activation(vst2, vst, ACT.Abs_reciprocal_sqrt).then_inc(g_act, 1)
            for j in range(8):
                act.wait_ge(f_mid, j + 1)
                if j >= 2:
                    act.wait_ge(f_sum, j - 1)
                act.activation(mid[j % 2], psum[:, j % 2, :].rearrange("p (n t) -> p n t", n=2), ACT.Copy).then_inc(f_mid_out, 1)
            act.wait_ge(f_sum_out, 8)
            act.activation(xn_hi[:, 0:4, :], o_t[:, 0:4, :], ACT.Copy).then_inc(o_hi, 1)
            for i in range(2):
                act.wait_ge(g_dve, 10 + 2 * i)
                k = slice(4 + 2 * i, 6 + 2 * i)
                act.activation(xn_hi[:, k, :], o_t[:, k, :], ACT.Copy).then_inc(o_hi, 1)
            run_act(act, jobs["ab_out"], then.act_squares_after(act))

        def branch_dve(dve, norm):
            norm.dve(dve)
            for name in ("ab_a", "ab_u", "ab_v"):
                run_dve(dve, jobs[name], None)
            mod_columns(dve, 2, ())
            n = 0

            def o(ins):
                nonlocal n
                n += 1
                ins.then_inc(g_dve, 1)
                dve.wait_ge(g_dve, n)
            v = v_t[:, :, :].rearrange("p n (g f) -> p (n g) f", f=P)
            dve.wait_ge(evacuated, jobs["ab_v"].base + 2)
            dve.wait_ge(l0_tables_in, 16 * len(L0_TABLES))
            o(dve.tensor_tensor(vsq, v, v, ALU.mult))
            o(dve.tensor_reduce(vst3, vsq, AX_X, ALU.add))
            o(dve.tensor_scalar(vst, vst3, 1.0 / P, EPS, ALU.mult, ALU.add))
            dve.wait_ge(g_act, 1)
            o(dve.scalar_tensor_tensor(vst3, vst2, -0.5, vst2, ALU.mult, ALU.mult))
            o(dve.tensor_tensor(vst3, vst3, vst, ALU.mult))
            o(dve.scalar_tensor_tensor(vst2, vst3, 1.5, vst2, ALU.add, ALU.mult))
            o(dve.tensor_tensor(v, v, vst2.unsqueeze(2).to_broadcast([P, 16, P]), ALU.mult))
            gv = gv_row[:, :, :].unsqueeze(1).to_broadcast([P, 4, 4, P])
            v4 = v_t[:, :, :].rearrange("p n (g f) -> p n g f", f=P)
            o(dve.tensor_tensor(v4, v4, gv, ALU.mult))
            for j in range(8):
                dve.wait_ge(f_sum, j + 1)
                dve.tensor_copy(o_t[:, j % 4, (j // 4) * T:(j // 4 + 1) * T], psum[:, 2 + j % 2, 0:T]).then_inc(f_sum_out, 1)

            def low(i, k):
                dve.wait_ge(o_hi, i + 1)
                dve.tensor_tensor(xn_lo[:, k, :], o_t[:, k, :], xn_hi[:, k, :].bitcast(F32), ALU.subtract).then_inc(o_lo, 1)

            low(0, slice(0, 4))
            dve.wait_ge(g_pe, 1)
            for i in range(2):
                k = slice(4 + 2 * i, 6 + 2 * i)
                gated = o_t[:, k, :].rearrange("p g (n t) -> p g n t", t=P)
                bs = bs_row[:, 2 * i:2 * i + 2, :].unsqueeze(2).to_broadcast([P, 2, 4, P])
                o(dve.tensor_tensor(gated, psum[:, k, :].rearrange("p g (n t) -> p g n t", t=P), bs, ALU.add))
                o(dve.tensor_tensor(o_t[:, k, :], o_t[:, k, :], u_t[:, 2 * i:2 * i + 2, :], ALU.mult))
            for i in range(2):
                low(1 + i, slice(4 + 2 * i, 6 + 2 * i))
            run_dve(dve, jobs["ab_out"], dve_add_gated(dve, 2, gate_of(1), 2))

        l0.close()
        l1 = ctx.enter_context(ExitStack())
        qk12 = sb("qk12", [P, 12, T], scope=l1)
        qk_tmp = sb("qk_tmp", [P, 12, T], scope=l1)
        v2 = sb("v2", [P, 4, T], scope=l1)
        ax_cos, ax_sin = sb("ax_cos", [P, T], scope=l1), sb("ax_sin", [P, T], scope=l1)
        ax_in, r_sq, r_sum, r_mean, r_guess, r_dve, r_unit, r_turned, r_done = (sem(x) for x in (
            "axial_in", "qk_squares", "qk_sums", "qk_mean_squares", "qk_guess", "qk_dve", "qk_unit", "qk_turned", "qk_rotated"))

        def four(i):
            return slice(4 * i, 4 * i + 4)

        qk_mean, qk_rstd = work[:, 0:12 * T].rearrange("p (n t) -> p n t", t=T), work[:, 12 * T:24 * T].rearrange("p (n t) -> p n t", t=T)
        kx = qk12[:, 8:12, :].rearrange("p (h w) t -> p h w t", w=2)[:, :, 0, :]
        k_all = qk12[:, 8:12, :].rearrange("p (h w) t -> p h (w t)", w=2)

        first = Norm(X, lambda k, h: col("mix_norm_w", k), direct=5)
        memory = Norm(C, lambda k, h: col("mem_norm_w", k), tiles=2, pool_low=True)
        cross = Norm(X, lambda k, h: col("xattn_norm_w", k), tiles=2)
        ffn = Norm(X, lambda k, h: col("ffn_norm_w", k), tiles=2)
        between = Norm(X, lambda k, h: col("final_norm_w", k), out=xc[:, :, X])
        n20, n21 = modulated(0, XC, direct=5), modulated(1, XC)
        n22, n23, n24 = modulated(2, XC, 2), modulated(3, XC), modulated(4, XC)
        n25 = modulated(5, X, 2)
        last = Norm(X, lambda k, h: col("g_final", k), out=nrm)
        feed0 = Feed("ffn", ffn, T, None, conv=True)
        feed1 = Feed("a1", n20, 2 * T, gate_of(0))
        feed2 = Feed("a2", n22, 2 * T, gate_of(2))
        feed3 = Feed("b1", n23, 2 * T, gate_of(3))
        feed4 = Feed("b2", n25, T, gate_of(5))
        k1, v1, q1 = z[:, 0:8, :], z[:, 8:16, :].rearrange("p (n a) t -> p n (a t)", n=2), z[:, 16:24, :]
        att1 = Attention(4, 2, T, lambda h, i: q1[:, 2 * h + i, :], lambda h, i: k1[:, 2 * h + i, :], lambda h, j: v1[:, j, h * T:(h + 1) * T])
        att2 = Attention(8, 1, 2 * T, lambda h, i: qk12[:, h, :], lambda h, i: k_all[:, h // 4, :], lambda h, j: v2[:, j, (h // 4) * P:(h // 4 + 1) * P])
        START = dict(small=small, ident=ident, ones=ones, rot=rot, row_sums=row_sums, gains=gains, b_mod=b_mod, c_in=c_in)
        residual_in, mem_in, out_in, set_up = sem("residual_in"), sem("mem_in"), sem("out_stored"), sem("constants_set")

        block = ctx.enter_context(nc.Block())

        @block.sync
        def _(sp):
            sp.dma_start(xc[:, :, X], io["x"]).then_inc(residual_in, 16)
            for name in START:
                sp.dma_start(START[name][:], io[name]).then_inc(start_in, 16)
            for n, (name, *_) in enumerate(plan):
                for s in steps(sp, jobs[name]):
                    load(sp, s)
                    if n == 0 and s.static == SLOTS - 1:
                        sp.dma_start(xc[:, :, C], io["mem"]).then_inc(mem_in, 16)
                if n == 0:
                    load_mixer_tables(sp)
            sp.wait_ge(n_scaled, last.scaled_base + KT)
            sp.dma_start(io["out"], nrm[:, :, X]).then_inc(out_in, 16)
            sp.wait_ge(out_in, 16)

        @block.tensor
        def _(pe):
            pe.wait_ge(start_in, 16 * len(START))
            pe.wait_ge(set_up, 1)
            first.pe(pe)
            pe_feature_major(pe, jobs["w_in_a"], xn_hi, xn_lo, X, before_k=first.ready_at_first(pe))
            pe_feature_major(pe, jobs["w_in_b"], xn_hi, xn_lo, X)
            pe_feature_major(pe, jobs["w_in_small"], xn_hi, xn_lo, X, n_tiles=1)
            memory.pe(pe)
            pe_feature_major(pe, jobs["w_in_g"], xn_hi, xn_lo, X)
            retention_pe(pe)
            gated_order = order(pe, "gat_pe")
            delta_pe(pe, lambda: gated_order(pe.matmul(psum[:, 7, 0:T], gk_up[64:80, :], zs[64:80, :], start=True, stop=True), "gk"))
            gated_pe(pe, gated_order)
            post_pe(pe)
            def mixed_k(s, k):
                if s.static == 1 and k % 2 == 0:
                    pe.wait_ge(post_lo, k // 2 + 1)
            pe_feature_major(pe, jobs["w_out"], xn_hi, xn_lo, X, before_k=mixed_k)
            memory.ready(pe, KT - 1)
            pe_feature_major(pe, jobs["wk"], xn_hi, xn_lo, C)
            cross.pe(pe)
            pe_token_major(pe, jobs["wv"], C)
            cross.ready(pe, KT - 1)
            pe_feature_major(pe, jobs["wq"], xn_hi, xn_lo, X)
            pe.wait_ge(evacuated, jobs["wq"].base + jobs["wq"].n)
            att1.pe(pe)
            pe.wait_ge(at_lo, att1.heads)
            pe_feature_major(pe, jobs["wo"], xn_hi, xn_lo, X)
            ffn.pe(pe)
            feed0.pe(pe)
            between.pe(pe)
            n20.pe(pe)
            pe.wait_ge(mod_dve, MOD_READ[0])
            feed1.pe(pe)
            n21.pe(pe)
            pe.wait_ge(mod_dve, MOD_READ[1])
            branch_pe(pe, n21)
            n22.pe(pe)
            feed2.pe(pe)
            n23.pe(pe)
            pe.wait_ge(mod_dve, MOD_READ[3])
            feed3.pe(pe)
            n24.pe(pe)
            pe.wait_ge(mod_dve, MOD_READ[4])
            pe_feature_major(pe, jobs["k2"], xn_hi, xn_lo, XC, before_k=n24.ready_at_first(pe))
            mod_last_turn(pe)
            pe_feature_major(pe, jobs["q2"], xn_hi, xn_lo, X)
            pe_token_major(pe, jobs["v2"], XC)
            for i in range(3):
                pe.wait_ge(r_sq, i + 1)
                for j in range(2):
                    mm = pe.matmul(bank(2 * i + j), ones[:, :], qk_tmp[:, 4 * i + 2 * j:4 * i + 2 * j + 2, :], start=True, stop=True)
                mm.then_inc(r_sum, 1)
            for i in range(3):
                pe.wait_ge(r_unit, i + 1)
                if i < 2:
                    for j in range(2):
                        mm = pe.matmul(bank(2 * i + j), rot[:, :], qk12[:, 4 * i + 2 * j:4 * i + 2 * j + 2, :], start=True, stop=True)
                else:
                    mm = pe.matmul(bank(4), rot[:, :], kx, start=True, stop=True)
                mm.then_inc(r_turned, 1)
            pe.wait_ge(r_done, 3)
            att2.pe(pe)
            pe.wait_ge(at_lo, att1.heads + att2.heads)
            pe_feature_major(pe, jobs["wo2"], xn_hi, xn_lo, X)
            n25.pe(pe)
            feed4.pe(pe)
            last.pe(pe)

        @block.scalar
        def _(act):
            act.wait_ge(residual_in, 16)
            first.act_squares(act)
            act.wait_ge(start_in, 16 * len(START))
            first_splits(act, split_hi)
            first.act_rest(act)
            run_act(act, jobs["w_in_a"], act_copy_to(act, z), counts=True)
            act.wait_ge(mem_in, 16)
            memory.act_squares(act)
            run_act(act, jobs["w_in_b"], act_copy_to(act, z[:, 2 * jobs["w_in_a"].n:2 * (jobs["w_in_a"].n + jobs["w_in_b"].n), :]), counts=True)

            def small_rows(s):
                act.wait_ge(chunk_done, s.g + 1)
                act.activation(zs[:, :], psum[:, s.bank, 0:T], ACT.Copy).then_inc(evacuated, 1)
            run_act(act, jobs["w_in_small"], small_rows, counts=True)
            memory.act_rest(act)
            mod_scalar(act)
            retention_act(act)
            run_act(act, jobs["w_in_g"], act_copy_to(act, z[:, RG:RG + 8, :], ACT.Silu), counts=True)
            delta_act(act)
            gated_act_first(act)
            gated_act(act)
            post_act(act)
            run_act(act, jobs["w_out"], cross.act_squares_after(act))
            run_act(act, jobs["wk"], act_copy_to(act, k1), counts=True)
            cross.act_rest(act)
            run_act(act, jobs["wv"], act_tokens_to(act, v1), counts=True)
            run_act(act, jobs["wq"], act_copy_to(act, q1), counts=True)
            att1.act(act)
            run_act(act, jobs["wo"], ffn.act_squares_after(act))
            ffn.act_rest(act)
            feed0.act(act, between)
            between.act_rest(act)
            act.wait_ge(ctx_in, 16)
            for k in range(KT):
                act.wait_ge(n_scaled, between.scaled_base + k + 1)
                act.activation(nrm[:, k, :], xc[:, k, :], ACT.Square).then_inc(n_sq, 1)
            n20.act_rest(act)
            feed1.act(act, n21)
            branch_act(act, n21, n22)
            n22.act_rest(act)
            feed2.act(act, n23)
            n23.act_rest(act)
            feed3.act(act, n24)
            act.dma_start(ax_cos[:, :], io["ax_cos"]).then_inc(ax_in, 16)
            act.dma_start(ax_sin[:, :], io["ax_sin"]).then_inc(ax_in, 16)
            n24.act_rest(act)

            def keys(s):
                act.wait_ge(chunk_done, s.g + 1)
                act.activation(k_all, psum[:, s.bank:s.bank + 2, :], ACT.Copy).then_inc(evacuated, 1)
            run_act(act, jobs["k2"], keys, counts=True)
            run_act(act, jobs["q2"], act_copy_to(act, qk12[:, 0:8, :]), counts=True)
            run_act(act, jobs["v2"], act_tokens_to(act, v2), counts=True)
            act.wait_ge(evacuated, jobs["v2"].base + 1)
            for i in range(3):
                act.activation(qk_tmp[:, four(i), :], qk12[:, four(i), :], ACT.Square).then_inc(r_sq, 1)
            for i in range(3):
                act.wait_ge(r_mean, i + 1)
                act.activation(qk_rstd[:, four(i), :], qk_mean[:, four(i), :], ACT.Abs_reciprocal_sqrt).then_inc(r_guess, 1)
            act.wait_ge(r_done, 3)
            att2.act(act)
            run_act(act, jobs["wo2"], n25.act_squares_after(act))
            n25.act_rest(act)
            feed4.act(act, last)
            last.act_rest(act)

        @block.vector
        def _(dve):
            dve.memset(zeros[:, :], 0.0).then_inc(set_up, 1)
            dve.wait_ge(set_up, 1)
            first_splits(dve, split_lo)
            dve.wait_ge(start_in, 16 * len(START))
            first.dve(dve)
            for name in ("w_in_a", "w_in_b", "w_in_small"):
                run_dve(dve, jobs[name], None)
            memory.dve(dve)
            retention_order = order(dve, "ret_dve")
            retention_dve_angles(dve, retention_order)
            run_dve(dve, jobs["w_in_g"], None)
            delta_order = order(dve, "gdn_dve")
            retention_dve(dve, retention_order, lambda: delta_dve_first(dve, delta_order))
            gated_order = order(dve, "gat_dve")

            def gated_copy():
                dve.wait_ge(n_scaled, memory.scaled_base + KT)
                gated_order(dve.tensor_copy(U3[:, 1:3, :], z[:, DF:DF + 2, :]), "u")
            delta_dve(dve, delta_order, gated_copy, lambda: gated_gates(dve, gated_order))
            gated_dve(dve, gated_order)
            mod_vector(dve)
            post_dve(dve)
            run_dve(dve, jobs["w_out"], dve_add_gated(dve, 2, None, 1))
            run_dve(dve, jobs["wk"], None)
            cross.dve(dve)
            run_dve(dve, jobs["wv"], None)
            run_dve(dve, jobs["wq"], None)
            att1.dve(dve)
            run_dve(dve, jobs["wo"], dve_add_gated(dve, 2, None, 1))
            ffn.dve(dve)
            feed0.dve(dve)
            between.dve(dve)
            mod_columns(dve, 0, (0,))
            n20.dve(dve)
            feed1.dve(dve)
            mod_columns(dve, 1, (1, 2))
            branch_dve(dve, n21)
            n22.dve(dve)
            feed2.dve(dve)
            mod_columns(dve, 3, (3,))
            n23.dve(dve)
            feed3.dve(dve)
            mod_columns(dve, 4, (4,))
            n24.dve(dve)
            for name in ("k2", "q2", "v2"):
                run_dve(dve, jobs[name], None)
            mod_columns(dve, 5, (5,))
            n = 0

            def o(ins):
                nonlocal n
                n += 1
                ins.then_inc(r_dve, 1)
                dve.wait_ge(r_dve, n)

            def mean_of(i):
                dve.wait_ge(r_sum, i + 1)
                dve.tensor_scalar(qk_mean[:, four(i), :], two_banks(2 * i, T), 1.0 / P, EPS, ALU.mult, ALU.add).then_inc(r_mean, 1)

            dve.wait_ge(ax_in, 32)
            mean_of(0)
            for i in range(3):
                if i < 2:
                    mean_of(i + 1)
                y, v, tmp, qk = qk_rstd[:, four(i), :], qk_mean[:, four(i), :], qk_tmp[:, four(i), :], qk12[:, four(i), :]
                dve.wait_ge(r_guess, i + 1)
                o(dve.scalar_tensor_tensor(tmp, y, -0.5, y, ALU.mult, ALU.mult))
                o(dve.tensor_tensor(tmp, tmp, v, ALU.mult))
                o(dve.scalar_tensor_tensor(y, tmp, 1.5, y, ALU.add, ALU.mult))
                dve.scalar_tensor_tensor(qk, qk, col("g_q" if i < 2 else "g_k"), y, ALU.mult, ALU.mult).then_inc(r_unit, 1)
            for i in range(3):
                w = 4 if i < 2 else 2
                x = qk12[:, four(i), :] if i < 2 else kx
                tmp = qk_tmp[:, 4 * i:4 * i + w, :]
                dve.wait_ge(r_turned, i + 1)
                o(dve.tensor_tensor(tmp, psum[:, 2 * i:2 * i + w // 2, :].rearrange("p b (n t) -> p (b n) t", t=T),
                                    ax_sin[:, :].unsqueeze(1).to_broadcast([P, w, T]), ALU.mult))
                o(dve.tensor_tensor(x, x, ax_cos[:, :].unsqueeze(1).to_broadcast([P, w, T]), ALU.mult))
                dve.tensor_tensor(x, x, tmp, ALU.add).then_inc(r_done, 1)
            att2.dve(dve)
            run_dve(dve, jobs["wo2"], dve_add_gated(dve, 2, gate_of(4), 1))
            n25.dve(dve)
            feed4.dve(dve)
            last.dve(dve)

        @block.gpsimd
        def _(pool):
            first.pool(pool)
            memory.pool(pool)
            memory.pool_lows(pool)
            gated_pool_first(pool)
            gated_pool(pool)
            cross.pool(pool)
            ffn.pool(pool)
            feed0.pool(pool)
            between.pool(pool)
            n20.pool(pool)
            feed1.pool(pool)
            n21.pool(pool)
            n22.pool(pool)
            feed2.pool(pool)
            n23.pool(pool)
            feed3.pool(pool)
            n24.pool(pool)
            n25.pool(pool)
            feed4.pool(pool)
            last.pool(pool)


def shape_tables():
    f64 = np.float64
    i = np.arange(P)
    t = {}
    t["ident"] = np.eye(P)
    t["ones"] = np.ones((P, P))
    rot = np.zeros((P, P))
    for m in range(P):
        if m % 64 < 32:
            rot[m + 32, m] = -1.0
        else:
            rot[m - 32, m] = 1.0
    t["rot"] = rot
    t["row_sums"] = (i[:, None] // 2 == np.arange(2)[None, :]) & (i[:, None] < 4)
    t["headones"] = (i[:, None] // HD == i[None, :] // HD)
    t["lagsel"] = np.stack([i[:, None] // 32 == 2 * j + i[None, :] // HD for j in range(2)], 1)
    t["triu"] = i[:, None] <= i[None, :]
    t["tril_strict"] = i[:, None] > i[None, :]
    t["second_half"] = np.stack([(i[:, None] // (2 * L) == i[None, :] // (2 * L)) & (i[:, None] // L % 2 == 1) & (i[None, :] // L % 2 == 0)
                                 for L in (1, 2, 4, 8, 16, 32, 64)], 1)
    gamma = np.log(1.0 - np.exp2(-5.0 - np.arange(HEADS)))
    rel = np.arange(T)[None, :] - i[:, None]
    t["decay"] = np.stack([np.where(rel >= 0, np.exp(g * np.maximum(rel, 0)), 0.0) * HD ** -0.5 for g in gamma], 1)
    n, c = np.arange(T, dtype=f64), np.arange(P, dtype=f64)
    chan = 2 * np.pi * (np.outer(c, c) % P) / P
    tok = 2 * np.pi * (np.outer(n, n) % T) / T
    t["dft_c"] = np.concatenate([np.cos(chan), -np.sin(chan)], 1)
    for name, f in (("dft_cos", np.cos), ("dft_sin", np.sin)):
        t[name] = (f(tok) / np.sqrt(T * P)).reshape(2, P, T).transpose(1, 0, 2)
    grid_w, axis = 64, HD
    inv = (10000.0 ** (-np.arange(0, axis, 2, dtype=np.float32) / np.float32(axis))).astype(np.float32)
    ang = np.zeros((P, T), np.float32)
    for m in range(P):
        where = (np.arange(T) // grid_w if m < HD else np.arange(T) % grid_w).astype(np.float32)
        ang[m] = where * inv[m % 32]
    t["ax_cos"], t["ax_sin"] = np.cos(ang.astype(f64)), np.sin(ang.astype(f64))
    freqs = (np.float32(10000.0) ** (-np.arange(0, HD, 2, dtype=np.float32) / np.float32(HD))).astype(np.float32)
    t["freq"] = freqs[i % 32][:, None]
    return {k: np.ascontiguousarray(v, dtype=np.float32) for k, v in t.items()}


def features(a):
    a = np.asarray(a)
    return np.moveaxis(a.reshape(a.shape[:-1] + (-1, P)), -1, 0)


def tiles_fm(w, n_tiles=2):
    k, n = w.shape
    a = w.reshape(k // P, P, n // (P * n_tiles), n_tiles, P)
    return np.ascontiguousarray(a.transpose(2, 1, 3, 0, 4)).reshape(n // (P * n_tiles), P, -1)


def tiles_tm(w):
    k, n = w.shape
    return np.ascontiguousarray(w.reshape(k // P, P, n // 256, 256).transpose(2, 1, 0, 3)).reshape(n // 256, P, -1)


def pair_up(w, ff):
    g = np.zeros((2, w.shape[0], FF_TILES * P), np.float32)
    g[0, :, :ff], g[1, :, :ff] = w[:, :ff], w[:, ff:]
    a = g.reshape(2, KT, P, FF_TILES, P)
    return np.ascontiguousarray(a.transpose(3, 2, 0, 1, 4)).reshape(FF_TILES, P, -1)


def down(w):
    g = np.zeros((FF_TILES * P, w.shape[1]), np.float32)
    g[:w.shape[0]] = w
    a = g.reshape(2, HALF, P, KT, P)
    return np.ascontiguousarray(a.transpose(0, 3, 2, 1, 4)).reshape(2, KT, P, -1)


def kernel(**inp):
    import concourse.bacc as bacc
    from concourse.bass_utils import run_bass_kernel_spmd

    inp = {k: np.asarray(v) for k, v in inp.items()}
    nc = bacc.Bacc("TRN2", target_bir_lowering=False, num_devices=1)
    arrays, io = {}, {}

    def give(name, a):
        a = np.ascontiguousarray(a)
        arrays[f"in_{name}"] = a
        io[name] = nc.dram_tensor(f"in_{name}", a.shape, mybir.dt.from_np(a.dtype), kind="ExternalInput").ap()

    tables = shape_tables()
    for name, a in tables.items():
        if name != "freq":
            give(name, a)

    def stream(a):
        return a.reshape(T, KT, P).transpose(2, 1, 0)

    give("x", stream(inp["x"][0]))
    give("mem", stream(inp["mem"][0]))
    give("ctx", stream(inp["ctx_2"][0]))
    give("pos", np.broadcast_to(inp["positions"][0].astype(np.int32), (P, T)))

    w = inp["w_in"][0]
    names = "rq rk rv rg bq bk bv ba bb bg cq ck cv c_lr cg dq df di dg".split()
    widths = [256, 256, 256, 256, 256, 256, 256, 4, 4, 256, 128, 128, 256, 16, 256, 256, 256, 256, 256]
    at = dict(zip(names, np.cumsum([0] + widths[:-1])))
    part = {n: w[:, at[n]:at[n] + wd] for n, wd in zip(names, widths)}
    most = tiles_fm(np.concatenate([part[n] for n in "rq rk bq bk bv cq dq ck df rv cv di".split()], 1))
    give("w_in_a", most[:8])
    give("w_in_b", most[8:])
    give("w_in_g", tiles_fm(np.concatenate([part[n] for n in "rg bg cg dg".split()], 1)))
    few = np.zeros((D, P), np.float32)
    few[:, 0:4], few[:, 32:36], few[:, 64:80] = part["ba"], part["bb"], part["c_lr"]
    give("w_in_small", tiles_fm(few, 1))
    gk = np.zeros((P, P), np.float32)
    gk[64:80] = inp["gla_gk_up"][0]
    give("gk_up", gk)
    give("w_out", tiles_fm(inp["w_out"][0]))
    give("wk", tiles_fm(inp["xattn_wk"][0]))
    give("wv", tiles_tm(inp["xattn_wv"][0]))
    give("wq", tiles_fm(inp["xattn_wq"][0]))
    give("wo", tiles_fm(inp["xattn_wo"][0]))
    ff1 = inp["ffn_down"].shape[1]
    feeds = {"ffn": (inp["ffn_up"][0], inp["ffn_down"][0]),
             "a1": (inp["w_ffn1_gu_2"][0], inp["w_ffn1_down_2"][0]), "a2": (inp["w_ffn2_gu_2"][0], inp["w_ffn2_down_2"][0]),
             "b1": (inp["w_ffn1_gu_2"][1], inp["w_ffn1_down_2"][1]), "b2": (inp["w_ffn2_gu_2"][1], inp["w_ffn2_down_2"][1])}
    for name, (w_up, w_down) in feeds.items():
        ff = w_down.shape[0]
        ups, downs = pair_up(w_up, ff), down(w_down)
        for half in range(2):
            give(f"{name}_up{half}", ups[half * HALF:(half + 1) * HALF])
            give(f"{name}_down{half}", downs[half])
        if ff % P:
            assert ff % P == HD
            give(f"{name}_up1_last", tiles_fm(np.concatenate([w_up[:, ff - HD:ff], w_up[:, 2 * ff - HD:]], 1), 1)[0])
    give("mod", np.concatenate([tiles_tm(inp["w_mod_2"][l]) for l in range(2)]))
    ab = inp["w_in_ab_2"][0]
    give("ab_a", tiles_fm(ab[:, 0:512]))
    give("ab_u", tiles_fm(ab[:, 512:1024]))
    give("ab_v", tiles_tm(ab[:, 1024:1536]))
    give("ab_out", tiles_fm(inp["w_out_ab_2"][0]))
    qkv = inp["w_qkv_2"][0]
    give("q2", tiles_fm(qkv[:, 0:1024]))
    give("k2", tiles_fm(qkv[:, 1024:1280]))
    give("v2", tiles_tm(qkv[:, 1280:1536]))
    give("wo2", tiles_fm(inp["w_o_2"][0]))
    give("ws_t", inp["w_s_2"][0].transpose(2, 0, 1))
    give("bs_row", np.broadcast_to(inp["b_s_2"][0], (P, 4, P)))
    give("gv_row", np.broadcast_to(inp["g_v_2"][0], (P, 4, P)))
    give("b_mod", features(inp["b_mod_2"].reshape(-1)))
    give("gains", np.stack([features(inp[g][l]) for l in range(2) for g in ("g_ffn1_2", "g_mix_2", "g_ffn2_2")], 1))
    give("c_in", np.stack([features(inp["c_2"][0]), features(inp["c_ctx_2"])], 2))

    blocks, cols, width = [], {}, 0

    def block(name, a):
        nonlocal width
        full = np.zeros((P, a.shape[1]), np.float32)
        full[:a.shape[0]] = a
        blocks.append(full)
        cols[name] = width
        width += a.shape[1]

    for name in ("mix_norm_w", "mem_norm_w", "xattn_norm_w", "ffn_norm_w", "final_norm_w"):
        block(name, features(inp[name].reshape(-1)))
    block("g_final", features(inp["g_final_2"]))
    for tap in range(4):
        block(f"gdn_conv{tap}", features(inp["gdn_conv_w"][0][tap]))
    for tap in range(3):
        w_tap = np.zeros((2, FF_TILES * P), np.float32)
        w_tap[:, :ff1] = inp["ffn_conv_w"][0][tap].reshape(2, ff1)
        block(f"ff_conv{tap}", features(w_tap.reshape(-1)))
    block("gdn_dt", inp["gdn_dt_bias"].T)
    block("gdn_a_log", inp["gdn_a_log"].T)
    block("rate", np.zeros((P, 1)))
    block("gk_bias", inp["gla_gk_bias"].T)
    block("freq", tables["freq"])
    block("tables", np.zeros((P, 16)))
    head_gain = np.ones((P, 8), np.float32)
    for j, name in enumerate(("gdn_norm_w", "gla_norm_w", "hgrn_norm_w")):
        for i in range(2):
            for tile in range(2):
                head_gain[i * HD:(i + 1) * HD, 2 + 2 * j + tile] = inp[name][0]
    block("head_gain", head_gain)
    block("g_q", inp["g_q_2"].T)
    block("g_k", inp["g_k_2"].T)
    for name, n in (("gcol", 8), ("bcol", 8), ("gam", 8), ("tailc", 4), ("att", 8)):
        block(name, np.zeros((P, n)))
    io["cols"] = cols
    give("small", np.concatenate(blocks, 1))

    io["out"] = nc.dram_tensor("out", (P, KT, T), F32, kind="ExternalOutput").ap()
    full, dn = CHUNK, HALF * P
    plan = [("w_in_a", 8, full), ("w_in_b", 3, full), ("w_in_small", 1, full // 2), ("w_in_g", 4, full), ("w_out", 6, full, 0), ("wk", 6, full, 0),
            ("wv", 6, full, 0), ("wq", 6, full, 0), ("wo", 6, full, 0)]

    def feed(name, ups_mixed=True, downs_mixed=True):
        jobs = []
        for half in range(2):
            jobs.append((f"{name}_up{half}", HALF + 6, full, 0) if ups_mixed else (f"{name}_up{half}", HALF, full))
            jobs.append((f"{name}_down{half}", KT + 4, dn, 1) if downs_mixed else (f"{name}_down{half}", KT, dn))
        return jobs

    plan += feed("ffn", ups_mixed=False) + feed("a1") + [("ab_a", 3, full, 0), ("ab_u", 2, full), ("ab_v", 2, full), ("ab_out", 4, full)]
    plan += feed("a2") + feed("b1", downs_mixed=False) + [("k2", 2, full, 0), ("q2", 4, full), ("v2", 1, full), ("wo2", 4, full)]
    plan += feed("b2", ups_mixed=False, downs_mixed=False)
    plan = [(job[0], job[1], job[2], io[job[0]], job[3] if len(job) > 3 else None) for job in plan]
    build(nc, io, plan)
    got = run_bass_kernel_spmd(nc, [arrays], core_ids=[0]).results[0]["out"]
    return np.ascontiguousarray(got.transpose(2, 1, 0)).reshape(1, T, D)
```
